# Optimizing a Trainium2 kernel written in Bass

```python
import math
import jax, jax.numpy as jnp
from jax import lax
import numpy as np

D_MODEL = 1024
BATCH = 1
SEQ = 512
DEPTH = 2

N_MIXERS = 2
CONV_CHANNELS = D_MODEL
CONV_WIDTH = 31
HEAD_DIM = 64
HEADS_PER_GROUP = 4
DILATION_PAIRS = ((128, 1), (512, 4), (2048, 16))
N_GROUPS = len(DILATION_PAIRS)
N_HEADS = N_GROUPS * HEADS_PER_GROUP
D_ATTN = N_HEADS * HEAD_DIM
N_BUCKETS = 32
REL_MAX_DISTANCE = 2048
D_FF = -(-8 * D_MODEL // (3 * 256)) * 256
EPS = 1e-6
N_CONV_LAYERS = (DEPTH + 1) // 2
N_ATTN_LAYERS = DEPTH // 2
NEG_INF = -1e30


def rmsnorm(x, g):
    x32 = x.astype(jnp.float32)
    y = x32 * lax.rsqrt(jnp.mean(x32 * x32, axis=-1, keepdims=True) + EPS)
    return (y * g.astype(jnp.float32)).astype(x.dtype)

def layernorm(x, g, b):
    x32 = x.astype(jnp.float32)
    mu = jnp.mean(x32, axis=-1, keepdims=True)
    xc = x32 - mu
    var = jnp.mean(xc * xc, axis=-1, keepdims=True)
    y = xc * lax.rsqrt(var + EPS) * g.astype(jnp.float32) + b.astype(jnp.float32)
    return y.astype(x.dtype)

def t5_bucket(dist):
    max_exact = N_BUCKETS // 2
    n = jnp.maximum(dist, 0)
    nf = jnp.maximum(n, 1).astype(jnp.float32)
    large = max_exact + (jnp.log(nf / max_exact) / math.log(REL_MAX_DISTANCE / max_exact)
                         * (N_BUCKETS - max_exact)).astype(jnp.int32)
    large = jnp.minimum(large, N_BUCKETS - 1)
    return jnp.where(n < max_exact, n, large)

def conformer_conv(h, w_pw1, b_pw1, w_dw, b_dw, ln_g, ln_b, w_pw2, b_pw2):
    u = h @ w_pw1 + b_pw1
    a, gate = jnp.split(u, 2, axis=-1)
    u = a * jax.nn.sigmoid(gate)
    u = lax.conv_general_dilated(
        u, w_dw[:, None, :], window_strides=(1,), padding=[(CONV_WIDTH - 1, 0)],
        dimension_numbers=("NWC", "WIO", "NWC"), feature_group_count=CONV_CHANNELS) + b_dw
    u = jax.nn.silu(layernorm(u, ln_g, ln_b))
    return u @ w_pw2 + b_pw2

def dilated_group(q, k, v, bias_table, window, dilation):
    b_, s, h, hd = q.shape
    n_back = window // dilation
    seg = n_back * dilation
    s_pad = -(-s // seg) * seg
    nb = s_pad // seg
    pad = ((0, 0), (0, s_pad - s), (0, 0), (0, 0))

    def blocks(t):
        return jnp.pad(t, pad).reshape(b_, nb, n_back, dilation, h, hd)

    def with_prev(t):
        prev = jnp.pad(t[:, :-1], ((0, 0), (1, 0), (0, 0), (0, 0), (0, 0), (0, 0)))
        return jnp.concatenate([prev, t], axis=2)

    qb = blocks(q)
    kk = with_prev(blocks(k))
    vv = with_prev(blocks(v))

    i_idx = jnp.arange(n_back)[:, None]
    j_idx = jnp.arange(2 * n_back)[None, :]
    dist = i_idx + n_back - j_idx
    bias = jnp.transpose(bias_table[t5_bucket(dist * dilation)], (2, 0, 1)).astype(jnp.float32)
    valid = (dist >= 0) & (dist <= n_back)
    not_before_start = (jnp.arange(nb)[:, None, None] > 0) | (j_idx[None] >= n_back)
    mask = valid[None] & not_before_start

    logits = jnp.einsum("bnidhc,bnjdhc->bndhij", qb, kk) * (HEAD_DIM ** -0.5) + bias
    logits = jnp.where(mask[None, :, None, None], logits, NEG_INF)
    m = jnp.max(logits, axis=-1, keepdims=True)
    p = jnp.exp(logits - m)
    den = jnp.sum(p, axis=-1)
    o = jnp.einsum("bndhij,bnjdhc->bnidhc", p, vv)
    den_t = jnp.transpose(den, (0, 1, 4, 2, 3))
    lse_t = jnp.transpose(m[..., 0] + jnp.log(den), (0, 1, 4, 2, 3))
    o = (o / den_t[..., None]).reshape(b_, s_pad, h, hd)[:, :s]
    lse = lse_t.reshape(b_, s_pad, h)[:, :s]
    return o, lse

def dilated_attention(h, w_qkv, w_o, rel_bias):
    b_, s, _ = h.shape
    qkv = (h @ w_qkv).astype(jnp.float32).reshape(b_, s, 3, N_HEADS, HEAD_DIM)
    outs, lses = [], []
    for g, (window, dilation) in enumerate(DILATION_PAIRS):
        hs = slice(g * HEADS_PER_GROUP, (g + 1) * HEADS_PER_GROUP)
        o, l = dilated_group(qkv[:, :, 0, hs], qkv[:, :, 1, hs], qkv[:, :, 2, hs],
                             rel_bias[:, hs], window, dilation)
        outs.append(o)
        lses.append(l)
    alpha = jax.nn.softmax(jnp.stack(lses, axis=0), axis=0)
    o = jnp.concatenate([outs[g] * alpha[g][..., None] for g in range(N_GROUPS)], axis=2)
    return o.reshape(b_, s, D_ATTN).astype(h.dtype) @ w_o

def swiglu(h, w_gate, w_up, w_down):
    return (jax.nn.silu(h @ w_gate) * (h @ w_up)) @ w_down

def first_inputs(seed: int = 0) -> dict:
    key = jax.random.key(seed)
    ks = jax.random.split(key, 20)
    f32 = jnp.float32

    def nrm(k, shape, scale):
        return jax.random.normal(k, shape, f32) * scale

    return {
        "x": nrm(ks[0], (BATCH, SEQ, D_MODEL), 1.0),
        "norm_mix": 1.0 + nrm(ks[1], (DEPTH, D_MODEL), 0.05),
        "norm_ffn": 1.0 + nrm(ks[2], (DEPTH, D_MODEL), 0.05),
        "final_norm": 1.0 + nrm(ks[3], (D_MODEL,), 0.05),
        "conv_w_pw1": nrm(ks[4], (N_CONV_LAYERS, D_MODEL, 2 * CONV_CHANNELS), D_MODEL ** -0.5),
        "conv_b_pw1": nrm(ks[5], (N_CONV_LAYERS, 2 * CONV_CHANNELS), 0.01),
        "conv_w_dw": nrm(ks[6], (N_CONV_LAYERS, CONV_WIDTH, CONV_CHANNELS), CONV_WIDTH ** -0.5),
        "conv_b_dw": nrm(ks[7], (N_CONV_LAYERS, CONV_CHANNELS), 0.01),
        "conv_ln_g": 1.0 + nrm(ks[8], (N_CONV_LAYERS, CONV_CHANNELS), 0.05),
        "conv_ln_b": nrm(ks[9], (N_CONV_LAYERS, CONV_CHANNELS), 0.01),
        "conv_w_pw2": nrm(ks[10], (N_CONV_LAYERS, CONV_CHANNELS, D_MODEL), CONV_CHANNELS ** -0.5),
        "conv_b_pw2": nrm(ks[11], (N_CONV_LAYERS, D_MODEL), 0.01),
        "attn_w_qkv": nrm(ks[12], (N_ATTN_LAYERS, D_MODEL, 3 * D_ATTN), D_MODEL ** -0.5),
        "attn_w_o": nrm(ks[13], (N_ATTN_LAYERS, D_ATTN, D_MODEL), D_ATTN ** -0.5),
        "rel_bias": nrm(ks[14], (N_BUCKETS, N_HEADS), 0.5),
        "ffn_w_gate": nrm(ks[15], (DEPTH, D_MODEL, D_FF), D_MODEL ** -0.5),
        "ffn_w_up": nrm(ks[16], (DEPTH, D_MODEL, D_FF), D_MODEL ** -0.5),
        "ffn_w_down": nrm(ks[17], (DEPTH, D_FF, D_MODEL), D_FF ** -0.5),
    }

def first_block(x, norm_mix, norm_ffn, final_norm, conv_w_pw1, conv_b_pw1, conv_w_dw, conv_b_dw,
              conv_ln_g, conv_ln_b, conv_w_pw2, conv_b_pw2, attn_w_qkv, attn_w_o, rel_bias,
              ffn_w_gate, ffn_w_up, ffn_w_down):
    for i in range(DEPTH):
        h = rmsnorm(x, norm_mix[i])
        j = i // N_MIXERS
        if i % N_MIXERS == 0:
            x = x + conformer_conv(h, conv_w_pw1[j], conv_b_pw1[j], conv_w_dw[j], conv_b_dw[j],
                                   conv_ln_g[j], conv_ln_b[j], conv_w_pw2[j], conv_b_pw2[j])
        else:
            x = x + dilated_attention(h, attn_w_qkv[j], attn_w_o[j], rel_bias)
        h = rmsnorm(x, norm_ffn[i])
        x = x + swiglu(h, ffn_w_gate[i], ffn_w_up[i], ffn_w_down[i])
    return rmsnorm(x, final_norm)


DEPTH_2 = 1

RET_HEADS = 8
DSA_HEADS = 8
RET_WIDTH = RET_HEADS * HEAD_DIM
DSA_WIDTH = DSA_HEADS * HEAD_DIM
MIX_WIDTH = RET_WIDTH + DSA_WIDTH
IDX_HEADS = 8
IDX_DIM = 64
TOPK_MAX = 256
RET_CHUNK = 128
Q_BLOCK = 128
D_FF_2 = 2816
CONV_WIDTH_2 = 3
ROPE_THETA = 10000.0
IN_SIZES = (RET_WIDTH, RET_WIDTH, RET_WIDTH, RET_WIDTH,
            DSA_WIDTH, HEAD_DIM, HEAD_DIM,
            IDX_HEADS * IDX_DIM, IDX_DIM, IDX_HEADS)
IN_WIDTH = 4 * RET_WIDTH + DSA_WIDTH + 2 * HEAD_DIM + IDX_HEADS * IDX_DIM + IDX_DIM + IDX_HEADS


def rms_norm(x, g):
    xf = x.astype(jnp.float32)
    y = xf * lax.rsqrt(jnp.mean(xf * xf, axis=-1, keepdims=True) + EPS)
    return (y * g.astype(jnp.float32)).astype(x.dtype)

def rope_tables(seq_len, dim):
    inv = ROPE_THETA ** (-jnp.arange(0, dim, 2, dtype=jnp.float32) / dim)
    ang = jnp.arange(seq_len, dtype=jnp.float32)[:, None] * inv[None, :]
    return jnp.cos(ang), jnp.sin(ang)

def apply_rope(x, cos, sin):
    shape = (cos.shape[0],) + (1,) * (x.ndim - 3) + (cos.shape[1],)
    c = cos.reshape(shape)
    s = sin.reshape(shape)
    xf = x.astype(jnp.float32)
    x1, x2 = jnp.split(xf, 2, axis=-1)
    return jnp.concatenate([x1 * c - x2 * s, x2 * c + x1 * s], axis=-1).astype(x.dtype)

def split_columns(p):
    pts, acc = [], 0
    for n in IN_SIZES[:-1]:
        acc += n
        pts.append(acc)
    return jnp.split(p, pts, axis=-1)

def retention(q, k, v, gate):
    B, S, H, d = q.shape
    C = RET_CHUNK
    N = S // C
    f32 = jnp.float32
    log_g = jnp.log(1.0 - 2.0 ** (-5.0 - jnp.arange(H, dtype=f32)))
    qf = q.astype(f32).reshape(B, N, C, H, d)
    kf = (k.astype(f32) * d ** -0.5).reshape(B, N, C, H, d)
    vf = v.astype(f32).reshape(B, N, C, H, d)
    pos = jnp.arange(C, dtype=f32)
    diff = pos[:, None] - pos[None, :]
    decay_in = jnp.where(diff >= 0, jnp.exp(log_g[:, None, None] * jnp.maximum(diff, 0.0)), 0.0)
    scores = jnp.einsum('bnchd,bnmhd->bnhcm', qf, kf) * decay_in[None, None]
    inner = jnp.einsum('bnhcm,bnmhd->bnchd', scores, vf)
    zeta = jnp.exp(log_g[:, None] * (C - 1.0 - pos)[None, :])
    chunk_state = jnp.einsum('bnmhk,hm,bnmhv->bnhkv', kf, zeta, vf)
    chunk_decay = jnp.exp(log_g * C)[None, :, None, None]

    def step(R, s):
        return chunk_decay * R + s, R

    _, prev = lax.scan(step, jnp.zeros((B, H, d, d), f32), jnp.moveaxis(chunk_state, 1, 0))
    prev = jnp.moveaxis(prev, 0, 1)
    xi = jnp.exp(log_g[:, None] * (pos + 1.0)[None, :])
    cross = jnp.einsum('bnchk,bnhkv,hc->bnchv', qf, prev, xi)
    o = (inner + cross).reshape(B, S, H, d)
    o = o * lax.rsqrt(jnp.mean(o * o, axis=-1, keepdims=True) + EPS)
    o = o * jax.nn.silu(gate.astype(f32).reshape(B, S, H, d))
    return o.reshape(B, S, H * d).astype(q.dtype)

def dsa_attention(q, k, v, qi, ki, wi):
    B, S, H, d = q.shape
    k_sel = min(TOPK_MAX, S // 4)
    NB = S // Q_BLOCK
    wi = wi * (IDX_HEADS ** -0.5 * IDX_DIM ** -0.5)

    def to_blocks(a):
        return jnp.moveaxis(a.reshape((B, NB, Q_BLOCK) + a.shape[2:]), 1, 0)

    key_pos = jnp.arange(S, dtype=jnp.int32)

    def block_fn(args):
        qb, qib, wib, blk = args
        t = blk * Q_BLOCK + jnp.arange(Q_BLOCK, dtype=jnp.int32)
        rel = jax.nn.relu(jnp.einsum('bthe,bse->bths', qib, ki))
        iscore = jnp.einsum('bths,bth->bts', rel, wib).astype(jnp.float32)
        causal = key_pos[None, :] <= t[:, None]
        iscore = jnp.where(causal[None], iscore, -jnp.inf)
        _, sel = lax.top_k(iscore, k_sel)
        valid = sel <= t[None, :, None]
        k_g = jax.vmap(lambda kb, ib: kb[ib])(k, sel)
        v_g = jax.vmap(lambda vb, ib: vb[ib])(v, sel)
        logits = jnp.einsum('bthd,btkd->bhtk', qb, k_g).astype(jnp.float32) * d ** -0.5
        logits = jnp.where(valid[:, None], logits, -1e30)
        p = jax.nn.softmax(logits, axis=-1).astype(v.dtype)
        return jnp.einsum('bhtk,btkd->bthd', p, v_g)

    out = lax.map(block_fn, (to_blocks(q), to_blocks(qi), to_blocks(wi),
                             jnp.arange(NB, dtype=jnp.int32)))
    return jnp.moveaxis(out, 0, 1).reshape(B, S, H * d)

def causal_dwconv(h, w, b):
    S = h.shape[1]
    hp = jnp.pad(h, ((0, 0), (CONV_WIDTH_2 - 1, 0), (0, 0)))
    y = b
    for j in range(CONV_WIDTH_2):
        y = y + hp[:, j:j + S] * w[j]
    return y

def second_inputs(seed: int = 0) -> dict:
    key = jax.random.key(seed)
    ks = jax.random.split(key, 11)
    f32 = jnp.float32
    nrm = lambda k, shape, scale: jax.random.normal(k, shape, f32) * scale
    gain = lambda k: 1.0 + 0.02 * jax.random.normal(k, (DEPTH_2, D_MODEL), f32)
    return {
        "x": jax.random.normal(ks[0], (BATCH, SEQ, D_MODEL), f32),
        "mix_norm_pre": gain(ks[1]),
        "mix_norm_post": gain(ks[2]),
        "w_in": nrm(ks[3], (DEPTH_2, D_MODEL, IN_WIDTH), D_MODEL ** -0.5),
        "w_out": nrm(ks[4], (DEPTH_2, MIX_WIDTH, D_MODEL), MIX_WIDTH ** -0.5),
        "ffn_norm_pre": gain(ks[5]),
        "ffn_norm_post": gain(ks[6]),
        "w_up": nrm(ks[7], (DEPTH_2, D_MODEL, 2 * D_FF_2), D_MODEL ** -0.5),
        "conv_w": nrm(ks[8], (DEPTH_2, CONV_WIDTH_2, 2 * D_FF_2), CONV_WIDTH_2 ** -0.5),
        "conv_b": nrm(ks[9], (DEPTH_2, 2 * D_FF_2), 0.01),
        "w_down": nrm(ks[10], (DEPTH_2, D_FF_2, D_MODEL), D_FF_2 ** -0.5),
    }

def second_block(x, mix_norm_pre, mix_norm_post, w_in, w_out, ffn_norm_pre, ffn_norm_post,
              w_up, conv_w, conv_b, w_down):
    B, S, _ = x.shape
    cos_h, sin_h = rope_tables(S, HEAD_DIM)
    cos_i, sin_i = rope_tables(S, IDX_DIM)
    h = x
    for l in range(DEPTH_2):
        hn = rms_norm(h, mix_norm_pre[l])
        proj = hn @ w_in[l]
        rq, rk, rv, rg, aq, ak, av, iq, ik, iw = split_columns(proj)
        rq = apply_rope(rq.reshape(B, S, RET_HEADS, HEAD_DIM), cos_h, sin_h)
        rk = apply_rope(rk.reshape(B, S, RET_HEADS, HEAD_DIM), cos_h, sin_h)
        rv = rv.reshape(B, S, RET_HEADS, HEAD_DIM)
        ret_out = retention(rq, rk, rv, rg)
        aq = apply_rope(aq.reshape(B, S, DSA_HEADS, HEAD_DIM), cos_h, sin_h)
        ak = apply_rope(ak, cos_h, sin_h)
        iq = apply_rope(iq.reshape(B, S, IDX_HEADS, IDX_DIM), cos_i, sin_i)
        ik = apply_rope(ik, cos_i, sin_i)
        att_out = dsa_attention(aq, ak, av, iq, ik, iw)
        mixed = jnp.concatenate([ret_out, att_out], axis=-1) @ w_out[l]
        h = h + rms_norm(mixed, mix_norm_post[l])
        hn = rms_norm(h, ffn_norm_pre[l])
        up = causal_dwconv(hn @ w_up[l], conv_w[l], conv_b[l])
        g, u = jnp.split(up, 2, axis=-1)
        ffn = (jax.nn.silu(g) * u) @ w_down[l]
        h = h + rms_norm(ffn, ffn_norm_post[l])
    return h


def setup_inputs(seed=0):
    out = dict(first_inputs(seed))
    for name, value in second_inputs(seed + 1).items():
        if name != "x":
            out[name + "_2"] = value
    return out


def reference(
    x, norm_mix, norm_ffn, final_norm, conv_w_pw1, conv_b_pw1, conv_w_dw, conv_b_dw, conv_ln_g,
    conv_ln_b, conv_w_pw2, conv_b_pw2, attn_w_qkv, attn_w_o, rel_bias, ffn_w_gate, ffn_w_up,
    ffn_w_down, mix_norm_pre_2, mix_norm_post_2, w_in_2, w_out_2, ffn_norm_pre_2,
    ffn_norm_post_2, w_up_2, conv_w_2, conv_b_2, w_down_2,
):
    x = first_block(
        x, norm_mix, norm_ffn, final_norm, conv_w_pw1, conv_b_pw1, conv_w_dw, conv_b_dw,
        conv_ln_g, conv_ln_b, conv_w_pw2, conv_b_pw2, attn_w_qkv, attn_w_o, rel_bias,
        ffn_w_gate, ffn_w_up, ffn_w_down,
    )
    return second_block(
        x, mix_norm_pre_2, mix_norm_post_2, w_in_2, w_out_2, ffn_norm_pre_2, ffn_norm_post_2,
        w_up_2, conv_w_2, conv_b_2, w_down_2,
    )


_drawn_inputs = setup_inputs


def setup_inputs(seed=0):
    import zlib

    import numpy as np

    out = dict(_drawn_inputs(seed))
    spreads = {}
    factors = {'conv_b_pw1': 2.685,
     'conv_ln_b': 3.103,
     'mix_norm_post_2': 3.507,
     'ffn_norm_pre_2': 3.483,
     'ffn_norm_post_2': 5.084,
     'conv_b_2': 7.058}
    for name, (base, spread) in spreads.items():
        noise = np.random.default_rng([zlib.crc32(name.encode()), seed]).standard_normal(out[name].shape)
        drawn = base * np.exp(spread * noise) if base else spread * noise
        out[name] = __import__('jax').numpy.asarray(drawn.astype(out[name].dtype))
    for name, factor in factors.items():
        out[name] = (out[name] * factor).astype(out[name].dtype)
    return out
```

```python
import concourse.bass as bass
from concourse import mybir
from concourse.alu_op_type import AluOpType as ALU
from contextlib import ExitStack

F32 = mybir.dt.float32
F32R = mybir.dt.float32r
ACT = mybir.ActivationFunctionType
AX = mybir.AxisListType

P = 128
SEQ = 512
D_MODEL = 1024
DT = D_MODEL // P
CONV_WIDTH = 31
FF_TILES = 22
FF_HALF = FF_TILES // 2
EPS = 1e-6
COLS = 256
UNIT_K = FF_HALF

LAYERS = [("pw1", 8, 8), ("pw2", 4, 8),
          ("gu0a", 11, 8), ("dn0a", 4, 11), ("gu0b", 11, 8), ("dn0b", 4, 11),
          ("qkv", 9, 8), ("wo", 4, 6),
          ("gu1a", 11, 8), ("dn1a", 4, 11), ("gu1b", 11, 8), ("dn1b", 4, 11),
          ("inp", 13, 8), ("wout", 4, 8),
          ("gu2a", 11, 8), ("dn2a", 4, 11), ("gu2b", 11, 8), ("dn2b", 4, 11)]

VECS = [("norm_mix0", 8), ("norm_mix1", 8), ("norm_ffn0", 8), ("norm_ffn1", 8), ("final", 8),
        ("b_pw1", 16), ("w_dw", CONV_WIDTH * 8), ("b_dw", 8), ("ln_g", 8), ("ln_b", 8), ("b_pw2", 8),
        ("mix_pre", 8), ("mix_post", 8), ("ffn_pre", 8), ("ffn_post", 8), ("conv3_w", 3 * 44), ("conv3_b", 44)]

MIX0, FFN0, MIX1, FFN1, FINAL, MIX_PRE, MIX_POST, FFN_PRE, FFN_POST = range(9)
X_BASE = {FFN0: 0, MIX1: 8, FFN1: 16, FINAL: 24, MIX_PRE: 32, FFN_PRE: 40}
H_BASE = {MIX0: 0, FFN0: 8, MIX1: 16, FFN1: 24, MIX_PRE: 32, FFN_PRE: 40}
Y_BASE = {MIX_POST: 0, FFN_POST: 8}

HD = 64
GROUP_HEADS = 4
BUCKETS = 32
NEG = -1e30
DIAG = 384
TOPK = 128
RET_HEADS = 8


def dilated_jobs():
    jobs = []
    for h in range(12):
        if h < GROUP_HEADS:
            jobs.append((h, [(0, 0, 128, [0]), (1, 128, 256, [0, 1])]))
            jobs.append((h, [(2, 0, 256, [1, 2]), (3, 256, 256, [2, 3])]))
        else:
            jobs.append((h, [(b, 128 * b, 128, [b]) for b in range(4)]))
    return jobs


DSA_JOBS = [(t, b, half) for t in range(4) for b in range(4) for half in range(2)]
RET_JOBS = [(h, mb) for h in range(RET_HEADS) for mb in range(4)]
INP_KINDS = ["kv", "iq", "iq", "rq", "rq", "rk", "rk", "rv", "rv", "rg", "rg", "aq", "aq"]
ROPE_UNITS = [j for j, k in enumerate(INP_KINDS) if k in ("iq", "rq", "rk", "aq")]
TOPK_AFTER = {5: 4, 6: 4, 7: 8, 8: 8, 9: 8, 10: 8, 11: 8}


class Layer:

    def __init__(self, name, n, kt, base):
        self.name, self.n, self.kt, self.base = name, n, kt, base


class At:

    def __init__(self, c, i=None):
        self.c, self.i = c, i

    def v(self, mult=1, add=0):
        if self.i is None:
            return mult * self.c + add
        return self.i * (2 * mult) + (mult * self.c + add)

    def plus(self, n):
        return At(self.c + n, self.i)

    def half(self, mult, add):
        if self.i is None:
            return mult * (self.c // 2) + add
        return self.i * mult + (mult * (self.c // 2) + add)

    @property
    def parity(self):
        return self.c % 2


def steps(eng, n, step, first=0, last=0):
    pairs = (n - first - last) // 2
    if pairs < 2:
        pairs = 0
    for j in range(first):
        step(At(j))
    if pairs:
        with eng.Fori(0, pairs) as i:
            step(At(first, i))
            step(At(first + 1, i))
    for j in range(first + 2 * pairs, n):
        step(At(j))


def build(nc, a, out):
    layers, base = {}, 0
    for name, n, kt in LAYERS:
        layers[name] = Layer(name, n, kt, base)
        base += n
    units = base
    order = [layers[x[0]] for x in LAYERS]
    kts = [l.kt for l in order for _ in range(l.n)]
    vec_at, n_vec = {}, 0
    for name, n in VECS:
        vec_at[name] = n_vec
        n_vec += n

    ctx = ExitStack()
    with ctx:
        top = [(nc.sbuf_base + 31) // 32 * 32]

        def sb(name, shape, dt=F32, at=None):
            size = 4
            for s in shape[1:]:
                size *= s
            size = (size + 31) // 32 * 32
            if at is None:
                at = top[0]
                top[0] += size
            return nc.alloc_sbuf_tensor_at(name, shape, dt, offset=at)

        X = sb("X", [P, DT, SEQ])
        H_hi = sb("H_hi", [P, DT, SEQ], F32R)
        H_lo = sb("H_lo", [P, DT, SEQ], F32R)
        W_raw = [sb(f"W_raw{b}", [P, UNIT_K * COLS]) for b in range(2)]
        W_hi = [sb(f"W_hi{b}", [P, UNIT_K * COLS], F32R) for b in range(2)]
        W_lo = [sb(f"W_lo{b}", [P, UNIT_K * COLS], F32R) for b in range(2)]
        cmat = sb("cmat", [P, 9, P])
        vecs = sb("vecs", [P, n_vec])
        epst = sb("epst", [P, 1])
        R = sb("R", [P, SEQ])
        STD = sb("STD", [P, SEQ])
        SSUM = sb("SSUM", [P, SEQ])
        SQ = sb("SQ", [P, 2, SEQ])
        T_g = sb("T_g", [P, SEQ])
        T_u = sb("T_u", [P, SEQ])
        T_act = sb("T_act", [P, SEQ])
        T_hid = sb("T_hid", [P, SEQ])
        arena = top[0]
        HID_hi = sb("HID_hi", [P, FF_HALF, SEQ], F32R, at=arena)
        HID_lo = sb("HID_lo", [P, FF_HALF, SEQ], F32R, at=arena + FF_HALF * SEQ * 4)
        PADDED = SEQ + CONV_WIDTH - 1 + 2
        U = sb("U", [P, DT, PADDED], at=arena)
        CV = sb("CV", [P, DT, SEQ], at=arena + 2 * FF_HALF * SEQ * 4)
        VQK = sb("VQK", [P, 18, SEQ], at=arena)
        OU = sb("OU", [P, 6, SEQ], at=arena)
        ROW_w = sb("ROW_w", [GROUP_HEADS, 3, SEQ], at=arena + 12288)
        ROW_max = sb("ROW_max", [GROUP_HEADS, SEQ], at=arena + 18432)
        ROW_sum = sb("ROW_sum", [GROUP_HEADS, SEQ], at=arena + 20480)
        ROW_den = sb("ROW_den", [GROUP_HEADS, 3, SEQ], at=arena + 36864)
        B0 = sb("B0", [P, GROUP_HEADS, 256], at=arena + 36864)
        B1 = sb("B1", [P, GROUP_HEADS, P], at=arena + 40960)
        B2 = sb("B2", [P, GROUP_HEADS, P], at=arena + 43008)
        VT = sb("VT", [P, 6, 4, P], at=arena + 45056)
        L1 = sb("L1", [P, 2, SEQ], at=arena + 57344)
        E1 = sb("E1", [P, 2, SEQ], at=arena + 61440)
        PT1 = sb("PT1", [P, 2, SEQ], at=arena + 65536)
        MD = sb("MD", [P, 2, 4, 12], at=arena + 69632)
        NM = sb("NM", [P, 2, 4], at=arena + 70016)
        onehot = sb("onehot", [BUCKETS + 1, 3, DIAG], at=arena + 57344)
        table = sb("table", [BUCKETS + 1, 12], at=arena + 62080)
        table_wide = sb("table_wide", [BUCKETS + 1, 12, P], at=arena + 45056)
        fvec = sb("fvec", [P, 12, DIAG], at=arena + 24576)
        Y = sb("Y", [P, DT, SEQ], at=arena + 45056)
        GP = sb("GP", [P, 2, SEQ + 2], at=arena + 61440)
        AQ = sb("AQ", [P, 4, SEQ], at=arena)
        RQK = sb("RQK", [P, 8, SEQ], at=arena + 8192)
        RVT = sb("RVT", [P, 4, SEQ], at=arena + 24576)
        GS = sb("GS", [P, 4, SEQ], at=arena + 32768)
        IQ = sb("IQ", [P, 4, SEQ], at=arena + 40960)
        CS = sb("CS", [P, 2, SEQ], at=arena + 49152)
        KK = sb("KK", [P, SEQ], at=arena + 53248)
        II = sb("II", [P, SEQ], at=arena + 55296)
        ISC = sb("ISC", [P, 3, SEQ], at=arena + 57344)
        WK = sb("WK", [P, SEQ], at=arena + 63488)
        AV = sb("AV", [P, 4, HD], at=arena + 65536)
        IW = sb("IW", [P, 4, 8], at=arena + 66560)
        TOP8 = sb("TOP8", [P, 8], at=arena + 66688)
        DEN = sb("DEN", [P, 2, 3], at=arena + 66720)
        DG = sb("DG", [P, 2, P], at=arena + 66752)
        L2 = sb("L2", [P, 2, SEQ], at=arena + 40960)
        E2 = sb("E2", [P, 2, SEQ], at=arena + 45056)
        PT2 = sb("PT2", [P, 2, SEQ], at=arena + 49152)
        CVacc = sb("CVacc", [P, SEQ], at=arena + 2 * FF_HALF * SEQ * 4 + DT * SEQ * 4)

        NM2 = sb("NM2", [P, 2], at=arena + 67776)
        L2k = [WK[:], ISC[:, 2, :]]
        T4 = [T_g, T_u, T_act, T_hid]
        bias_scratch = nc.dram_tensor("bias_scratch", (12, P, DIAG), F32, kind="Internal").ap()

        PS = [ctx.enter_context(nc.psum_tensor(f"PS{i}", [P, SEQ], F32)) for i in range(8)]
        AUX = PS[4:8]

        def vec(name, j, n=1):
            o = vec_at[name]
            if isinstance(j, At):
                return vecs[:, bass.ds(j.v(1, o), 1)]
            return vecs[:, o + j:o + j + 1]

        ident, ones, swap, dup, dupswap, headsum = (cmat[:, i, :] for i in range(6))
        sel = [cmat[0:GROUP_HEADS, 6 + i, :] for i in range(2)]
        later = cmat[:, 8, :]

        def tokens(ap, blk):
            return ap[:, blk * P:(blk + 1) * P]

        DILATION = (1, 4, 16)

        def permuted(ap, g):
            return ap.rearrange("p (r i) -> p i r", r=DILATION[g]) if g else ap

        def by_step(ap, g):
            return ap.rearrange("p (i r) -> p i r", r=DILATION[g]) if g else ap

        def unpermuted(ap, g):
            if g == 0:
                return ap
            if g == 1:
                return ap.rearrange("p (i b) -> p b i", b=4)
            return ap.rearrange("p (i r) -> p r i", r=16)

        def blocked(ap, g):
            if g == 0:
                return ap
            return ap.rearrange("p (b i) -> p b i", b=4 if g == 1 else 16)

        JOBS = dilated_jobs()

        def sem(name):
            return ctx.enter_context(nc.semaphore(name))

        x_in = sem("x_in")
        const_in = sem("const_in")
        eps_set = sem("eps_set")
        raw_in = [sem(f"raw_in{b}") for b in range(2)]
        w_hi = sem("w_hi")
        w_lo = sem("w_lo")
        acc_ready = sem("acc_ready")
        acc_free = sem("acc_free")
        x_ready = sem("x_ready")
        h_hi_made = sem("h_hi_made")
        h_lo_made = sem("h_lo_made")
        sq_made = sem("sq_made")
        ss_made = sem("ss_made")
        stat_ready = sem("stat_ready")
        std_made = sem("std_made")
        r_made = sem("r_made")
        gate_in = sem("gate_in")
        gate_act = sem("gate_act")
        hid_made = sem("hid_made")
        hid_hi_made = sem("hid_hi_made")
        hid_lo_made = sem("hid_lo_made")
        pads_set = sem("pads_set")
        glu_made = sem("glu_made")
        conv_step = sem("conv_step")
        conv_made = sem("conv_made")
        ln_sum = sem("ln_sum")
        ln_sum_ready = sem("ln_sum_ready")
        mu_made = sem("mu_made")
        xc_made = sem("xc_made")
        xc_sq = sem("xc_sq")
        ln_var_ready = sem("ln_var_ready")
        ln_std = sem("ln_std")
        ln_r = sem("ln_r")
        ln_scaled = sem("ln_scaled")
        ln_act = sem("ln_act")
        ln_hi_made = sem("ln_hi_made")
        ln_lo_made = sem("ln_lo_made")
        x_half = sem("x_half")
        out_done = sem("out_done")
        (tab_wide, pv_part, v_t, v_tok, tab_in, tab_pad, fvec_ps, fvec_made, scr_out, b2_set, bias_in, qkv_made, s_made, l_made, m_made, nm_made, e_made, pt_ps, pt_made, o_ps, ou_made, st_ps, row_made, rowmax, rowd, roww, rowwd, rows_, rowf, f_ps, o_made, o_hi_made, o_lo_made, y_ready, f_applied, cs_in, rt_made, sw_ps, rope_c, rope_s, rope_made, kv_ps, kv_c, kv_s, kv_made, tr_ps, av_made, rv_ps, rv_tok, rg_made, idx_ps, idx_rel, isc_made, isc_mask, top_max, top_rep, left_out, d_in, rs_ps, rd_made, ro_ps, r_sq, rsum_ps, rstd, rrec, ro1, ro2, m_hi_made, m_lo_made, a_s, a_l, a_m, a_nm, a_e, a_rd, a_dg, a_pt_ps, a_pt, a_o, c3_y, c3_y1, c3_y2, pad3_set, g3_in) = (sem(n) for n in """tab_wide pv_part v_t v_tok tab_in tab_pad fvec_ps fvec_made scr_out b2_set bias_in qkv_made s_made l_made m_made nm_made e_made pt_ps pt_made o_ps ou_made st_ps row_made rowmax rowd roww rowwd rows_ rowf f_ps o_made o_hi_made o_lo_made y_ready f_applied cs_in rt_made sw_ps rope_c rope_s rope_made kv_ps kv_c kv_s kv_made tr_ps av_made rv_ps rv_tok rg_made idx_ps idx_rel isc_made isc_mask top_max top_rep left_out d_in rs_ps rd_made ro_ps r_sq rsum_ps rstd rrec ro1 ro2 m_hi_made m_lo_made a_s a_l a_m a_nm a_e a_rd a_dg a_pt_ps a_pt a_o c3_y c3_y1 c3_y2 pad3_set g3_in""".split())

        block = ctx.enter_context(nc.Block())

        def acc(u, half):
            return PS[2 * (u % 2) + half]

        gu_base = {f"gu{l}{h}": 22 * l + 11 * k for l in range(3) for k, h in enumerate("ab")}

        @block.sync
        def _(sp):
            sp.dma_start(X[:], a["x"]).then_inc(x_in, 16)
            sp.dma_start(vecs[:], a["vecs"]).then_inc(const_in, 16)

            def load(L, src, j):
                u = j.plus(L.base)
                b = u.parity
                if u.i is not None or u.c >= 2:
                    sp.wait_ge(w_lo, u.v(1, -1))
                n = L.kt * COLS
                sp.dma_start(W_raw[b][:, 0:n], src[bass.ds(j.v(), 1)].rearrange("o p n -> p (o n)") if j.i is not None else src[j.c]).then_inc(raw_in[b], 16)

            for k, L in enumerate(order):
                steps(sp, L.n, lambda j: load(L, a[L.name], j), first=2 if k == 0 else 0)
            sp.wait_ge(x_ready, 56)
            sp.dma_start(out, X[:]).then_inc(out_done, 16)
            sp.wait_ge(out_done, 16)

        @block.tensor
        def _(pe):
            def products(b, kt, half, x_hi, x_lo, ready=None):
                dst = PS[2 * b + half]
                for k in range(kt):
                    if ready is not None:
                        pe.wait_ge(ready[0], ready[1] + k + 1)
                    c = k * COLS + half * P
                    wh, wl = W_hi[b][:, c:c + P], W_lo[b][:, c:c + P]
                    nc.tensor.matmul(dst[:], wh, x_hi[:, k, :], start=(k == 0), stop=False)
                    nc.tensor.matmul(dst[:], wh, x_lo[:, k, :], start=False, stop=False)
                    last = nc.tensor.matmul(dst[:], wl, x_hi[:, k, :], start=False, stop=(k == kt - 1))
                last.then_inc(acc_ready, 1)

            def unit(L, j, x_hi, x_lo, ready=None):
                u = j.plus(L.base)
                pe.wait_ge(w_lo, u.v(1, 1))
                if u.i is not None or u.c >= 2:
                    pe.wait_ge(acc_free, u.v(1, -1))
                products(u.parity, L.kt, 0, x_hi, x_lo, ready)
                products(u.parity, L.kt, 1, x_hi, x_lo)

            def rms_sum(n):
                pe.wait_ge(ss_made, 8 * (n + 1))
                if n:
                    pe.wait_ge(std_made, n)
                nc.tensor.matmul(AUX[0][:], ones, SSUM[:], start=True, stop=True).then_inc(stat_ready, 1)

            def linear(name, x_hi=H_hi, x_lo=H_lo, ready=None, norm=None):
                L = layers[name]

                def step(j):
                    first = j.i is None and j.c == 0
                    unit(L, j, x_hi, x_lo, ready if first else None)
                    if first and norm is not None:
                        rms_sum(norm)
                steps(pe, L.n, step, first=1)

            pe.wait_ge(const_in, 32)
            pe.wait_ge(tab_wide, 1)
            for h in range(12):
                if h >= 3:
                    pe.wait_ge(fvec_made, h - 2)
                nc.tensor.matmul(PS[5 + h % 3][:, 0:DIAG], table_wide[:, h, :], onehot[:, h // GROUP_HEADS, :],
                                 start=True, stop=True).then_inc(fvec_ps, 1)
            linear("pw1", ready=(h_lo_made, 0), norm=0)
            pe.wait_ge(fvec_made, 12)
            pe.wait_ge(ln_sum, 8)
            nc.tensor.matmul(AUX[1][:], ones, SSUM[:], start=True, stop=True).then_inc(ln_sum_ready, 1)
            for m in range(DT):
                pe.wait_ge(xc_sq, m + 1)
                last = nc.tensor.matmul(AUX[2][:], ones, H_lo32[m], start=(m == 0), stop=(m == DT - 1)) if False else \
                    nc.tensor.matmul(AUX[2][:], ones, SQ[:, m % 2, :], start=(m == 0), stop=(m == DT - 1))
                last.then_inc(ln_var_ready, 1)
            linear("pw2", HID_hi, HID_lo, ready=(ln_lo_made, 0))

            def feed_forward(l, norm):
                linear(f"gu{l}a", ready=(h_lo_made, H_BASE[norm]), norm=norm)
                linear(f"dn{l}a", HID_hi, HID_lo, ready=(hid_lo_made, gu_base[f"gu{l}a"]))
                linear(f"gu{l}b")
                linear(f"dn{l}b", HID_hi, HID_lo, ready=(hid_lo_made, gu_base[f"gu{l}b"]))

            feed_forward(0, FFN0)

            linear("qkv", ready=(h_lo_made, H_BASE[MIX1]), norm=MIX1)
            for t in range(6):
                pe.wait_ge(qkv_made, t + 1)
                if t == 0:
                    pe.wait_ge(std_made, MIX1 + 1)
                if t >= 4:
                    pe.wait_ge(v_tok, t - 3)
                for b in range(4):
                    last = nc.tensor.transpose(AUX[t % 4][:, b * P:(b + 1) * P], tokens(VQK[:, t, :], b), ident)
                last.then_inc(v_t, 1)

            def dilated_scores(n):
                h, blks = JOBS[n]
                g, t, lo = h // GROUP_HEADS, h // 2, HD * (h % 2)
                if n == 0:
                    pe.wait_ge(qkv_made, 18)
                if n >= 2:
                    pe.wait_ge(l_made, n - 1)
                for blk, c, w, keys in blks:
                    q = tokens(VQK[lo:lo + HD, 6 + t, :], blk)
                    k = VQK[lo:lo + HD, 12 + t, :]
                    k = k[:, P * keys[0]:P * (keys[-1] + 1)] if g == 0 else tokens(k, blk)
                    last = nc.tensor.matmul(PS[n % 2][:, c:c + w], q, k, start=True, stop=True)
                last.then_inc(s_made, 1)

            dilated_scores(0)
            dilated_scores(1)
            for n, (h, blks) in enumerate(JOBS):
                g, t, lo = h // GROUP_HEADS, h // 2, HD * (h % 2)
                pe.wait_ge(e_made, n + 1)
                if n >= 2:
                    pe.wait_ge(pt_made, n - 1)
                chunks = [(blk, c + P * i, key) for blk, c, w, keys in blks for i, key in enumerate(keys)]
                for i, (blk, c, key) in enumerate(chunks):
                    last = nc.tensor.transpose(PS[2 + n % 2][:, i * P:(i + 1) * P], E1[:, n % 2, c:c + P], ident)
                last.then_inc(pt_ps, 1)
                if n + 2 < len(JOBS):
                    dilated_scores(n + 2)
                pe.wait_ge(pt_made, n + 1)
                if n == 0:
                    pe.wait_ge(v_tok, 6)
                if h % 2 == 0 and blks[0][0] == 0 and t >= 2:
                    pe.wait_ge(ou_made, t - 1)
                for i, (blk, c, key) in enumerate(chunks):
                    first = i == 0 or chunks[i - 1][0] != blk
                    end = i + 1 == len(chunks) or chunks[i + 1][0] != blk
                    last = nc.tensor.matmul(PS[4 + t % 2][lo:lo + HD, blk * P:(blk + 1) * P],
                                            VT[:, t, key, lo:lo + HD], PT1[:, n % 2, i * P:(i + 1) * P],
                                            start=first, stop=end)
                if h % 2 == 1 and blks[-1][0] == 3:
                    last.then_inc(o_ps, 1)
                else:
                    last.then_inc(pv_part, 1)
            for i in range(6):
                kind, g = i // 3, i % 3
                if i >= 2:
                    pe.wait_ge(row_made, i - 1)
                for b in range(4):
                    last = nc.tensor.matmul(PS[6 + i % 2][0:GROUP_HEADS, b * P:(b + 1) * P],
                                            MD[:, kind, b, 4 * g:4 * g + 4], ident, start=True, stop=True)
                last.then_inc(st_ps, 1)
            for t in range(6):
                if t == 0:
                    pe.wait_ge(rowf, 1)
                    pe.wait_ge(row_made, 6)
                if t >= 2:
                    pe.wait_ge(o_made, t - 1)
                nc.tensor.matmul(PS[6 + t % 2][:], sel[t % 2], ROW_w[:, t // 2, :], start=True,
                                 stop=True).then_inc(f_ps, 1)
            linear("wo", HID_hi, HID_lo, ready=(o_lo_made, 0))

            feed_forward(1, FFN1)
            rms_sum(FINAL)

            L = layers["inp"]

            def post(j):
                kind = INP_KINDS[j]
                pe.wait_ge(rt_made, 2 * j + 2)
                if kind == "kv":
                    for i in range(4):
                        nc.tensor.matmul(AUX[i][:], (dup, dupswap)[i % 2], T4[i // 2][:], start=True,
                                         stop=True).then_inc(kv_ps, 1)
                    for i in range(2):
                        pe.wait_ge(kv_c, 2)
                        pe.wait_ge(kv_s, 2)
                        for b in range(4):
                            last = nc.tensor.transpose(AUX[i][:, b * P:(b + 1) * P], T4[i][:, b * P:(b + 1) * P], ident)
                        last.then_inc(tr_ps, 1)
                elif j in ROPE_UNITS:
                    r = ROPE_UNITS.index(j)
                    for i in range(2):
                        if j == ROPE_UNITS[0]:
                            pe.wait_ge(av_made, 2)
                        elif r:
                            pe.wait_ge(rope_s, 2 * r - 1 + i)
                        if j in (11,):
                            pe.wait_ge(rv_tok, 4)
                        nc.tensor.matmul(AUX[i][:], swap, T4[2 * (j % 2) + i][:], start=True, stop=True).then_inc(sw_ps, 1)
                elif kind == "rv":
                    for i in range(2):
                        n = 2 * (j - 7) + i
                        pe.wait_ge(rope_s, 12)
                        if n >= 2:
                            pe.wait_ge(rv_tok, n - 1)
                        for b in range(4):
                            last = nc.tensor.transpose(AUX[i][:, b * P:(b + 1) * P],
                                                       T4[2 * (j % 2) + i][:, b * P:(b + 1) * P], ident)
                        last.then_inc(rv_ps, 1)

            def index_scores(b):
                w = P * (b + 1)
                for h in range(8):
                    n = 8 * (b - 1) + h
                    if n == 0:
                        pe.wait_ge(rope_made, 4)
                        pe.wait_ge(kv_made, 2)
                    if n >= 2:
                        pe.wait_ge(idx_rel, n - 1)
                    lo = HD * (h % 2)
                    nc.tensor.matmul(AUX[2 + n % 2][:, 0:w], IQ[lo:lo + HD, h // 2, b * P:(b + 1) * P],
                                     II[lo:lo + HD, 0:w], start=True, stop=True).then_inc(idx_ps, 1)

            for j in range(L.n):
                unit(L, At(j), H_hi, H_lo, (h_lo_made, H_BASE[MIX_PRE]) if j == 0 else None)
                if j == 0:
                    rms_sum(MIX_PRE)
                else:
                    post(j - 1)
                if 4 <= j <= 6:
                    index_scores(j - 3)
            post(L.n - 1)

            def ret_scores(n):
                h, mb = RET_JOBS[n]
                t, lo = h // 2, HD * (h % 2)
                if n == 0:
                    pe.wait_ge(rope_made, 12)
                    pe.wait_ge(acc_free, L.base + L.n)
                if n >= 2:
                    pe.wait_ge(rd_made, n - 1)
                nc.tensor.matmul(PS[n % 2][:, 0:SEQ - P * mb], RQK[lo:lo + HD, 4 + t, P * mb:P * (mb + 1)],
                                 RQK[lo:lo + HD, t, P * mb:SEQ], start=True, stop=True).then_inc(rs_ps, 1)

            def ret_norm(t):
                pe.wait_ge(r_sq, t + 1)
                if t:
                    pe.wait_ge(rstd, t)
                nc.tensor.matmul(AUX[2][:], headsum, L2[:, 0, :], start=True, stop=True).then_inc(rsum_ps, 1)

            ret_scores(0)
            ret_scores(1)
            for n, (h, mb) in enumerate(RET_JOBS):
                t, lo = h // 2, HD * (h % 2)
                pe.wait_ge(rd_made, n + 1)
                if n == 0:
                    pe.wait_ge(rv_tok, 4)
                    pe.wait_ge(rope_s, 16)
                if mb == 0 and h % 2 == 0 and t >= 2:
                    pe.wait_ge(ro1, t - 1)
                last = nc.tensor.matmul(AUX[t % 2][lo:lo + HD, P * mb:SEQ], RVT[:, mb, HD * h:HD * (h + 1)],
                                        T4[n % 2][:, 0:SEQ - P * mb], start=(mb == 0), stop=(mb == 3))
                last.then_inc(ro_ps, 1)
                if n + 2 < len(RET_JOBS):
                    ret_scores(n + 2)
                if n % 8 == 3 and n > 8:
                    ret_norm(n // 8 - 1)
            ret_norm(3)

            def dsa_scores(n):
                t, b, half = DSA_JOBS[n]
                lo = HD * half
                if n == 0:
                    pe.wait_ge(rope_made, 16)
                if n >= 2:
                    pe.wait_ge(a_l, n - 1)
                nc.tensor.matmul(PS[n % 2][:, 0:P * (b + 1)], AQ[lo:lo + HD, t, b * P:(b + 1) * P],
                                 KK[lo:lo + HD, 0:P * (b + 1)], start=True, stop=True).then_inc(a_s, 1)

            dsa_scores(0)
            dsa_scores(1)
            for n, (t, b, half) in enumerate(DSA_JOBS):
                lo = HD * half
                pe.wait_ge(a_dg, n + 1)
                if n >= 2:
                    pe.wait_ge(a_pt, n - 1)
                for c in range(b + 1):
                    last = nc.tensor.matmul(PS[2 + n % 2][:, c * P:(c + 1) * P], E2[:, n % 2, c * P:(c + 1) * P],
                                            DG[:, n % 2, :], start=True, stop=True)
                last.then_inc(a_pt_ps, 1)
                if n + 2 < len(DSA_JOBS):
                    dsa_scores(n + 2)
                pe.wait_ge(a_pt, n + 1)
                if n == 0:
                    pe.wait_ge(ro1, 4)
                if n % 8 == 0 and t >= 2:
                    pe.wait_ge(m_lo_made, 4 + t - 1)
                for c in range(b + 1):
                    last = nc.tensor.matmul(AUX[t % 2][lo:lo + HD, b * P:(b + 1) * P], AV[:, c, :],
                                            PT2[:, n % 2, c * P:(c + 1) * P], start=(c == 0), stop=(c == b))
                last.then_inc(a_o, 1)
            linear("wout", ready=(m_lo_made, 0))
            rms_sum(MIX_POST)
            feed_forward(2, FFN_PRE)
            rms_sum(FFN_POST)

        def split_hi(act, L, j):
            u = j.plus(L.base + 2)
            if u.i is None and u.c >= units:
                return
            kt = L.kt if u.i is not None else kts[u.c]
            hi_of(act, u, kt)

        def hi_of(act, u, kt):
            b = u.parity
            n = kt * COLS
            act.wait_ge(raw_in[b], u.half(16, 16))
            if u.i is not None or u.c >= 2:
                act.wait_ge(acc_ready, u.v(2, -2))
            nc.scalar.activation(W_hi[b][:, 0:n], W_raw[b][:, 0:n], ACT.Copy).then_inc(w_hi, 1)

        @block.scalar
        def _(act):
            act.dma_start(cmat[:], a["cmat"]).then_inc(const_in, 16)
            act.dma_start(onehot[:], a["onehot"]).then_inc(tab_in, 16)
            act.dma_start(table[0:BUCKETS, :], a["rel_bias"]).then_inc(tab_in, 16)
            hi_of(act, At(0), kts[0])
            act.wait_ge(x_in, 16)
            act.wait_ge(const_in, 32)

            def h_hi(n, gain, m):
                if n:
                    act.wait_ge(x_ready, m.v(1, X_BASE[n] + 1))
                dst = H_hi[:, bass.ds(m.v(), 1), :].rearrange("p o n -> p (o n)")
                src = X[:, bass.ds(m.v(), 1), :].rearrange("p o n -> p (o n)")
                nc.scalar.activation(dst, src, ACT.Copy, scale=vec(gain, m)).then_inc(h_hi_made, 1)

            def std(n):
                act.wait_ge(stat_ready, n + 1)
                nc.scalar.activation(STD[:], AUX[0][:], ACT.Sqrt, bias=epst[:], scale=1.0 / D_MODEL).then_inc(std_made, 1)

            for m in range(DT):
                h_hi(MIX0, "norm_mix0", At(m))
            hi_of(act, At(1), kts[1])
            for h in range(12):
                act.wait_ge(fvec_ps, h + 1)
                nc.scalar.activation(fvec[:, h, :], PS[5 + h % 3][:, 0:DIAG], ACT.Copy).then_inc(fvec_made, 1)
            act.wait_ge(fvec_made, 12)
            act.dma_start(bias_scratch.rearrange("h p d -> p h d"), fvec[:]).then_inc(scr_out, 16)

            L = layers["pw1"]
            act.wait_ge(eps_set, 1)

            def glu_step(j):
                split_hi(act, L, j)
                if j.i is None and j.c == 0:
                    std(0)
                act.wait_ge(gate_in, j.v(1, 1))
                nc.scalar.activation(T_act[:], T_g[:], ACT.Sigmoid, bias=vec("b_pw1", j.plus(DT))).then_inc(gate_act, 1)
            steps(act, L.n, glu_step, first=1, last=2)
            act.wait_ge(ln_sum_ready, 1)
            nc.scalar.activation(STD[:], AUX[1][:], ACT.Copy, scale=1.0 / D_MODEL).then_inc(mu_made, 1)
            for m in range(DT):
                act.wait_ge(xc_made, m + 1)
                if m >= 2:
                    act.wait_ge(ln_var_ready, m - 1)
                nc.scalar.activation(SQ[:, m % 2, :], CV[:, m, :], ACT.Square).then_inc(xc_sq, 1)
            act.wait_ge(ln_var_ready, DT)
            nc.scalar.activation(STD[:], AUX[2][:], ACT.Sqrt, bias=epst[:], scale=1.0 / D_MODEL).then_inc(ln_std, 1)
            for m in range(DT):
                act.wait_ge(ln_scaled, m + 1)
                nc.scalar.activation(CV[:, m, :], CV[:, m, :], ACT.Silu, bias=vec("ln_b", m), scale=vec("ln_g", m)).then_inc(ln_act, 1)
                act.wait_ge(ln_act, m + 1)
                nc.scalar.activation(HID_hi[:, m, :], CV[:, m, :], ACT.Copy).then_inc(ln_hi_made, 1)

            def add_steps(name, norm=None, gain=None):
                L = layers[name]

                def step(j):
                    split_hi(act, L, j)
                    if norm is not None:
                        h_hi(norm, gain, At(2 * j.c, None if j.i is None else j.i * 2))
                        h_hi(norm, gain, At(2 * j.c + 1, None if j.i is None else j.i * 2))
                steps(act, L.n, step, last=2)

            def gate_steps(name, norm=None):
                L, q0 = layers[name], gu_base[name]

                def step(j):
                    split_hi(act, L, j)
                    if j.i is None and j.c == 0 and norm is not None:
                        std(norm)
                    act.wait_ge(gate_in, j.v(1, 8 + q0 + 1))
                    nc.scalar.activation(T_act[:], T_g[:], ACT.Silu).then_inc(gate_act, 1)
                    hid_hi(j, q0)
                steps(act, L.n, step, first=1, last=2)

            def hid_hi(j, q0):
                act.wait_ge(hid_made, j.v(1, q0 + 1))
                dst = HID_hi[:, bass.ds(j.v(), 1), :].rearrange("p o n -> p (o n)")
                nc.scalar.activation(dst, T_hid[:], ACT.Copy).then_inc(hid_hi_made, 1)

            add_steps("pw2", FFN0, "norm_ffn0")
            gate_steps("gu0a", norm=FFN0)
            add_steps("dn0a")
            gate_steps("gu0b")
            add_steps("dn0b", MIX1, "norm_mix1")

            L = layers["qkv"]
            for j in range(L.n):
                split_hi(act, L, At(j))
                if j == 0:
                    std(MIX1)
                    act.wait_ge(scr_out, 16)
                    t = bias_scratch.tensor
                    def diagonals(h, rows, n):
                        return bass.AP(t, h * P * DIAG + rows - 1, [[DIAG - 1, rows], [P * DIAG, GROUP_HEADS], [1, n]])
                    act.dma_start(B0[:], diagonals(0, P, 2 * P)).then_inc(bias_in, 16)
                    act.dma_start(B1[:], diagonals(4, P, P)).then_inc(bias_in, 16)
                    act.wait_ge(b2_set, 1)
                    for r in range(4):
                        act.dma_start(B2[32 * r:32 * r + 32, :, 32 * r:32 * r + 32], diagonals(8, 32, 32)).then_inc(bias_in, 16)
            for t in range(6):
                act.wait_ge(v_t, t + 1)
                nc.scalar.activation(VT[:, t, :, :].rearrange("p b n -> p (b n)"), AUX[t % 4][:], ACT.Copy).then_inc(v_tok, 1)
            for n, (h, blks) in enumerate(JOBS):
                act.wait_ge(nm_made, n + 1)
                if n >= 2:
                    act.wait_ge(pt_ps, n - 1)
                for i, (blk, c, w, keys) in enumerate(blks):
                    last = nc.scalar.activation(E1[:, n % 2, c:c + w], L1[:, n % 2, c:c + w], ACT.Exp,
                                                bias=NM[:, n % 2, i:i + 1], accum_out=MD[:, 1, blk, h:h + 1])
                last.then_inc(e_made, 1)
                act.wait_ge(pt_ps, n + 1)
                if n == 2:
                    act.wait_ge(pv_part, 1)
                if n > 2:
                    act.wait_ge(o_ps, sum(1 for h_, b_ in JOBS[:n - 1] if h_ % 2 == 1 and b_[-1][0] == 3)) if sum(
                        1 for h_, b_ in JOBS[:n - 1] if h_ % 2 == 1 and b_[-1][0] == 3) else None
                    act.wait_ge(pv_part, sum(1 for h_, b_ in JOBS[:n - 1] if not (h_ % 2 == 1 and b_[-1][0] == 3)))
                w = P * sum(len(keys) for _, _, _, keys in blks)
                nc.scalar.activation(PT1[:, n % 2, 0:w], PS[2 + n % 2][:, 0:w], ACT.Copy).then_inc(pt_made, 1)
            for i in range(6):
                kind, g = i // 3, i % 3
                act.wait_ge(st_ps, i + 1)
                dst = (ROW_w, ROW_den)[kind]
                nc.scalar.activation(unpermuted(dst[:, g, :], g), blocked(PS[6 + i % 2][0:GROUP_HEADS, :], g),
                                     ACT.Copy).then_inc(row_made, 1)
            act.wait_ge(rowd, 1)
            nc.scalar.activation(ROW_w[:], ROW_w[:], ACT.Exp).then_inc(roww, 1)
            for t in range(6):
                act.wait_ge(o_made, t + 1)
                nc.scalar.activation(HID_hi[:, t, :], T4[t % 2][:], ACT.Copy).then_inc(o_hi_made, 1)

            add_steps("wo", FFN1, "norm_ffn1")
            gate_steps("gu1a", norm=FFN1)
            add_steps("dn1a")
            gate_steps("gu1b")
            add_steps("dn1b")
            std(FINAL)
            for m in range(DT):
                h_hi(MIX_PRE, "mix_pre", At(m))

            L = layers["inp"]

            def index_relu(b):
                w = P * (b + 1)
                for h in range(8):
                    n = 8 * (b - 1) + h
                    act.wait_ge(idx_ps, n + 1)
                    if n >= 2:
                        act.wait_ge(isc_made, n - 1)
                    nc.scalar.activation(SQ[:, n % 2, 0:w], AUX[2 + n % 2][:, 0:w], ACT.Relu).then_inc(idx_rel, 1)

            def post(j):
                kind = INP_KINDS[j]
                if kind == "rv":
                    for i in range(2):
                        n = 2 * (j - 7) + i
                        act.wait_ge(rv_ps, n + 1)
                        dst = RVT[:, :, n * P:(n + 1) * P]
                        nc.scalar.activation(dst, AUX[i][:].rearrange("p (b n) -> p b n", b=4), ACT.Copy).then_inc(rv_tok, 1)
                elif kind == "rg":
                    for i in range(2):
                        act.wait_ge(rt_made, 2 * j + 1 + i)
                        nc.scalar.activation(GS[:, 2 * (j - 9) + i, :], T4[2 * (j % 2) + i][:], ACT.Silu).then_inc(rg_made, 1)

            for j in range(L.n):
                split_hi(act, L, At(j))
                if j == 0:
                    std(MIX_PRE)
                    act.dma_start(CS[:], a["rotary"]).then_inc(cs_in, 16)
                else:
                    post(j - 1)
                if 4 <= j <= 6:
                    index_relu(j - 3)
            act.wait_ge(isc_made, 24)
            for h in range(2):
                act.dma_start(SQ[:, h, :], a["decay"][h]).then_inc(d_in, 16)

            def ret_norm_sq(t):
                act.wait_ge(ro_ps, 8 * t + 8)
                if t:
                    act.wait_ge(rsum_ps, t)
                else:
                    act.wait_ge(rope_made, 16)
                nc.scalar.activation(L2[:, 0, :], AUX[t % 2][:], ACT.Square).then_inc(r_sq, 1)
                act.wait_ge(rsum_ps, t + 1)
                if t:
                    act.wait_ge(rrec, t)
                nc.scalar.activation(STD[:], AUX[2][:], ACT.Sqrt, bias=epst[:], scale=1.0 / HD).then_inc(rstd, 1)
                act.wait_ge(ro2, t + 1)
                nc.scalar.activation(H_hi[:, t, :], E2[:, 0, :], ACT.Copy).then_inc(m_hi_made, 1)

            for h in range(2, RET_HEADS):
                act.wait_ge(rd_made, 4 * (h - 1))
                act.wait_ge(d_in, 16 * h)
                act.dma_start(SQ[:, h % 2, :], a["decay"][h]).then_inc(d_in, 16)
                if h % 2 == 1:
                    ret_norm_sq(h // 2 - 1)
            ret_norm_sq(3)
            for n, (t, b, half) in enumerate(DSA_JOBS):
                w = P * (b + 1)
                act.wait_ge(a_nm, n + 1)
                if n >= 2:
                    act.wait_ge(a_pt_ps, n - 1)
                if n == 0:
                    act.wait_ge(m_lo_made, 4)
                nc.scalar.activation(E2[:, n % 2, 0:w], L2[:, n % 2, 0:w], ACT.Exp, scale=HD ** -0.5,
                                     bias=DEN[:, n % 2, 0:1], accum_out=DEN[:, n % 2, 1:2]).then_inc(a_e, 1)
                act.wait_ge(a_pt_ps, n + 1)
                if n >= 2:
                    act.wait_ge(a_o, n - 1)
                nc.scalar.activation(PT2[:, n % 2, 0:w], PS[2 + n % 2][:, 0:w], ACT.Copy).then_inc(a_pt, 1)
                if n % 8 == 7:
                    act.wait_ge(a_o, n + 1)
                    nc.scalar.activation(H_hi[:, 4 + t, :], AUX[t % 2][:], ACT.Copy).then_inc(m_hi_made, 1)

            add_steps("wout")
            std(MIX_POST)
            for m in range(DT):
                h_hi(FFN_PRE, "ffn_pre", At(m))

            def conv_gate_steps(name, j0, norm=None):
                L, q0 = layers[name], gu_base[name]

                def step(j):
                    split_hi(act, L, j)
                    if j.i is None and j.c == 0 and norm is not None:
                        std(norm)
                    q = q0 - 44
                    for i, y in enumerate((T_g, T_u)):
                        act.wait_ge(g3_in, j.v(2, 2 * q + 1 + i))
                        nc.scalar.activation(y[:], GP[:, i, 2:SEQ + 2], ACT.Identity, scale=vec("conv3_w", j.plus(88 + 22 * i + j0)),
                                             bias=vec("conv3_b", j.plus(22 * i + j0))).then_inc(c3_y, 1)
                    act.wait_ge(gate_in, j.v(1, 8 + q0 + 1))
                    nc.scalar.activation(T_act[:], T_g[:], ACT.Silu).then_inc(gate_act, 1)
                    hid_hi(j, q0)
                steps(act, L.n, step, first=1, last=2)

            conv_gate_steps("gu2a", 0, norm=FFN_PRE)
            add_steps("dn2a")
            conv_gate_steps("gu2b", 11)
            add_steps("dn2b")
            std(FFN_POST)

        @block.gpsimd
        def _(pool):
            nc.gpsimd.memset(epst[:], EPS).then_inc(eps_set, 1)
            nc.gpsimd.memset(U[:, :, 0:CONV_WIDTH - 1], 0.0).then_inc(pads_set, 1)
            pool.wait_ge(pads_set, 1)
            nc.gpsimd.memset(table[BUCKETS:BUCKETS + 1, :], NEG).then_inc(tab_pad, 1)

            def lo_of(u, kt):
                b = u.parity
                n = kt * COLS
                pool.wait_ge(w_hi, u.v(1, 1))
                nc.gpsimd.tensor_tensor(W_lo[b][:, 0:n], W_raw[b][:, 0:n], W_hi[b][:, 0:n].bitcast(F32),
                                        ALU.subtract).then_inc(w_lo, 1)

            def split_lo(L, j):
                u = j.plus(L.base + 2)
                if u.i is None and u.c >= units:
                    return
                lo_of(u, L.kt if u.i is not None else kts[u.c])

            def square(n, m, ssum0=0):
                k = m.plus(0)
                src = X[:, bass.ds(m.v(), 1), :].rearrange("p o n -> p (o n)")
                if n in X_BASE:
                    pool.wait_ge(x_ready, m.v(1, X_BASE[n] + 1))
                elif n:
                    src = Y[:, bass.ds(m.v(), 1), :].rearrange("p o n -> p (o n)")
                    pool.wait_ge(y_ready, m.v(1, Y_BASE[n] + 1))
                if m.i is None and m.c == 0:
                    if n == 1:
                        pool.wait_ge(ln_sum_ready, 1)
                    elif n:
                        pool.wait_ge(stat_ready, n)
                    nc.gpsimd.tensor_tensor(SSUM[:], src, src, ALU.mult).then_inc(ss_made, 1)
                else:
                    pool.wait_ge(ss_made, m.v(1, 8 * n))
                    nc.gpsimd.tensor_tensor(SQ[:, 0, :], src, src, ALU.mult).then_inc(sq_made, 1)
                    pool.wait_ge(sq_made, m.v(1, 7 * n))
                    nc.gpsimd.tensor_tensor(SSUM[:], SSUM[:], SQ[:, 0, :], ALU.add).then_inc(ss_made, 1)

            pool.wait_ge(tab_pad, 1)
            lo_of(At(0), kts[0])
            lo_of(At(1), kts[1])
            pool.wait_ge(x_in, 16)
            for m in range(DT):
                square(0, At(m))
            L = layers["pw1"]
            steps(pool, L.n, lambda j: split_lo(L, j), last=2)
            pool.wait_ge(stat_ready, 1)
            for m in range(DT):
                pool.wait_ge(conv_made, m + 1)
                if m == 0:
                    nc.gpsimd.tensor_copy(SSUM[:], CV[:, 0, :]).then_inc(ln_sum, 1)
                else:
                    pool.wait_ge(ln_sum, m)
                    nc.gpsimd.tensor_tensor(SSUM[:], SSUM[:], CV[:, m, :], ALU.add).then_inc(ln_sum, 1)

            def add_steps(name, norm=None):
                L = layers[name]

                def step(j):
                    split_lo(L, j)
                    if norm is not None:
                        square(norm, At(2 * j.c, None if j.i is None else j.i * 2))
                        square(norm, At(2 * j.c + 1, None if j.i is None else j.i * 2))
                steps(pool, L.n, step, first=1 if norm is not None else 0, last=2)

            def gate_steps(name):
                L = layers[name]
                steps(pool, L.n, lambda j: split_lo(L, j), last=2)

            add_steps("pw2", FFN0)
            gate_steps("gu0a")
            add_steps("dn0a")
            gate_steps("gu0b")
            add_steps("dn0b", MIX1)
            L = layers["qkv"]
            for j in range(L.n):
                split_lo(L, At(j))
                if j == 0:
                    nc.gpsimd.memset(B2[:], NEG).then_inc(b2_set, 1)
            add_steps("wo", FFN1)
            gate_steps("gu1a")
            add_steps("dn1a")
            gate_steps("gu1b")
            add_steps("dn1b", FINAL)
            for m in range(DT):
                square(MIX_PRE, At(m))

            L = layers["inp"]

            def rope(j):
                r = ROPE_UNITS.index(j)
                dst = {"iq": IQ, "rq": RQK, "rk": RQK, "aq": AQ}[INP_KINDS[j]]
                m0 = {1: 0, 2: 2, 3: 0, 4: 2, 5: 4, 6: 6, 11: 0, 12: 2}[j]
                if j == 1:
                    pool.wait_ge(cs_in, 16)
                for i in range(2):
                    pool.wait_ge(rt_made, 2 * j + 1 + i)
                    nc.gpsimd.tensor_tensor(dst[:, m0 + i, :], T4[2 * (j % 2) + i][:], CS[:, 0, :],
                                            ALU.mult).then_inc(rope_c, 1)
                for i in range(2):
                    pool.wait_ge(rope_s, 2 * r + 1 + i)
                    pool.wait_ge(rope_c, 2 * r + 1 + i)
                    nc.gpsimd.tensor_tensor(dst[:, m0 + i, :], dst[:, m0 + i, :], T4[2 * (j % 2) + i][:],
                                            ALU.add).then_inc(rope_made, 1)

            for j in range(L.n):
                split_lo(L, At(j))
                if j - 1 in ROPE_UNITS:
                    rope(j - 1)
            rope(L.n - 1)
            add_steps("wout", MIX_POST)
            for m in range(DT):
                square(FFN_PRE, At(m))
            nc.gpsimd.memset(GP[:, :, 0:2], 0.0).then_inc(pad3_set, 1)
            gate_steps("gu2a")
            add_steps("dn2a")
            gate_steps("gu2b")
            add_steps("dn2b", FFN_POST)

        @block.vector
        def _(dve):
            dve.wait_ge(x_in, 16)
            dve.wait_ge(const_in, 32)
            dve.wait_ge(tab_in, 32)
            dve.wait_ge(tab_pad, 1)
            nc.vector.tensor_copy(table_wide[:], table[:].unsqueeze(2).to_broadcast([BUCKETS + 1, 12, P])).then_inc(tab_wide, 1)

            def h_lo(n, gain, m):
                dve.wait_ge(h_hi_made, m.v(1, H_BASE[n] + 1))
                dst = H_lo[:, bass.ds(m.v(), 1), :].rearrange("p o n -> p (o n)")
                hi = H_hi[:, bass.ds(m.v(), 1), :].rearrange("p o n -> p (o n)").bitcast(F32)
                src = X[:, bass.ds(m.v(), 1), :].rearrange("p o n -> p (o n)")
                nc.vector.scalar_tensor_tensor(out=dst, in0=src, scalar=vec(gain, m), in1=hi, op0=ALU.mult,
                                               op1=ALU.subtract).then_inc(h_lo_made, 1)

            def rms(n):
                dve.wait_ge(std_made, n + 1)
                nc.vector.reciprocal(R[:], STD[:]).then_inc(r_made, 1)
                dve.wait_ge(r_made, n + 1)

            for m in range(DT):
                h_lo(0, "norm_mix0", At(m))

            L = layers["pw1"]
            HALO = CONV_WIDTH - 1
            taps = [0]

            def conv(m):
                dst = (CV[:, m, :], CVacc[:])
                for t in range(CONV_WIDTH):
                    w = vec("w_dw", t * DT + m)
                    src = U[:, m, t:t + SEQ]
                    if t >= 2:
                        dve.wait_ge(conv_step, taps[0] - 1)
                    if t == 0:
                        i = nc.vector.tensor_scalar(dst[0], src, w, vec("b_dw", m), ALU.mult, ALU.add)
                    elif t == 1:
                        if taps[0] > 1:
                            dve.wait_ge(conv_step, taps[0] - 1)
                        i = nc.vector.tensor_scalar(dst[1], src, w, None, ALU.mult)
                    else:
                        i = nc.vector.scalar_tensor_tensor(out=dst[t % 2], in0=src, scalar=w, in1=dst[t % 2],
                                                           op0=ALU.mult, op1=ALU.add)
                    i.then_inc(conv_step, 1)
                    taps[0] += 1
                dve.wait_ge(conv_step, taps[0])
                nc.vector.tensor_tensor(dst[0], dst[0], dst[1], ALU.add).then_inc(conv_made, 1)
                dve.wait_ge(conv_made, m + 1)

            dve.wait_ge(pads_set, 1)
            for j in range(L.n):
                u = At(L.base + j)
                if j == 0:
                    rms(0)
                dve.wait_ge(acc_ready, u.v(2, 2))
                b = u.parity
                if j:
                    dve.wait_ge(gate_act, j)
                nc.vector.tensor_tensor(T_g[:], PS[2 * b + 1][:], R[:], ALU.mult).then_inc(gate_in, 1)
                if j:
                    dve.wait_ge(glu_made, j)
                nc.vector.tensor_tensor(T_u[:], PS[2 * b][:], R[:], ALU.mult).then_inc(acc_free, 1)
                dve.wait_ge(gate_act, j + 1)
                dve.wait_ge(acc_free, j + 1)
                nc.vector.scalar_tensor_tensor(out=U[:, j, HALO:HALO + SEQ], in0=T_u[:], scalar=vec("b_pw1", j),
                                               in1=T_act[:], op0=ALU.add, op1=ALU.mult).then_inc(glu_made, 1)
                dve.wait_ge(glu_made, j + 1)
                conv(j)
            dve.wait_ge(mu_made, 1)
            for m in range(DT):
                nc.vector.tensor_tensor(CV[:, m, :], CV[:, m, :], STD[:], ALU.subtract).then_inc(xc_made, 1)
            dve.wait_ge(ln_std, 1)
            nc.vector.reciprocal(T_g[:], STD[:]).then_inc(ln_r, 1)
            dve.wait_ge(ln_r, 1)
            for m in range(DT):
                nc.vector.tensor_tensor(CV[:, m, :], CV[:, m, :], T_g[:], ALU.mult).then_inc(ln_scaled, 1)
            dve.wait_ge(scr_out, 16)
            for m in range(DT):
                dve.wait_ge(ln_hi_made, m + 1)
                nc.vector.tensor_tensor(HID_lo[:, m, :], CV[:, m, :], HID_hi[:, m, :].bitcast(F32),
                                        ALU.subtract).then_inc(ln_lo_made, 1)

            def add_steps(name, x0, norm=None, gain=None, bias=None):
                L = layers[name]

                def step(j):
                    u = j.plus(L.base)
                    b = u.parity
                    for half in range(2):
                        m = At(2 * j.c + half, None if j.i is None else j.i * 2)
                        dve.wait_ge(acc_ready, u.v(2, half + 1))
                        x = X[:, bass.ds(m.v(), 1), :].rearrange("p o n -> p (o n)")
                        if bias is None:
                            i = nc.vector.tensor_tensor(x, x, PS[2 * b + half][:], ALU.add)
                        else:
                            i = nc.vector.scalar_tensor_tensor(out=x, in0=PS[2 * b + half][:], scalar=vec(bias, m),
                                                               in1=x, op0=ALU.add, op1=ALU.add)
                        i.then_inc(x_ready, 1) if x0 is not None else i.then_inc(x_half, 1)
                    if x0 is not None:
                        dve.wait_ge(x_ready, j.v(2, x0 + 2))
                    else:
                        dve.wait_ge(x_half, j.v(2, (0 if name == "dn0a" else 8) + 2))
                    nc.vector.sem_inc(acc_free, 1)
                    if norm is not None:
                        for half in range(2):
                            h_lo(norm, gain, At(2 * j.c + half, None if j.i is None else j.i * 2))
                steps(dve, L.n, step)

            def gate_steps(name, norm=None):
                L, q0 = layers[name], gu_base[name]

                def step(j):
                    u = j.plus(L.base)
                    b = u.parity
                    if j.i is None and j.c == 0 and norm is not None:
                        rms(norm)
                    dve.wait_ge(acc_ready, u.v(2, 1))
                    nc.vector.tensor_tensor(T_g[:], PS[2 * b][:], R[:], ALU.mult).then_inc(gate_in, 1)
                    dve.wait_ge(acc_ready, u.v(2, 2))
                    nc.vector.tensor_tensor(T_u[:], PS[2 * b + 1][:], R[:], ALU.mult).then_inc(acc_free, 1)
                    dve.wait_ge(acc_free, u.v(1, 1))
                    hidden(j, q0)
                steps(dve, L.n, step, first=1)

            def hidden(j, q0):
                dve.wait_ge(gate_act, j.v(1, 8 + q0 + 1))
                nc.vector.tensor_tensor(T_hid[:], T_u[:], T_act[:], ALU.mult).then_inc(hid_made, 1)
                dve.wait_ge(hid_hi_made, j.v(1, q0 + 1))
                k = bass.ds(j.v(), 1)
                hi = HID_hi[:, k, :].rearrange("p o n -> p (o n)").bitcast(F32)
                nc.vector.tensor_tensor(HID_lo[:, k, :].rearrange("p o n -> p (o n)"), T_hid[:], hi,
                                        ALU.subtract).then_inc(hid_lo_made, 1)
                dve.wait_ge(hid_lo_made, j.v(1, q0 + 1))

            add_steps("pw2", 0, FFN0, "norm_ffn0", bias="b_pw2")
            gate_steps("gu0a", norm=FFN0)
            add_steps("dn0a", None)
            gate_steps("gu0b")
            add_steps("dn0b", 8, MIX1, "norm_mix1")

            def take_pair(t):
                dve.wait_ge(o_ps, t + 1)
                g = t // 2
                nc.vector.tensor_copy(unpermuted(OU[:, t, :], g), blocked(PS[4 + t % 2][:], g)).then_inc(ou_made, 1)

            L = layers["qkv"]
            rms(MIX1)
            for j in range(L.n):
                u = At(L.base + j)
                for half in range(2):
                    dve.wait_ge(acc_ready, u.v(2, 1 + half))
                    m = 2 * j + half
                    g = m % 6 // 2
                    nc.vector.tensor_tensor(permuted(VQK[:, m, :], g), by_step(PS[2 * u.parity + half][:], g),
                                            by_step(R[:], g), ALU.mult).then_inc(qkv_made, 1)
                dve.wait_ge(qkv_made, 2 * j + 2)
                nc.vector.sem_inc(acc_free, 1)
            dve.wait_ge(bias_in, 96)
            for n, (h, blks) in enumerate(JOBS):
                g, hh = h // GROUP_HEADS, h % GROUP_HEADS
                dve.wait_ge(s_made, n + 1)
                if n >= 2:
                    dve.wait_ge(e_made, n - 1)
                for blk, c, w, keys in blks:
                    bias = (B0[:, hh, 256 - w:256], B1[:, hh, :], B2[:, hh, :])[g]
                    last = nc.vector.scalar_tensor_tensor(out=L1[:, n % 2, c:c + w], in0=PS[n % 2][:, c:c + w],
                                                          scalar=HD ** -0.5, in1=bias, op0=ALU.mult, op1=ALU.add)
                last.then_inc(l_made, 1)
                dve.wait_ge(l_made, n + 1)
                for blk, c, w, keys in blks:
                    last = nc.vector.reduce_max(MD[:, 0, blk, h:h + 1], L1[:, n % 2, c:c + w], AX.X)
                last.then_inc(m_made, 1)
                dve.wait_ge(m_made, n + 1)
                b0, nb = blks[0][0], len(blks)
                nc.vector.tensor_scalar(NM[:, n % 2, 0:nb], MD[:, 0, b0:b0 + nb, h:h + 1].rearrange("p b o -> p (b o)"),
                                        -1.0, None, ALU.mult).then_inc(nm_made, 1)
                if h % 2 == 1 and blks[-1][0] == 3:
                    pass
                if n >= 1:
                    hp, bp = JOBS[n - 1]
                    if hp % 2 == 1 and bp[-1][0] == 3:
                        take_pair(hp // 2)
            take_pair(5)
            dve.wait_ge(row_made, 3)
            nc.vector.tensor_tensor(ROW_max[:], ROW_w[:, 0, :], ROW_w[:, 1, :], ALU.max).then_inc(rowmax, 1)
            dve.wait_ge(rowmax, 1)
            nc.vector.tensor_tensor(ROW_max[:], ROW_max[:], ROW_w[:, 2, :], ALU.max).then_inc(rowmax, 1)
            dve.wait_ge(rowmax, 2)
            for g in range(3):
                last = nc.vector.tensor_tensor(ROW_w[:, g, :], ROW_w[:, g, :], ROW_max[:], ALU.subtract)
            last.then_inc(rowd, 1)
            dve.wait_ge(roww, 1)
            dve.wait_ge(row_made, 6)
            nc.vector.tensor_tensor(ROW_den[:], ROW_den[:], ROW_w[:], ALU.mult).then_inc(rowwd, 1)
            dve.wait_ge(rowwd, 1)
            nc.vector.tensor_tensor(ROW_sum[:], ROW_den[:, 0, :], ROW_den[:, 1, :], ALU.add).then_inc(rows_, 1)
            dve.wait_ge(rows_, 1)
            nc.vector.tensor_tensor(ROW_sum[:], ROW_sum[:], ROW_den[:, 2, :], ALU.add).then_inc(rows_, 1)
            dve.wait_ge(rows_, 2)
            nc.vector.reciprocal(ROW_max[:], ROW_sum[:]).then_inc(rows_, 1)
            dve.wait_ge(rows_, 3)
            for g in range(3):
                last = nc.vector.tensor_tensor(ROW_w[:, g, :], ROW_w[:, g, :], ROW_max[:], ALU.mult)
            last.then_inc(rowf, 1)
            for t in range(6):
                dve.wait_ge(f_ps, t + 1)
                nc.vector.tensor_tensor(T4[t % 2][:], OU[:, t, :], PS[6 + t % 2][:], ALU.mult).then_inc(o_made, 1)
                dve.wait_ge(o_hi_made, t + 1)
                nc.vector.tensor_tensor(HID_lo[:, t, :], T4[t % 2][:], HID_hi[:, t, :].bitcast(F32),
                                        ALU.subtract).then_inc(o_lo_made, 1)
                dve.wait_ge(o_lo_made, t + 1)

            add_steps("wo", 16, FFN1, "norm_ffn1")
            gate_steps("gu1a", norm=FFN1)
            add_steps("dn1a", None)
            gate_steps("gu1b")
            add_steps("dn1b", 24)
            rms(FINAL)
            for m in range(DT):
                nc.vector.scalar_tensor_tensor(out=X[:, m, :], in0=X[:, m, :], scalar=vec("final", m), in1=R[:],
                                               op0=ALU.mult, op1=ALU.mult).then_inc(x_ready, 1)
            for m in range(DT):
                h_lo(MIX_PRE, "mix_pre", At(m))

            L = layers["inp"]

            def post(j):
                if INP_KINDS[j] == "kv":
                    dve.wait_ge(cs_in, 16)
                    for i, dst in enumerate((KK, II)):
                        dve.wait_ge(kv_ps, 2 * i + 1)
                        nc.vector.tensor_tensor(dst[:], AUX[2 * i][:], CS[:, 0, :], ALU.mult).then_inc(kv_c, 1)
                        dve.wait_ge(kv_ps, 2 * i + 2)
                        nc.vector.tensor_tensor(L2k[i], AUX[2 * i + 1][:], CS[:, 1, :], ALU.mult).then_inc(kv_s, 1)
                        dve.wait_ge(kv_s, i + 1)
                        dve.wait_ge(kv_c, i + 1)
                        nc.vector.tensor_tensor(dst[:], dst[:], L2k[i], ALU.add).then_inc(kv_made, 1)
                    dve.wait_ge(tr_ps, 1)
                    nc.vector.tensor_copy(AV[:], AUX[0][:].rearrange("p (b n) -> p b n", b=4)[:, :, HD:2 * HD]).then_inc(av_made, 1)
                    dve.wait_ge(tr_ps, 2)
                    nc.vector.tensor_scalar(IW[:], AUX[1][:].rearrange("p (b n) -> p b n", b=4)[:, :, HD:HD + 8],
                                            8.0 ** -0.5 * HD ** -0.5, None, ALU.mult).then_inc(av_made, 1)
                elif j in ROPE_UNITS:
                    r = ROPE_UNITS.index(j)
                    for i in range(2):
                        dve.wait_ge(sw_ps, 2 * r + 1 + i)
                        dve.wait_ge(rope_c, 2 * r + 1 + i)
                        nc.vector.tensor_tensor(T4[2 * (j % 2) + i][:], AUX[i][:], CS[:, 1, :], ALU.mult).then_inc(rope_s, 1)

            def index_sum(b):
                w = P * (b + 1)
                if b == 1:
                    dve.wait_ge(av_made, 2)
                for h in range(8):
                    n = 8 * (b - 1) + h
                    dve.wait_ge(idx_rel, n + 1)
                    dst = ISC[:, b - 1, 0:w]
                    if h == 0:
                        i = nc.vector.tensor_scalar(dst, SQ[:, n % 2, 0:w], IW[:, b, h:h + 1], None, ALU.mult)
                    else:
                        dve.wait_ge(isc_made, n)
                        i = nc.vector.scalar_tensor_tensor(out=dst, in0=SQ[:, n % 2, 0:w], scalar=IW[:, b, h:h + 1],
                                                           in1=dst, op0=ALU.mult, op1=ALU.add)
                    i.then_inc(isc_made, 1)
                dve.wait_ge(isc_made, 8 * b)
                dst = ISC[:, b - 1, b * P:(b + 1) * P]
                nc.vector.scalar_tensor_tensor(out=dst, in0=later, scalar=-3.0e38, in1=dst, op0=ALU.mult,
                                               op1=ALU.add).then_inc(isc_mask, 1)

            rounds = [(b, i) for b in (1, 2, 3) for i in range(TOPK // 8)]

            def choose(count):
                for _ in range(count):
                    b, i = rounds.pop(0)
                    n = (b - 1) * (TOPK // 8) + i
                    w = P * (b + 1)
                    src = ISC[:, b - 1, 0:w] if i == 0 else WK[:, 0:w]
                    if i == 0:
                        dve.wait_ge(isc_mask, b)
                        if b > 1:
                            dve.wait_ge(left_out, b - 1)
                    if n:
                        dve.wait_ge(top_rep, n)
                    nc.vector.max(TOP8[:], src).then_inc(top_max, 1)
                    dve.wait_ge(top_max, n + 1)
                    nc.vector.match_replace(WK[:, 0:w], TOP8[:], src, -3.4e38).then_inc(top_rep, 1)
                    if i == TOPK // 8 - 1:
                        dve.wait_ge(top_rep, n + 1)
                        nc.vector.tensor_tensor(ISC[:, b - 1, 0:w], ISC[:, b - 1, 0:w], WK[:, 0:w],
                                                ALU.is_equal).then_inc(left_out, 1)

            for j in range(L.n):
                u = At(L.base + j)
                if j == 0:
                    rms(MIX_PRE)
                if j >= 2:
                    k = INP_KINDS[j - 2]
                    if k == "kv":
                        dve.wait_ge(tr_ps, 2)
                    elif j - 2 in ROPE_UNITS:
                        dve.wait_ge(rope_made, 2 * ROPE_UNITS.index(j - 2) + 2)
                    elif k == "rv":
                        dve.wait_ge(rv_ps, 2 * (j - 2 - 7) + 2)
                    else:
                        dve.wait_ge(rg_made, 2 * (j - 2 - 9) + 2)
                for half in range(2):
                    dve.wait_ge(acc_ready, u.v(2, 1 + half))
                    nc.vector.tensor_tensor(T4[2 * (j % 2) + half][:], PS[2 * u.parity + half][:], R[:],
                                            ALU.mult).then_inc(rt_made, 1)
                dve.wait_ge(rt_made, 2 * j + 2)
                nc.vector.sem_inc(acc_free, 1)
                if j:
                    post(j - 1)
                if 4 <= j <= 6:
                    index_sum(j - 3)
                if j in TOPK_AFTER:
                    choose(TOPK_AFTER[j])
            post(L.n - 1)

            def ret_out(t):
                dve.wait_ge(rstd, t + 1)
                nc.vector.reciprocal(L2[:, 1, :], STD[:]).then_inc(rrec, 1)
                dve.wait_ge(rrec, t + 1)
                if t:
                    dve.wait_ge(m_lo_made, t)
                nc.vector.tensor_tensor(E2[:, 0, :], AUX[t % 2][:], L2[:, 1, :], ALU.mult).then_inc(ro1, 1)
                dve.wait_ge(ro1, t + 1)
                nc.vector.tensor_tensor(E2[:, 0, :], E2[:, 0, :], GS[:, t, :], ALU.mult).then_inc(ro2, 1)
                dve.wait_ge(m_hi_made, t + 1)
                nc.vector.tensor_tensor(H_lo[:, t, :], E2[:, 0, :], H_hi[:, t, :].bitcast(F32),
                                        ALU.subtract).then_inc(m_lo_made, 1)

            dve.wait_ge(rope_made, 16)
            for n, (h, mb) in enumerate(RET_JOBS):
                w = SEQ - P * mb
                dve.wait_ge(rs_ps, n + 1)
                if mb == 0:
                    dve.wait_ge(d_in, 16 * (h + 1) if h >= 1 else 32)
                if n >= 2:
                    dve.wait_ge(ro_ps, n - 1)
                nc.vector.tensor_tensor(T4[n % 2][:, 0:w], PS[n % 2][:, 0:w], SQ[:, h % 2, 0:w], ALU.mult).then_inc(rd_made, 1)
                if n % 8 == 7 and n > 8:
                    ret_out(n // 8 - 1)
            ret_out(3)

            for n, (t, b, half) in enumerate(DSA_JOBS):
                w = P * (b + 1)
                dve.wait_ge(a_s, n + 1)
                if n >= 2:
                    dve.wait_ge(a_e, n - 1)
                out_mask = later if b == 0 else ISC[:, b - 1, 0:w]
                if n == 0:
                    dve.wait_ge(left_out, 3)
                    dve.wait_ge(m_lo_made, 4)
                nc.vector.scalar_tensor_tensor(out=L2[:, n % 2, 0:w], in0=out_mask, scalar=NEG, in1=PS[n % 2][:, 0:w],
                                               op0=ALU.mult, op1=ALU.add).then_inc(a_l, 1)
                dve.wait_ge(a_l, n + 1)
                nc.vector.reduce_max(NM2[:, n % 2:n % 2 + 1], L2[:, n % 2, 0:w], AX.X).then_inc(a_m, 1)
                dve.wait_ge(a_m, n + 1)
                nc.vector.tensor_scalar(DEN[:, n % 2, 0:1], NM2[:, n % 2:n % 2 + 1], -HD ** -0.5, None, ALU.mult).then_inc(a_nm, 1)
                dve.wait_ge(a_e, n + 1)
                nc.vector.reciprocal(DEN[:, n % 2, 2:3], DEN[:, n % 2, 1:2]).then_inc(a_rd, 1)
                dve.wait_ge(a_rd, n + 1)
                if n >= 2:
                    dve.wait_ge(a_pt_ps, n - 1)
                nc.vector.tensor_scalar(DG[:, n % 2, :], ident, DEN[:, n % 2, 2:3], None, ALU.mult).then_inc(a_dg, 1)
                if n % 8 == 7:
                    dve.wait_ge(m_hi_made, 4 + t + 1)
                    nc.vector.tensor_tensor(H_lo[:, 4 + t, :], AUX[t % 2][:], H_hi[:, 4 + t, :].bitcast(F32),
                                            ALU.subtract).then_inc(m_lo_made, 1)

            def y_steps(name, y0, add):
                L = layers[name]

                def step(j):
                    u = j.plus(L.base)
                    for half in range(2):
                        dve.wait_ge(acc_ready, u.v(2, half + 1))
                        m = At(2 * j.c + half, None if j.i is None else j.i * 2)
                        y = Y[:, bass.ds(m.v(), 1), :].rearrange("p o n -> p (o n)")
                        ps = PS[2 * u.parity + half][:]
                        if add:
                            i = nc.vector.tensor_tensor(y, ps, y, ALU.add)
                        else:
                            i = nc.vector.tensor_copy(y, ps)
                        i.then_inc(x_half, 1) if y0 is None else i.then_inc(y_ready, 1)
                    if y0 is None:
                        dve.wait_ge(x_half, j.v(2, 16 + 2))
                    else:
                        dve.wait_ge(y_ready, j.v(2, y0 + 2))
                    nc.vector.sem_inc(acc_free, 1)
                steps(dve, L.n, step)

            def add_normed(n, gain, k):
                rms(n)
                for m in range(DT):
                    if m >= 2 or k:
                        dve.wait_ge(x_ready, 40 + 8 * k + m - 1)
                    nc.vector.scalar_tensor_tensor(out=T4[m % 2][:], in0=Y[:, m, :], scalar=vec(gain, m), in1=R[:],
                                                   op0=ALU.mult, op1=ALU.mult).then_inc(f_applied, 1)
                    dve.wait_ge(f_applied, 8 * k + m + 1)
                    nc.vector.tensor_tensor(X[:, m, :], X[:, m, :], T4[m % 2][:], ALU.add).then_inc(x_ready, 1)

            y_steps("wout", 0, False)
            add_normed(MIX_POST, "mix_post", 0)
            for m in range(DT):
                h_lo(FFN_PRE, "ffn_pre", At(m))

            def conv_gate_steps(name, j0, norm=None):
                L, q0 = layers[name], gu_base[name]
                q = q0 - 44

                def step(j):
                    u = j.plus(L.base)
                    b = u.parity
                    if j.i is None and j.c == 0 and norm is not None:
                        rms(norm)
                        dve.wait_ge(pad3_set, 1)
                    for i in range(2):
                        dve.wait_ge(acc_ready, u.v(2, 1 + i))
                        nc.vector.tensor_tensor(GP[:, i, 2:SEQ + 2], PS[2 * b + i][:], R[:], ALU.mult).then_inc(g3_in, 1)
                    dve.wait_ge(g3_in, j.v(2, 2 * q + 2))
                    nc.vector.sem_inc(acc_free, 1)
                    for i, y in enumerate((T_g, T_u)):
                        dve.wait_ge(c3_y, j.v(2, 2 * q + 1 + i))
                        nc.vector.scalar_tensor_tensor(out=y[:], in0=GP[:, i, 1:SEQ + 1], scalar=vec("conv3_w", j.plus(44 + 22 * i + j0)),
                                                       in1=y[:], op0=ALU.mult, op1=ALU.add).then_inc(c3_y1, 1)
                    for i, y in enumerate((T_g, T_u)):
                        dve.wait_ge(c3_y1, j.v(2, 2 * q + 1 + i))
                        nc.vector.scalar_tensor_tensor(out=y[:], in0=GP[:, i, 0:SEQ], scalar=vec("conv3_w", j.plus(22 * i + j0)),
                                                       in1=y[:], op0=ALU.mult, op1=ALU.add).then_inc(gate_in if i == 0 else c3_y2, 1)
                    dve.wait_ge(c3_y2, j.v(1, q + 1))
                    hidden(j, q0)
                steps(dve, L.n, step, first=1)

            conv_gate_steps("gu2a", 0, norm=FFN_PRE)
            y_steps("dn2a", None, False)
            conv_gate_steps("gu2b", 11)
            y_steps("dn2b", 8, True)
            add_normed(FFN_POST, "ffn_post", 1)


def constants(np):
    f = np.float32
    cmat = np.zeros((P, 9, P), f)
    p = np.arange(P)
    cmat[p, 0, p] = 1
    cmat[:, 1] = 1
    cmat[(p // HD) * HD + (p + HD // 2) % HD, 2, p] = 1
    cmat[p % HD, 3, p] = 1
    cmat[(p + HD // 2) % HD, 4, p] = 1
    cmat[:, 5] = p[:, None] // HD == p[None, :] // HD
    for i in range(2):
        cmat[2 * i + p // HD, 6 + i, p] = 1
    cmat[:, 8] = p[None, :] > p[:, None]

    onehot = np.zeros((BUCKETS + 1, 3, DIAG), f)
    for g, (dilation, zero, far) in enumerate(((1, 2 * P - 1, P), (4, P - 1, P - 1), (16, 31, 31))):
        for x in range(DIAG):
            dist = zero - x
            if not 0 <= dist <= far:
                onehot[BUCKETS, g, x] = 1
                continue
            n = dist * dilation
            large = 16 + int(np.log(f(max(n, 1)) / f(16)) / f(np.log(2048 / 16)) * f(16)) if n >= 16 else 0
            onehot[n if n < 16 else min(large, BUCKETS - 1), g, x] = 1

    inv = f(10000.0) ** (-np.arange(0, HD, 2, dtype=f) / f(HD))
    ang = np.arange(SEQ, dtype=f)[:, None] * inv[None, :]
    cos, sin = np.cos(ang).T, np.sin(ang).T
    rotary = np.stack([np.concatenate([cos] * 4), np.concatenate([-sin, sin] * 2)], 1)

    diff = np.arange(SEQ)[None, :] - p[:, None]
    log_g = np.log(1.0 - 2.0 ** (-5.0 - np.arange(RET_HEADS)))
    decay = np.where(diff >= 0, np.exp(log_g[:, None, None] * np.maximum(diff, 0)), 0.0) * HD ** -0.5
    return {"cmat": cmat, "onehot": onehot, "rotary": rotary.astype(f), "decay": decay.astype(f)}


def kernel(**inputs):
    import numpy as np
    import concourse.bacc as bacc
    from concourse.bass_utils import run_bass_kernel_spmd as run

    g = {k: np.asarray(v) for k, v in inputs.items()}

    def rows(w, cols, kt):
        w = w[:, cols] if cols is not None else w
        k, n = w.shape
        return np.ascontiguousarray(w.reshape(k // P, P, n // COLS, COLS)[:].transpose(2, 1, 0, 3)
                                    .reshape(n // COLS, P, (k // P) * COLS))

    def paired(a, b):
        k, n = a.shape
        return np.stack([a.reshape(k, n // P, P), b.reshape(k, n // P, P)], 2).reshape(k, 2 * n)

    def tiles(v):
        v = v.reshape(-1, v.shape[-1] // P, P)
        return v.transpose(2, 0, 1).reshape(P, -1)

    arrays = {}
    pw1 = g["conv_w_pw1"][0]
    arrays["pw1"] = rows(paired(pw1[:, :D_MODEL], pw1[:, D_MODEL:]), None, 8)
    arrays["pw2"] = rows(g["conv_w_pw2"][0], None, 8)
    up2 = g["w_up_2"][0]
    gates = [g["ffn_w_gate"][0], g["ffn_w_gate"][1], up2[:, :FF_TILES * P]]
    ups = [g["ffn_w_up"][0], g["ffn_w_up"][1], up2[:, FF_TILES * P:]]
    downs = [g["ffn_w_down"][0], g["ffn_w_down"][1], g["w_down_2"][0]]
    qkv = g["attn_w_qkv"][0]
    arrays["qkv"] = rows(np.concatenate([qkv[:, 1536:], qkv[:, :1536]], 1), None, 8)
    arrays["wo"] = rows(g["attn_w_o"][0], None, 6)
    w_in = g["w_in_2"][0]
    arrays["inp"] = rows(np.concatenate([w_in[:, 2560:2688], w_in[:, 3200:3272], np.zeros((D_MODEL, 56), np.float32),
                                         w_in[:, 2688:3200], w_in[:, :2560]], 1), None, 8)
    arrays["wout"] = rows(g["w_out_2"][0], None, 8)
    arrays["rel_bias"] = g["rel_bias"]
    for l in range(3):
        gu = rows(paired(gates[l], ups[l]), None, 8)
        dn = downs[l]
        h = FF_HALF * P
        arrays[f"gu{l}a"], arrays[f"gu{l}b"] = gu[:FF_HALF], gu[FF_HALF:]
        arrays[f"dn{l}a"], arrays[f"dn{l}b"] = rows(dn[:h], None, 11), rows(dn[h:], None, 11)
    arrays["x"] = g["x"][0].T.reshape(DT, P, SEQ).transpose(1, 0, 2)
    parts = {"norm_mix0": g["norm_mix"][0], "norm_mix1": g["norm_mix"][1], "norm_ffn0": g["norm_ffn"][0],
             "norm_ffn1": g["norm_ffn"][1], "final": g["final_norm"], "b_pw1": g["conv_b_pw1"][0],
             "w_dw": g["conv_w_dw"][0], "b_dw": g["conv_b_dw"][0], "ln_g": g["conv_ln_g"][0],
             "ln_b": g["conv_ln_b"][0], "b_pw2": g["conv_b_pw2"][0],
             "mix_pre": g["mix_norm_pre_2"][0], "mix_post": g["mix_norm_post_2"][0],
             "ffn_pre": g["ffn_norm_pre_2"][0], "ffn_post": g["ffn_norm_post_2"][0],
             "conv3_w": g["conv_w_2"][0], "conv3_b": g["conv_b_2"][0]}
    arrays["vecs"] = np.concatenate([tiles(parts[n]) for n, _ in VECS], 1)
    arrays.update(constants(np))
    arrays = {k: np.ascontiguousarray(v) for k, v in arrays.items()}

    nc = bacc.Bacc("TRN2", target_bir_lowering=False, num_devices=1)
    aps = {k: nc.dram_tensor(f"in_{k}", v.shape, mybir.dt.from_np(v.dtype), kind="ExternalInput").ap()
           for k, v in arrays.items()}
    out = nc.dram_tensor("out", (P, DT, SEQ), F32, kind="ExternalOutput").ap()
    build(nc, aps, out)
    r = run(nc, [{f"in_{k}": v for k, v in arrays.items()}], core_ids=[0])
    y = r.results[0]["out"]
    return np.ascontiguousarray(np.asarray(y).transpose(1, 0, 2).reshape(D_MODEL, SEQ).T)[None]
```

```python
import concourse.bass as bass
from concourse import mybir
from concourse.alu_op_type import AluOpType as ALU
from contextlib import ExitStack

F32 = mybir.dt.float32
F32R = mybir.dt.float32r
ACT = mybir.ActivationFunctionType
AX = mybir.AxisListType

P = 128
SEQ = 512
D_MODEL = 1024
DT = D_MODEL // P
CONV_WIDTH = 31
FF_TILES = 22
FF_HALF = FF_TILES // 2
EPS = 1e-6
COLS = 256
UNIT_K = FF_HALF

LAYERS = [("pw1", 8, 8), ("pw2", 4, 8),
          ("gu0a", 11, 8), ("dn0a", 4, 11), ("gu0b", 11, 8), ("dn0b", 4, 11),
          ("qkv", 9, 8), ("wo", 4, 6),
          ("gu1a", 11, 8), ("dn1a", 4, 11), ("gu1b", 11, 8), ("dn1b", 4, 11),
          ("inp", 13, 8), ("wout", 4, 8),
          ("gu2a", 11, 8), ("dn2a", 4, 11), ("gu2b", 11, 8), ("dn2b", 4, 11)]

VECS = [("norm_mix0", 8), ("norm_mix1", 8), ("norm_ffn0", 8), ("norm_ffn1", 8), ("final", 8),
        ("b_pw1", 16), ("w_dw", CONV_WIDTH * 8), ("b_dw", 8), ("ln_g", 8), ("ln_b", 8), ("b_pw2", 8),
        ("mix_pre", 8), ("mix_post", 8), ("ffn_pre", 8), ("ffn_post", 8), ("conv3_w", 3 * 44), ("conv3_b", 44)]

MIX0, FFN0, MIX1, FFN1, FINAL, MIX_POST, FFN_PRE, FFN_POST = range(8)
X_BASE = {FFN0: 0, MIX1: 8, FFN1: 16, FINAL: 24, FFN_PRE: 40}
H_BASE = {MIX0: 0, FFN0: 8, MIX1: 16, FFN1: 24, FINAL: 32, FFN_PRE: 40}
Y_BASE = {MIX_POST: 0, FFN_POST: 8}

HD = 64
GROUP_HEADS = 4
BUCKETS = 32
NEG = -1e30
DIAG = 384
TOPK = 128
RET_HEADS = 8


CONV_DVE = 6
TAP_CHUNK = 16
CONV_CHUNKS = [(m, c, min(CONV_WIDTH, c + TAP_CHUNK)) for m in range(CONV_DVE, DT) for c in range(0, CONV_WIDTH, TAP_CHUNK)]
TAPS_PER_UNIT = 15


def dilated_jobs():
    jobs = []
    for h in range(12):
        if h < GROUP_HEADS:
            jobs.append((h, [(0, 0, 128, [0]), (1, 128, 256, [0, 1])]))
            jobs.append((h, [(2, 0, 256, [1, 2]), (3, 256, 256, [2, 3])]))
        else:
            jobs.append((h, [(b, 128 * b, 128, [b]) for b in range(4)]))
    return jobs


DSA_JOBS = [(t, b, half) for t in range(4) for b in range(4) for half in range(2)]
RET_JOBS = [(h, mb) for h in range(RET_HEADS) for mb in range(4)]
INP_KINDS = ["kv", "iq", "iq", "rq", "rq", "rk", "rk", "rv", "rv", "rg", "rg", "aq", "aq"]
ROPE_UNITS = [j for j, k in enumerate(INP_KINDS) if k in ("iq", "rq", "rk", "aq")]
TOPK_AFTER = {5: 4, 6: 4, 7: 8, 8: 8, 9: 8, 10: 8, 11: 8}


class Layer:

    def __init__(self, name, n, kt, base):
        self.name, self.n, self.kt, self.base = name, n, kt, base


class At:

    def __init__(self, c, i=None):
        self.c, self.i = c, i

    def v(self, mult=1, add=0):
        if self.i is None:
            return mult * self.c + add
        return self.i * (2 * mult) + (mult * self.c + add)

    def plus(self, n):
        return At(self.c + n, self.i)

    def half(self, mult, add):
        if self.i is None:
            return mult * (self.c // 2) + add
        return self.i * mult + (mult * (self.c // 2) + add)

    @property
    def parity(self):
        return self.c % 2


def steps(eng, n, step, first=0, last=0):
    pairs = (n - first - last) // 2
    if pairs < 2:
        pairs = 0
    for j in range(first):
        step(At(j))
    if pairs:
        with eng.Fori(0, pairs) as i:
            step(At(first, i))
            step(At(first + 1, i))
    for j in range(first + 2 * pairs, n):
        step(At(j))


def build(nc, a, out):
    layers, base = {}, 0
    for name, n, kt in LAYERS:
        layers[name] = Layer(name, n, kt, base)
        base += n
    units = base
    order = [layers[x[0]] for x in LAYERS]
    kts = [l.kt for l in order for _ in range(l.n)]
    vec_at, n_vec = {}, 0
    for name, n in VECS:
        vec_at[name] = n_vec
        n_vec += n

    ctx = ExitStack()
    with ctx:
        top = [(nc.sbuf_base + 31) // 32 * 32]

        def sb(name, shape, dt=F32, at=None):
            size = 4
            for s in shape[1:]:
                size *= s
            size = (size + 31) // 32 * 32
            if at is None:
                at = top[0]
                top[0] += size
            return nc.alloc_sbuf_tensor_at(name, shape, dt, offset=at)

        X = sb("X", [P, DT, SEQ])
        H_hi = sb("H_hi", [P, DT, SEQ], F32R)
        H_lo = sb("H_lo", [P, DT, SEQ], F32R)
        W_raw = [sb(f"W_raw{b}", [P, UNIT_K * COLS]) for b in range(2)]
        W_hi = [sb(f"W_hi{b}", [P, UNIT_K * COLS], F32R) for b in range(2)]
        W_lo = [sb(f"W_lo{b}", [P, UNIT_K * COLS], F32R) for b in range(2)]
        cmat = sb("cmat", [P, 9, P])
        vecs = sb("vecs", [P, n_vec])
        epst = sb("epst", [P, 1])
        R = sb("R", [P, SEQ])
        STD = sb("STD", [P, SEQ])
        SSUM = sb("SSUM", [P, SEQ])
        SQ = sb("SQ", [P, 2, SEQ])
        T_g = sb("T_g", [P, SEQ])
        T_u = sb("T_u", [P, SEQ])
        T_act = sb("T_act", [P, SEQ])
        T_hid = sb("T_hid", [P, SEQ])
        FG = sb("FG", [P, DT])
        arena = top[0]
        HID_hi = sb("HID_hi", [P, FF_HALF, SEQ], F32R, at=arena)
        HID_lo = sb("HID_lo", [P, FF_HALF, SEQ], F32R, at=arena + FF_HALF * SEQ * 4)
        PADDED = SEQ + CONV_WIDTH - 1 + 2
        U = sb("U", [P, DT, PADDED], at=arena)
        CV = sb("CV", [P, DT, SEQ], at=arena + 2 * FF_HALF * SEQ * 4)
        VQK = sb("VQK", [P, 18, SEQ], at=arena)
        OU = sb("OU", [P, 6, SEQ], at=arena)
        ROW_w = sb("ROW_w", [GROUP_HEADS, 3, SEQ], at=arena + 12288)
        ROW_max = sb("ROW_max", [GROUP_HEADS, SEQ], at=arena + 18432)
        ROW_sum = sb("ROW_sum", [GROUP_HEADS, SEQ], at=arena + 20480)
        ROW_den = sb("ROW_den", [GROUP_HEADS, 3, SEQ], at=arena + 36864)
        B0 = sb("B0", [P, GROUP_HEADS, 256], at=arena + 36864)
        B1 = sb("B1", [P, GROUP_HEADS, P], at=arena + 40960)
        B2 = sb("B2", [P, GROUP_HEADS, P], at=arena + 43008)
        VT = sb("VT", [P, 6, 4, P], at=arena + 45056)
        L1 = sb("L1", [P, 2, SEQ], at=arena + 57344)
        E1 = sb("E1", [P, 2, SEQ], at=arena + 61440)
        PT1 = sb("PT1", [P, 2, SEQ], at=arena + 65536)
        MD = sb("MD", [P, 2, 4, 12], at=arena + 69632)
        NM = sb("NM", [P, 2, 4], at=arena + 70016)
        onehot = sb("onehot", [BUCKETS + 1, 3, DIAG], at=arena + 57344)
        table = sb("table", [BUCKETS + 1, 12], at=arena + 62080)
        table_wide = sb("table_wide", [BUCKETS + 1, 12, P], at=arena + 62208)
        fvec = sb("fvec", [P, 12, DIAG], at=arena + 26112)
        Y = sb("Y", [P, DT, SEQ], at=arena + 45056)
        GP = sb("GP", [P, 2, SEQ + 2], at=arena + 61440)
        AQ = sb("AQ", [P, 4, SEQ], at=arena)
        RQK = sb("RQK", [P, 8, SEQ], at=arena + 8192)
        RVT = sb("RVT", [P, 4, SEQ], at=arena + 24576)
        GS = sb("GS", [P, 4, SEQ], at=arena + 32768)
        IQ = sb("IQ", [P, 4, SEQ], at=arena + 40960)
        CS = sb("CS", [P, 2, SEQ], at=arena + 49152)
        KK = sb("KK", [P, SEQ], at=arena + 53248)
        II = sb("II", [P, SEQ], at=arena + 55296)
        ISC = sb("ISC", [P, 3, SEQ], at=arena + 57344)
        WK = sb("WK", [P, SEQ], at=arena + 63488)
        AV = sb("AV", [P, 4, HD], at=arena + 65536)
        IW = sb("IW", [P, 4, 8], at=arena + 66560)
        TOP8 = sb("TOP8", [P, 8], at=arena + 66688)
        DEN = sb("DEN", [P, 2, 3], at=arena + 66720)
        L2 = sb("L2", [P, 2, SEQ], at=arena + 40960)
        E2 = sb("E2", [P, 2, SEQ], at=arena + 45056)
        PT2 = sb("PT2", [P, 2, SEQ], at=arena + 49152)
        CVacc = T_hid
        UP_hi = sb("UP_hi", [P, DT - CONV_DVE, PADDED], F32R, at=arena + 17408)
        UP_lo = sb("UP_lo", [P, DT - CONV_DVE, PADDED], F32R, at=arena + 21760)
        tap_hi = sb("tap_hi", [P, CONV_WIDTH * DT], F32R, at=arena + 68352)
        tap_lo = sb("tap_lo", [P, CONV_WIDTH * DT], F32R, at=arena + 69344)
        RF = sb("RF", [P, SEQ], at=arena + 32768)
        SSUM2 = sb("SSUM2", [P, SEQ], at=arena + 61440)
        SQ2 = sb("SQ2", [P, 2, SEQ], at=arena + 63488)

        NM2 = sb("NM2", [P, 2], at=arena + 67776)
        L2k = [WK[:], ISC[:, 2, :]]
        T4 = [T_g, T_u, T_act, T_hid]
        bias_scratch = nc.dram_tensor("bias_scratch", (12, P, DIAG), F32, kind="Internal").ap()

        PS = [ctx.enter_context(nc.psum_tensor(f"PS{i}", [P, SEQ], F32)) for i in range(8)]
        AUX = PS[4:8]

        def vec(name, j, n=1):
            o = vec_at[name]
            if isinstance(j, At):
                return vecs[:, bass.ds(j.v(1, o), 1)]
            return vecs[:, o + j:o + j + 1]

        ident, ones, swap, dup, dupswap, headsum = (cmat[:, i, :] for i in range(6))
        sel = [cmat[0:GROUP_HEADS, 6 + i, :] for i in range(2)]
        later = cmat[:, 8, :]

        def tokens(ap, blk):
            return ap[:, blk * P:(blk + 1) * P]

        DILATION = (1, 4, 16)

        def permuted(ap, g):
            return ap.rearrange("p (r i) -> p i r", r=DILATION[g]) if g else ap

        def by_step(ap, g):
            return ap.rearrange("p (i r) -> p i r", r=DILATION[g]) if g else ap

        def unpermuted(ap, g):
            if g == 0:
                return ap
            if g == 1:
                return ap.rearrange("p (i b) -> p b i", b=4)
            return ap.rearrange("p (i r) -> p r i", r=16)

        def blocked(ap, g):
            if g == 0:
                return ap
            return ap.rearrange("p (b i) -> p b i", b=4 if g == 1 else 16)

        JOBS = dilated_jobs()

        def sem(name):
            return ctx.enter_context(nc.semaphore(name))

        x_in = [sem(f"x_in{i}") for i in range(4)]
        vec_in = sem("vec_in")
        const2_in = sem("const2_in")
        const_in = sem("const_in")
        eps_set = sem("eps_set")
        raw_in = [sem(f"raw_in{b}") for b in range(2)]
        w_hi = sem("w_hi")
        w_lo = sem("w_lo")
        acc_ready = sem("acc_ready")
        acc_free = sem("acc_free")
        x_ready = sem("x_ready")
        h_hi_made = sem("h_hi_made")
        h_lo_made = sem("h_lo_made")
        sq_made = sem("sq_made")
        ss_made = sem("ss_made")
        stat_ready = sem("stat_ready")
        std_made = sem("std_made")
        r_made = sem("r_made")
        gate_in = sem("gate_in")
        gate_act = sem("gate_act")
        hid_made = sem("hid_made")
        hid_hi_made = sem("hid_hi_made")
        hid_lo_made = sem("hid_lo_made")
        pads_set = sem("pads_set")
        glu_made = sem("glu_made")
        conv_step = sem("conv_step")
        conv_made = sem("conv_made")
        ln_sum = sem("ln_sum")
        ln_sum_ready = sem("ln_sum_ready")
        mu_made = sem("mu_made")
        xc_made = sem("xc_made")
        xc_sq = sem("xc_sq")
        ln_var_ready = sem("ln_var_ready")
        ln_std = sem("ln_std")
        ln_r = sem("ln_r")
        ln_scaled = sem("ln_scaled")
        ln_act = sem("ln_act")
        ln_hi_made = sem("ln_hi_made")
        ln_lo_made = sem("ln_lo_made")
        x_half = sem("x_half")
        out_done = sem("out_done")
        tab_wide = sem("tab_wide")
        pv_done = sem("pv_done")
        v_t = sem("v_t")
        v_tok = sem("v_tok")
        tab_in = sem("tab_in")
        tab_pad = sem("tab_pad")
        fvec_ps = sem("fvec_ps")
        fvec_made = sem("fvec_made")
        scr_out = sem("scr_out")
        b2_set = sem("b2_set")
        bias_in = sem("bias_in")
        qkv_made = sem("qkv_made")
        s_made = sem("s_made")
        l_made = sem("l_made")
        m_made = sem("m_made")
        nm_made = sem("nm_made")
        e_made = sem("e_made")
        pt_ps = sem("pt_ps")
        pt_made = sem("pt_made")
        ou_made = sem("ou_made")
        st_ps = sem("st_ps")
        row_made = sem("row_made")
        rowmax = sem("rowmax")
        rowd = sem("rowd")
        roww = sem("roww")
        rowwd = sem("rowwd")
        rows_ = sem("rows_")
        rowf = sem("rowf")
        f_ps = sem("f_ps")
        o_made = sem("o_made")
        o_hi_made = sem("o_hi_made")
        o_lo_made = sem("o_lo_made")
        y_ready = sem("y_ready")
        f_applied = sem("f_applied")
        cs_in = sem("cs_in")
        rt_made = sem("rt_made")
        sw_ps = sem("sw_ps")
        rope_c = sem("rope_c")
        rope_s = sem("rope_s")
        rope_made = sem("rope_made")
        kv_ps = sem("kv_ps")
        kv_c = sem("kv_c")
        kv_s = sem("kv_s")
        kv_made = sem("kv_made")
        tr_ps = sem("tr_ps")
        av_made = sem("av_made")
        rv_ps = sem("rv_ps")
        rv_tok = sem("rv_tok")
        rg_made = sem("rg_made")
        idx_ps = sem("idx_ps")
        idx_rel = sem("idx_rel")
        isc_made = sem("isc_made")
        isc_mask = sem("isc_mask")
        top_max = sem("top_max")
        top_rep = sem("top_rep")
        left_out = sem("left_out")
        d_in = sem("d_in")
        rs_ps = sem("rs_ps")
        rd_made = sem("rd_made")
        ro_ps = sem("ro_ps")
        r_sq = sem("r_sq")
        rsum_ps = sem("rsum_ps")
        rstd = sem("rstd")
        rrec = sem("rrec")
        ro1 = sem("ro1")
        ro2 = sem("ro2")
        m_hi_made = sem("m_hi_made")
        m_lo_made = sem("m_lo_made")
        a_s = sem("a_s")
        a_l = sem("a_l")
        a_m = sem("a_m")
        a_nm = sem("a_nm")
        a_e = sem("a_e")
        a_rd = sem("a_rd")
        a_dg = sem("a_dg")
        a_pt_ps = sem("a_pt_ps")
        a_pt = sem("a_pt")
        a_o = sem("a_o")
        c3_y = sem("c3_y")
        c3_y1 = sem("c3_y1")
        c3_y2 = sem("c3_y2")
        pad3_set = sem("pad3_set")
        g3_in = sem("g3_in")
        w_parts = sem("w_parts")
        u_hi = sem("u_hi")
        u_lo = sem("u_lo")
        diag_hi = sem("diag_hi")
        diag_lo = sem("diag_lo")
        conv_pe = sem("conv_pe")
        conv_pe_taken = sem("conv_pe_taken")
        fg_made = sem("fg_made")
        rf_sq = sem("rf_sq")
        rf_scaled = sem("rf_scaled")
        r_pair = sem("r_pair")
        t_applied = sem("t_applied")
        x1_made = sem("x1_made")
        ssum2 = sem("ssum2")
        ssum2_sq = sem("ssum2_sq")
        stat2_ready = sem("stat2_ready")
        std2_made = sem("std2_made")

        block = ctx.enter_context(nc.Block())

        def acc(u, half):
            return PS[2 * (u % 2) + half]

        gu_base = {f"gu{l}{h}": 22 * l + 11 * k for l in range(3) for k, h in enumerate("ab")}

        @block.sync
        def _(sp):
            def load(L, src, j):
                u = j.plus(L.base)
                b = u.parity
                if u.i is not None or u.c >= 2:
                    sp.wait_ge(w_lo, u.v(1, -1))
                n = L.kt * COLS
                sp.dma_start(W_raw[b][:, 0:n], src[bass.ds(j.v(), 1)].rearrange("o p n -> p (o n)") if j.i is not None else src[j.c]).then_inc(raw_in[b], 16)

            sp.dma_start(vecs[:], a["vecs"]).then_inc(vec_in, 16)
            for i in range(4):
                sp.dma_start(X[:, 2 * i:2 * i + 2, :], a["x"][:, 2 * i:2 * i + 2, :]).then_inc(x_in[i], 16)
                if i < 2:
                    load(order[0], a["pw1"], At(i))

            for k, L in enumerate(order):
                if k == 0:
                    with sp.Fori(0, L.n // 2 - 1) as i:
                        load(L, a[L.name], At(2, i))
                        load(L, a[L.name], At(3, i))
                    continue
                steps(sp, L.n, lambda j: load(L, a[L.name], j))
            sp.wait_ge(x_ready, 56)
            sp.dma_start(out, X[:]).then_inc(out_done, 16)
            sp.wait_ge(out_done, 16)

        @block.tensor
        def _(pe):
            def products(b, kt, half, x_hi, x_lo, ready=None, between=None):
                dst = PS[2 * b + half]
                for k in range(kt):
                    if ready is not None:
                        pe.wait_ge(ready[0], ready[1] + k + 1)
                    c = k * COLS + half * P
                    wh, wl = W_hi[b][:, c:c + P], W_lo[b][:, c:c + P]
                    nc.tensor.matmul(dst[:], wh, x_hi[:, k, :], start=(k == 0), stop=False)
                    nc.tensor.matmul(dst[:], wh, x_lo[:, k, :], start=False, stop=False)
                    last = nc.tensor.matmul(dst[:], wl, x_hi[:, k, :], start=False, stop=(k == kt - 1))
                    if between is not None and k % 2 and k < kt - 1:
                        between()
                last.then_inc(acc_ready, 1)
                if between is not None:
                    between()

            def unit(L, j, x_hi, x_lo, ready=None, between=None):
                u = j.plus(L.base)
                pe.wait_ge(w_lo, u.v(1, 1))
                if u.i is not None or u.c >= 2:
                    pe.wait_ge(acc_free, u.v(1, -1))
                products(u.parity, L.kt, 0, x_hi, x_lo, ready, between)
                products(u.parity, L.kt, 1, x_hi, x_lo, None, between)

            def rms_sum(n, tail=0):
                if n:
                    pe.wait_ge(std_made, n)
                pe.wait_ge(ss_made, 7 * (n + 1))
                last = nc.tensor.matmul(AUX[0][:], ones, SSUM[:], start=True, stop=True)
                last.then_inc(stat_ready, 1)

            def linear(name, x_hi=H_hi, x_lo=H_lo, ready=None, norm=None):
                L = layers[name]

                def step(j):
                    first = j.i is None and j.c == 0
                    unit(L, j, x_hi, x_lo, ready if first else None)
                    if first and norm is not None:
                        rms_sum(norm)
                steps(pe, L.n, step, first=1)

            pe.wait_ge(const_in, 16)
            linear("pw1", ready=(h_lo_made, 0), norm=0)
            pe.wait_ge(tab_wide, 1)
            pe.wait_ge(const2_in, 16)
            for h in range(12):
                if h >= 2:
                    pe.wait_ge(fvec_made, h - 1)
                nc.tensor.matmul(AUX[1 + h % 2][:, 0:DIAG], table_wide[:, h, :], onehot[:, h // GROUP_HEADS, :],
                                 start=True, stop=True).then_inc(fvec_ps, 1)
            pe.wait_ge(fvec_made, 12)
            for n, (m, t0, t1) in enumerate(CONV_CHUNKS):
                p, b = m - CONV_DVE, n % 2
                pe.wait_ge(diag_lo, n + 1)
                pe.wait_ge(diag_hi, n + 1)
                if t0 == 0:
                    pe.wait_ge(u_lo, p + 1)
                for t in range(t0, t1):
                    k = TAP_CHUNK * b + t - t0
                    d_hi = H_hi[:, k // 4, P * (k % 4):P * (k % 4 + 1)]
                    d_lo = H_lo[:, k // 4, P * (k % 4):P * (k % 4 + 1)]
                    x_hi, x_lo = UP_hi[:, p, t:t + SEQ], UP_lo[:, p, t:t + SEQ]
                    nc.tensor.matmul(AUX[1 + p][:], d_hi, x_hi, start=(t == 0), stop=False)
                    nc.tensor.matmul(AUX[1 + p][:], d_hi, x_lo, start=False, stop=False)
                    last = nc.tensor.matmul(AUX[1 + p][:], d_lo, x_hi, start=False, stop=(t == CONV_WIDTH - 1))
                last.then_inc(conv_pe, 1)
            pe.wait_ge(ln_sum, CONV_DVE)
            nc.tensor.matmul(AUX[3][:], ones, SSUM[:], start=True, stop=False)
            for m in range(CONV_DVE, DT):
                pe.wait_ge(conv_pe_taken, m - CONV_DVE + 1)
                last = nc.tensor.matmul(AUX[3][:], ones, CV[:, m, :], start=False, stop=(m == DT - 1))
            last.then_inc(ln_sum_ready, 1)
            for m in range(DT):
                pe.wait_ge(xc_sq, m + 1)
                nc.tensor.matmul(AUX[2][:], ones, SQ[:, m % 2, :], start=(m == 0), stop=(m == DT - 1)).then_inc(ln_var_ready, 1)
            linear("pw2", HID_hi, HID_lo, ready=(ln_lo_made, 0))

            def feed_forward(l, norm):
                linear(f"gu{l}a", ready=(h_lo_made, H_BASE[norm]), norm=norm)
                linear(f"dn{l}a", HID_hi, HID_lo, ready=(hid_lo_made, gu_base[f"gu{l}a"]))
                linear(f"gu{l}b")
                linear(f"dn{l}b", HID_hi, HID_lo, ready=(hid_lo_made, gu_base[f"gu{l}b"]))

            feed_forward(0, FFN0)

            linear("qkv", ready=(h_lo_made, H_BASE[MIX1]), norm=MIX1)
            for t in range(6):
                pe.wait_ge(qkv_made, t + 1)
                if t == 0:
                    pe.wait_ge(std_made, MIX1 + 1)
                if t >= 4:
                    pe.wait_ge(v_tok, t - 3)
                for b in range(4):
                    last = nc.tensor.transpose(AUX[t % 4][:, b * P:(b + 1) * P], tokens(VQK[:, t, :], b), ident)
                last.then_inc(v_t, 1)

            def dilated_scores(n):
                h, blks = JOBS[n]
                g, t, lo = h // GROUP_HEADS, h // 2, HD * (h % 2)
                if n == 0:
                    pe.wait_ge(qkv_made, 18)
                if n >= 2:
                    pe.wait_ge(l_made, n - 1)
                for blk, c, w, keys in blks:
                    q = tokens(VQK[lo:lo + HD, 6 + t, :], blk)
                    k = VQK[lo:lo + HD, 12 + t, :]
                    k = k[:, P * keys[0]:P * (keys[-1] + 1)] if g == 0 else tokens(k, blk)
                    last = nc.tensor.matmul(PS[n % 2][:, c:c + w], q, k, start=True, stop=True)
                last.then_inc(s_made, 1)

            dilated_scores(0)
            dilated_scores(1)
            def chunks(n):
                return [(blk, c + P * i, key) for blk, c, w, keys in JOBS[n][1] for i, key in enumerate(keys)]

            def dilated_values(n):
                h, blks = JOBS[n]
                t, lo = h // 2, HD * (h % 2)
                pe.wait_ge(pt_made, n + 1)
                if n == 0:
                    pe.wait_ge(v_tok, 6)
                if h % 2 == 0 and blks[0][0] == 0 and t >= 2:
                    pe.wait_ge(ou_made, t - 1)
                ch = chunks(n)
                for i, (blk, c, key) in enumerate(ch):
                    first = i == 0 or ch[i - 1][0] != blk
                    end = i + 1 == len(ch) or ch[i + 1][0] != blk
                    last = nc.tensor.matmul(PS[4 + t % 2][lo:lo + HD, blk * P:(blk + 1) * P],
                                            VT[:, t, key, lo:lo + HD], PT1[:, n % 2, i * P:(i + 1) * P],
                                            start=first, stop=end)
                last.then_inc(pv_done, 1)

            for n in range(len(JOBS)):
                pe.wait_ge(e_made, n + 1)
                if n >= 2:
                    pe.wait_ge(pt_made, n - 1)
                for i, (blk, c, key) in enumerate(chunks(n)):
                    last = nc.tensor.transpose(PS[2 + n % 2][:, i * P:(i + 1) * P], E1[:, n % 2, c:c + P], ident)
                last.then_inc(pt_ps, 1)
                if n:
                    dilated_values(n - 1)
                if n + 2 < len(JOBS):
                    dilated_scores(n + 2)
            dilated_values(len(JOBS) - 1)
            for i in range(6):
                kind, g = i // 3, i % 3
                if i >= 2:
                    pe.wait_ge(row_made, i - 1)
                for b in range(4):
                    last = nc.tensor.matmul(PS[6 + i % 2][0:GROUP_HEADS, b * P:(b + 1) * P],
                                            MD[:, kind, b, 4 * g:4 * g + 4], ident, start=True, stop=True)
                last.then_inc(st_ps, 1)
            for t in range(6):
                if t == 0:
                    pe.wait_ge(rowf, 1)
                    pe.wait_ge(row_made, 6)
                if t >= 2:
                    pe.wait_ge(o_made, t - 1)
                nc.tensor.matmul(PS[6 + t % 2][:], sel[t % 2], ROW_w[:, t // 2, :], start=True,
                                 stop=True).then_inc(f_ps, 1)
            linear("wo", HID_hi, HID_lo, ready=(o_lo_made, 0))

            feed_forward(1, FFN1)
            L = layers["inp"]

            def post(j):
                kind = INP_KINDS[j]
                pe.wait_ge(rt_made, 2 * j + 2)
                if kind == "kv":
                    for i in range(4):
                        nc.tensor.matmul(AUX[i][:], (dup, dupswap)[i % 2], T4[i // 2][:], start=True,
                                         stop=True).then_inc(kv_ps, 1)
                    for i in range(2):
                        pe.wait_ge(kv_c, 2)
                        pe.wait_ge(kv_s, 2)
                        for b in range(4):
                            last = nc.tensor.transpose(AUX[i][:, b * P:(b + 1) * P], T4[i][:, b * P:(b + 1) * P], ident)
                        last.then_inc(tr_ps, 1)
                elif j in ROPE_UNITS:
                    r = ROPE_UNITS.index(j)
                    for i in range(2):
                        if j == ROPE_UNITS[0]:
                            pe.wait_ge(av_made, 2)
                        elif r:
                            pe.wait_ge(rope_s, 2 * r - 1 + i)
                        if j in (11,):
                            pe.wait_ge(rv_tok, 4)
                        nc.tensor.matmul(AUX[i][:], swap, T4[2 * (j % 2) + i][:], start=True, stop=True).then_inc(sw_ps, 1)
                elif kind == "rv":
                    for i in range(2):
                        n = 2 * (j - 7) + i
                        pe.wait_ge(rope_s, 12)
                        if n >= 2:
                            pe.wait_ge(rv_tok, n - 1)
                        for b in range(4):
                            last = nc.tensor.transpose(AUX[i][:, b * P:(b + 1) * P],
                                                       T4[2 * (j % 2) + i][:, b * P:(b + 1) * P], ident)
                        last.then_inc(rv_ps, 1)

            index_jobs = [(b, h) for b in (1, 2, 3) for h in range(8)]

            def index_scores():
                b, h = index_jobs.pop(0)
                n = 8 * (b - 1) + h
                if n == 0:
                    pe.wait_ge(rope_made, 4)
                    pe.wait_ge(kv_made, 2)
                if n >= 2:
                    pe.wait_ge(idx_rel, n - 1)
                lo, w = HD * (h % 2), P * (b + 1)
                nc.tensor.matmul(AUX[2 + n % 2][:, 0:w], IQ[lo:lo + HD, h // 2, b * P:(b + 1) * P],
                                 II[lo:lo + HD, 0:w], start=True, stop=True).then_inc(idx_ps, 1)

            for j in range(L.n):
                unit(L, At(j), H_hi, H_lo, (h_lo_made, H_BASE[FINAL]) if j == 0 else None,
                     index_scores if 4 <= j <= 6 else None)
                if j == 0:
                    rms_sum(FINAL)
                    pe.wait_ge(ssum2, 7)
                    nc.tensor.matmul(AUX[1][:], ones, SSUM2[:], start=True, stop=True).then_inc(stat2_ready, 1)
                else:
                    post(j - 1)
            post(L.n - 1)

            def ret_scores(n):
                h, mb = RET_JOBS[n]
                t, lo = h // 2, HD * (h % 2)
                if n == 0:
                    pe.wait_ge(rope_made, 12)
                    pe.wait_ge(acc_free, L.base + L.n)
                if n >= 2:
                    pe.wait_ge(rd_made, n - 1)
                nc.tensor.matmul(PS[n % 2][:, 0:SEQ - P * mb], RQK[lo:lo + HD, 4 + t, P * mb:P * (mb + 1)],
                                 RQK[lo:lo + HD, t, P * mb:SEQ], start=True, stop=True).then_inc(rs_ps, 1)

            def ret_norm(t):
                pe.wait_ge(r_sq, t + 1)
                if t:
                    pe.wait_ge(rstd, t)
                nc.tensor.matmul(AUX[2][:], headsum, L2[:, 0, :], start=True, stop=True).then_inc(rsum_ps, 1)

            ret_scores(0)
            ret_scores(1)
            for n, (h, mb) in enumerate(RET_JOBS):
                t, lo = h // 2, HD * (h % 2)
                pe.wait_ge(rd_made, n + 1)
                if n == 0:
                    pe.wait_ge(rv_tok, 4)
                    pe.wait_ge(rope_s, 16)
                if mb == 0 and h % 2 == 0 and t >= 2:
                    pe.wait_ge(ro1, t - 1)
                last = nc.tensor.matmul(AUX[t % 2][lo:lo + HD, P * mb:SEQ], RVT[:, mb, HD * h:HD * (h + 1)],
                                        T4[n % 2][:, 0:SEQ - P * mb], start=(mb == 0), stop=(mb == 3))
                last.then_inc(ro_ps, 1)
                if n + 2 < len(RET_JOBS):
                    ret_scores(n + 2)
                if n % 8 == 7 or n == len(RET_JOBS) - 1:
                    ret_norm(n // 8)

            def dsa_scores(n):
                t, b, half = DSA_JOBS[n]
                lo = HD * half
                if n == 0:
                    pe.wait_ge(rope_made, 16)
                if n >= 2:
                    pe.wait_ge(a_l, n - 1)
                nc.tensor.matmul(PS[n % 2][:, 0:P * (b + 1)], AQ[lo:lo + HD, t, b * P:(b + 1) * P],
                                 KK[lo:lo + HD, 0:P * (b + 1)], start=True, stop=True).then_inc(a_s, 1)

            def dsa_values(n):
                t, b, half = DSA_JOBS[n]
                lo = HD * half
                pe.wait_ge(a_pt, n + 1)
                if n == 0:
                    pe.wait_ge(ro1, 4)
                if n % 8 == 0 and t >= 2:
                    pe.wait_ge(m_lo_made, 4 + t - 1)
                for c in range(b + 1):
                    last = nc.tensor.matmul(AUX[t % 2][lo:lo + HD, b * P:(b + 1) * P], AV[:, c, :],
                                            PT2[:, n % 2, c * P:(c + 1) * P], start=(c == 0), stop=(c == b))
                last.then_inc(a_o, 1)

            dsa_scores(0)
            dsa_scores(1)
            for n, (t, b, half) in enumerate(DSA_JOBS):
                if n + 2 < len(DSA_JOBS):
                    dsa_scores(n + 2)
                pe.wait_ge(a_dg, n + 1)
                if n >= 2:
                    pe.wait_ge(a_pt, n - 1)
                for c in range(b + 1):
                    last = nc.tensor.transpose(PS[2 + n % 2][:, c * P:(c + 1) * P], E2[:, n % 2, c * P:(c + 1) * P], ident)
                last.then_inc(a_pt_ps, 1)
                if n:
                    dsa_values(n - 1)
            dsa_values(len(DSA_JOBS) - 1)
            linear("wout", ready=(m_lo_made, 0))
            rms_sum(MIX_POST)
            feed_forward(2, FFN_PRE)
            rms_sum(FFN_POST)

        def split_hi(act, L, j):
            u = j.plus(L.base + 2)
            if u.i is None and u.c >= units:
                return
            kt = L.kt if u.i is not None else kts[u.c]
            hi_of(act, u, kt)

        def hi_of(act, u, kt):
            b = u.parity
            n = kt * COLS
            act.wait_ge(raw_in[b], u.half(16, 16))
            if u.i is not None or u.c >= 2:
                act.wait_ge(acc_ready, u.v(2, -2))
            nc.scalar.activation(W_hi[b][:, 0:n], W_raw[b][:, 0:n], ACT.Copy).then_inc(w_hi, 1)

        @block.scalar
        def _(act):
            act.dma_start(cmat[:, 0:2, :], a["cmat"][:, 0:2, :]).then_inc(const_in, 16)
            act.dma_start(onehot[:], a["onehot"]).then_inc(tab_in, 16)
            act.dma_start(table[0:BUCKETS, :], a["rel_bias"]).then_inc(tab_in, 16)
            act.wait_ge(vec_in, 16)
            act.wait_ge(eps_set, 1)

            def h_hi(n, gain, m):
                if n:
                    act.wait_ge(x_ready, m.v(1, X_BASE[n] + 1))
                dst = H_hi[:, bass.ds(m.v(), 1), :].rearrange("p o n -> p (o n)")
                src = X[:, bass.ds(m.v(), 1), :].rearrange("p o n -> p (o n)")
                scale = vec(gain, m) if gain is not None else FG[:, bass.ds(m.v(), 1)]
                nc.scalar.activation(dst, src, ACT.Copy, scale=scale).then_inc(h_hi_made, 1)

            def square(n, m, src=None):
                if src is None:
                    src = X[:, bass.ds(m.v(), 1), :].rearrange("p o n -> p (o n)")
                first = m.i is None and m.c == 0
                i = m.v(1, 7 * n - 2) if m.i is not None or m.c >= 2 else 7 * n
                if i if isinstance(i, int) else True:
                    act.wait_ge(ss_made, i)
                if first and n:
                    act.wait_ge(stat_ready, n)
                if first and n == FFN0:
                    act.wait_ge(ln_sum_ready, 1)
                dst = SSUM[:] if first else SQ[:, m.parity, :]
                nc.scalar.activation(dst, src, ACT.Square).then_inc(sq_made, 1)
                if n == FINAL:
                    dst = SSUM2[:] if first else SQ2[:, m.parity, :]
                    if m.i is not None or m.c >= 3:
                        act.wait_ge(ssum2, m.v(1, -2))
                    nc.scalar.activation(dst, src, ACT.Square, scale=vec("final", m)).then_inc(ssum2_sq, 1)

            def std(n):
                act.wait_ge(stat_ready, n + 1)
                nc.scalar.activation(STD[:], AUX[0][:], ACT.Sqrt, bias=epst[:], scale=1.0 / D_MODEL).then_inc(std_made, 1)

            for m in range(DT):
                if m % 2 == 0:
                    act.wait_ge(x_in[m // 2], 16)
                h_hi(MIX0, "norm_mix0", At(m))
                square(MIX0, At(m))
                if m == 1:
                    hi_of(act, At(0), kts[0])
                if m == 5:
                    hi_of(act, At(1), kts[1])
            act.dma_start(cmat[:, 2:9, :], a["cmat"][:, 2:9, :]).then_inc(const2_in, 16)
            nc.scalar.activation(tap_hi[:], vecs[:, vec_at["w_dw"]:vec_at["w_dw"] + CONV_WIDTH * DT], ACT.Copy).then_inc(w_parts, 1)

            L = layers["pw1"]
            act.wait_ge(eps_set, 1)

            def take_conv(m):
                act.wait_ge(conv_pe, 2 * (m - CONV_DVE + 1))
                nc.scalar.activation(CV[:, m, :], AUX[1 + m - CONV_DVE][:], ACT.Identity, bias=vec("b_dw", m)).then_inc(conv_pe_taken, 1)

            def glu_step(j):
                split_hi(act, L, j)
                if j.i is None and j.c == 0:
                    std(0)
                act.wait_ge(gate_in, j.v(1, 1))
                nc.scalar.activation(T_act[:], T_g[:], ACT.Sigmoid, bias=vec("b_pw1", j.plus(DT))).then_inc(gate_act, 1)
            steps(act, L.n, glu_step, first=1, last=2)
            for p in range(DT - CONV_DVE):
                act.wait_ge(glu_made, CONV_DVE + p + 1)
                n = SEQ + CONV_WIDTH - 1
                nc.scalar.activation(UP_hi[:, p, 0:n], U[:, CONV_DVE + p, 0:n], ACT.Copy).then_inc(u_hi, 1)
            act.wait_ge(const2_in, 16)
            for h in range(12):
                act.wait_ge(fvec_ps, h + 1)
                nc.scalar.activation(fvec[:, h, :], AUX[1 + h % 2][:, 0:DIAG], ACT.Copy).then_inc(fvec_made, 1)
            act.wait_ge(fvec_made, 12)
            act.dma_start(bias_scratch.rearrange("h p d -> p h d"), fvec[:]).then_inc(scr_out, 16)
            act.wait_ge(w_parts, 2)
            for n, (m, t0, t1) in enumerate(CONV_CHUNKS):
                if n >= 2:
                    act.wait_ge(conv_pe, n - 1)
                for t in range(t0, t1):
                    k = TAP_CHUNK * (n % 2) + t - t0
                    w = tap_hi[:, t * DT + m:t * DT + m + 1].bitcast(F32)
                    last = nc.scalar.activation(H_hi[:, k // 4, P * (k % 4):P * (k % 4 + 1)], ident, ACT.Copy, scale=w)
                last.then_inc(diag_hi, 1)
                if t0 and m > CONV_DVE:
                    take_conv(m - 1)
            take_conv(DT - 1)
            act.wait_ge(ln_sum_ready, 1)
            nc.scalar.activation(STD[:], AUX[3][:], ACT.Copy, scale=1.0 / D_MODEL).then_inc(mu_made, 1)
            for m in range(DT):
                act.wait_ge(xc_made, m + 1)
                if m >= 2:
                    act.wait_ge(ln_var_ready, m - 1)
                nc.scalar.activation(SQ[:, m % 2, :], CV[:, m, :], ACT.Square).then_inc(xc_sq, 1)
            act.wait_ge(ln_var_ready, DT)
            nc.scalar.activation(STD[:], AUX[2][:], ACT.Sqrt, bias=epst[:], scale=1.0 / D_MODEL).then_inc(ln_std, 1)
            for m in range(DT):
                act.wait_ge(ln_scaled, m + 1)
                nc.scalar.activation(CV[:, m, :], CV[:, m, :], ACT.Silu, bias=vec("ln_b", m), scale=vec("ln_g", m)).then_inc(ln_act, 1)
                act.wait_ge(ln_act, m + 1)
                nc.scalar.activation(HID_hi[:, m, :], CV[:, m, :], ACT.Copy).then_inc(ln_hi_made, 1)

            def add_steps(name, norm=None, gain=None):
                L = layers[name]

                def step(j):
                    split_hi(act, L, j)
                    if norm is None:
                        return
                    for half in range(2):
                        m = At(2 * j.c + half, None if j.i is None else j.i * 2)
                        if norm in H_BASE or norm == FINAL:
                            h_hi(norm, gain, m)
                            square(norm, m)
                        else:
                            act.wait_ge(y_ready, m.v(1, Y_BASE[norm] + 1))
                            square(norm, m, Y[:, bass.ds(m.v(), 1), :].rearrange("p o n -> p (o n)"))
                steps(act, L.n, step, first=1 if norm is not None else 0, last=2)

            def gate_steps(name, norm=None):
                L, q0 = layers[name], gu_base[name]

                def step(j):
                    split_hi(act, L, j)
                    if j.i is None and j.c == 0 and norm is not None:
                        std(norm)
                    act.wait_ge(gate_in, j.v(1, 8 + q0 + 1))
                    nc.scalar.activation(T_act[:], T_g[:], ACT.Silu).then_inc(gate_act, 1)
                    hid_hi(j, q0)
                steps(act, L.n, step, first=1, last=2)

            def hid_hi(j, q0):
                act.wait_ge(hid_made, j.v(1, q0 + 1))
                dst = HID_hi[:, bass.ds(j.v(), 1), :].rearrange("p o n -> p (o n)")
                nc.scalar.activation(dst, T_hid[:], ACT.Copy).then_inc(hid_hi_made, 1)

            add_steps("pw2", FFN0, "norm_ffn0")
            gate_steps("gu0a", norm=FFN0)
            add_steps("dn0a")
            gate_steps("gu0b")
            add_steps("dn0b", MIX1, "norm_mix1")

            L = layers["qkv"]
            for j in range(L.n):
                split_hi(act, L, At(j))
                if j == 0:
                    std(MIX1)
                    act.wait_ge(scr_out, 16)
                    t = bias_scratch.tensor
                    def diagonals(h, rows, n):
                        return bass.AP(t, h * P * DIAG + rows - 1, [[DIAG - 1, rows], [P * DIAG, GROUP_HEADS], [1, n]])
                    act.dma_start(B0[:], diagonals(0, P, 2 * P)).then_inc(bias_in, 16)
                    act.dma_start(B1[:], diagonals(4, P, P)).then_inc(bias_in, 16)
                    act.wait_ge(b2_set, 1)
                    for r in range(4):
                        act.dma_start(B2[32 * r:32 * r + 32, :, 32 * r:32 * r + 32], diagonals(8, 32, 32)).then_inc(bias_in, 16)
            for t in range(6):
                act.wait_ge(v_t, t + 1)
                nc.scalar.activation(VT[:, t, :, :].rearrange("p b n -> p (b n)"), AUX[t % 4][:], ACT.Copy).then_inc(v_tok, 1)
            def dilated_exp(n):
                h, blks = JOBS[n]
                act.wait_ge(nm_made, n + 1)
                if n >= 2:
                    act.wait_ge(pt_ps, n - 1)
                for i, (blk, c, w, keys) in enumerate(blks):
                    last = nc.scalar.activation(E1[:, n % 2, c:c + w], L1[:, n % 2, c:c + w], ACT.Exp,
                                                bias=NM[:, n % 2, i:i + 1], accum_out=MD[:, 1, blk, h:h + 1])
                last.then_inc(e_made, 1)

            dilated_exp(0)
            for n, (h, blks) in enumerate(JOBS):
                if n + 1 < len(JOBS):
                    dilated_exp(n + 1)
                act.wait_ge(pt_ps, n + 1)
                if n >= 2:
                    act.wait_ge(pv_done, n - 1)
                w = P * sum(len(keys) for _, _, _, keys in blks)
                nc.scalar.activation(PT1[:, n % 2, 0:w], PS[2 + n % 2][:, 0:w], ACT.Copy).then_inc(pt_made, 1)
            for i in range(6):
                kind, g = i // 3, i % 3
                act.wait_ge(st_ps, i + 1)
                dst = (ROW_w, ROW_den)[kind]
                nc.scalar.activation(unpermuted(dst[:, g, :], g), blocked(PS[6 + i % 2][0:GROUP_HEADS, :], g),
                                     ACT.Copy).then_inc(row_made, 1)
            act.wait_ge(rowd, 1)
            nc.scalar.activation(ROW_w[:], ROW_w[:], ACT.Exp).then_inc(roww, 1)
            for t in range(6):
                act.wait_ge(o_made, t + 1)
                nc.scalar.activation(HID_hi[:, t, :], T4[t % 2][:], ACT.Copy).then_inc(o_hi_made, 1)

            add_steps("wo", FFN1, "norm_ffn1")
            gate_steps("gu1a", norm=FFN1)
            add_steps("dn1a")
            gate_steps("gu1b")
            act.wait_ge(fg_made, 1)
            add_steps("dn1b", FINAL)

            L = layers["inp"]

            def index_relu(b):
                w = P * (b + 1)
                for h in range(8):
                    n = 8 * (b - 1) + h
                    act.wait_ge(idx_ps, n + 1)
                    if n >= 2:
                        act.wait_ge(isc_made, n - 1)
                    nc.scalar.activation(SQ[:, n % 2, 0:w], AUX[2 + n % 2][:, 0:w], ACT.Relu).then_inc(idx_rel, 1)

            def post(j):
                kind = INP_KINDS[j]
                if kind == "rv":
                    for i in range(2):
                        n = 2 * (j - 7) + i
                        act.wait_ge(rv_ps, n + 1)
                        dst = RVT[:, :, n * P:(n + 1) * P]
                        nc.scalar.activation(dst, AUX[i][:].rearrange("p (b n) -> p b n", b=4), ACT.Copy).then_inc(rv_tok, 1)
                elif kind == "rg":
                    for i in range(2):
                        act.wait_ge(rt_made, 2 * j + 1 + i)
                        nc.scalar.activation(GS[:, 2 * (j - 9) + i, :], T4[2 * (j % 2) + i][:], ACT.Silu).then_inc(rg_made, 1)

            for j in range(L.n):
                if 4 <= j <= 6:
                    index_relu(j - 3)
                split_hi(act, L, At(j))
                if j == 0:
                    std(FINAL)
                    act.wait_ge(rf_scaled, 1)
                    nc.scalar.activation(STD[:], T_u[:], ACT.Sqrt, bias=epst[:], scale=1.0 / D_MODEL).then_inc(std2_made, 1)
                    act.dma_start(CS[:], a["rotary"]).then_inc(cs_in, 16)
                else:
                    post(j - 1)
            act.wait_ge(isc_made, 24)
            for h in range(2):
                act.dma_start(SQ[:, h, :], a["decay"][h]).then_inc(d_in, 16)

            def ret_norm_sq(t):
                act.wait_ge(ro_ps, 8 * t + 8)
                if t:
                    act.wait_ge(rsum_ps, t)
                else:
                    act.wait_ge(rope_made, 16)
                nc.scalar.activation(L2[:, 0, :], AUX[t % 2][:], ACT.Square).then_inc(r_sq, 1)
                act.wait_ge(rsum_ps, t + 1)
                if t:
                    act.wait_ge(rrec, 4 * t)
                nc.scalar.activation(STD[:], AUX[2][:], ACT.Sqrt, bias=epst[:], scale=1.0 / HD).then_inc(rstd, 1)
                act.wait_ge(ro2, t + 1)
                nc.scalar.activation(H_hi[:, t, :], E2[:, 0, :], ACT.Copy).then_inc(m_hi_made, 1)

            for h in range(2, RET_HEADS):
                act.wait_ge(rd_made, 4 * (h - 1))
                act.wait_ge(d_in, 16 * h)
                act.dma_start(SQ[:, h % 2, :], a["decay"][h]).then_inc(d_in, 16)
                if h % 2 == 1:
                    ret_norm_sq(h // 2 - 1)
            ret_norm_sq(3)
            def dsa_exp(n):
                w = P * (DSA_JOBS[n][1] + 1)
                act.wait_ge(a_nm, n + 1)
                if n >= 2:
                    act.wait_ge(a_pt_ps, n - 1)
                if n == 0:
                    act.wait_ge(m_lo_made, 4)
                nc.scalar.activation(E2[:, n % 2, 0:w], L2[:, n % 2, 0:w], ACT.Exp, scale=HD ** -0.5,
                                     bias=DEN[:, n % 2, 0:1], accum_out=DEN[:, n % 2, 1:2]).then_inc(a_e, 1)

            def hi_of_pair(t):
                act.wait_ge(a_o, 8 * t + 8)
                nc.scalar.activation(H_hi[:, 4 + t, :], AUX[t % 2][:], ACT.Copy).then_inc(m_hi_made, 1)

            dsa_exp(0)
            for n, (t, b, half) in enumerate(DSA_JOBS):
                w = P * (b + 1)
                if n + 1 < len(DSA_JOBS):
                    dsa_exp(n + 1)
                act.wait_ge(a_pt_ps, n + 1)
                if n >= 2:
                    act.wait_ge(a_o, n - 1)
                nc.scalar.activation(PT2[:, n % 2, 0:w], PS[2 + n % 2][:, 0:w], ACT.Copy).then_inc(a_pt, 1)
                if n % 8 == 1 and n > 8:
                    hi_of_pair(t - 1)
            hi_of_pair(3)

            add_steps("wout", MIX_POST)
            std(MIX_POST)
            for m in range(DT):
                h_hi(FFN_PRE, "ffn_pre", At(m))
                square(FFN_PRE, At(m))

            def conv_gate_steps(name, j0, norm=None):
                L, q0 = layers[name], gu_base[name]

                def step(j):
                    split_hi(act, L, j)
                    if j.i is None and j.c == 0 and norm is not None:
                        std(norm)
                    q = q0 - 44
                    for i, y in enumerate((T_g, T_u)):
                        act.wait_ge(g3_in, j.v(2, 2 * q + 1 + i))
                        nc.scalar.activation(y[:], GP[:, i, 2:SEQ + 2], ACT.Identity, scale=vec("conv3_w", j.plus(88 + 22 * i + j0)),
                                             bias=vec("conv3_b", j.plus(22 * i + j0))).then_inc(c3_y, 1)
                    act.wait_ge(gate_in, j.v(1, 8 + q0 + 1))
                    nc.scalar.activation(T_act[:], T_g[:], ACT.Silu).then_inc(gate_act, 1)
                    hid_hi(j, q0)
                steps(act, L.n, step, first=1, last=2)

            conv_gate_steps("gu2a", 0, norm=FFN_PRE)
            add_steps("dn2a")
            conv_gate_steps("gu2b", 11)
            add_steps("dn2b", FFN_POST)
            std(FFN_POST)

        @block.gpsimd
        def _(pool):
            nc.gpsimd.memset(epst[:], EPS).then_inc(eps_set, 1)
            nc.gpsimd.memset(U[:, :, 0:CONV_WIDTH - 1], 0.0).then_inc(pads_set, 1)
            pool.wait_ge(pads_set, 1)
            nc.gpsimd.memset(table[BUCKETS:BUCKETS + 1, :], NEG).then_inc(tab_pad, 1)

            def lo_of(u, kt):
                b = u.parity
                n = kt * COLS
                pool.wait_ge(w_hi, u.v(1, 1))
                nc.gpsimd.tensor_tensor(W_lo[b][:, 0:n], W_raw[b][:, 0:n], W_hi[b][:, 0:n].bitcast(F32),
                                        ALU.subtract).then_inc(w_lo, 1)

            def split_lo(L, j):
                u = j.plus(L.base + 2)
                if u.i is None and u.c >= units:
                    return
                lo_of(u, L.kt if u.i is not None else kts[u.c])

            def add_square(n, m):
                if m.i is None and m.c == 0:
                    return
                pool.wait_ge(sq_made, m.v(1, 8 * n + 1))
                if m.i is not None or m.c >= 2:
                    pool.wait_ge(ss_made, m.v(1, 7 * n - 1))
                nc.gpsimd.tensor_tensor(SSUM[:], SSUM[:], SQ[:, m.parity, :], ALU.add).then_inc(ss_made, 1)
                if n == FINAL:
                    pool.wait_ge(ssum2_sq, m.v(1, 1))
                    if m.i is not None or m.c >= 2:
                        pool.wait_ge(ssum2, m.v(1, -1))
                    nc.gpsimd.tensor_tensor(SSUM2[:], SSUM2[:], SQ2[:, m.parity, :], ALU.add).then_inc(ssum2, 1)

            pool.wait_ge(tab_pad, 1)
            add_square(MIX0, At(1))
            lo_of(At(0), kts[0])
            for m in range(2, DT):
                add_square(MIX0, At(m))
            lo_of(At(1), kts[1])
            L = layers["pw1"]
            steps(pool, L.n, lambda j: split_lo(L, j), last=2)
            for n, (m, t0, t1) in enumerate(CONV_CHUNKS):
                pool.wait_ge(acc_ready, 2 * (L.base + L.n))
                pool.wait_ge(const2_in, 16)
                pool.wait_ge(w_parts, 2)
                if n >= 2:
                    pool.wait_ge(conv_pe, n - 1)
                k = TAP_CHUNK * (n % 2) // 4
                dst = H_lo[:, k:k + TAP_CHUNK // 4, :].rearrange("p a (b n) -> p (a b) n", n=P)[:, 0:t1 - t0]
                w = tap_lo[:].rearrange("p (t m) -> p t m", m=DT)[:, t0:t1, m:m + 1].bitcast(F32)
                nc.gpsimd.tensor_tensor(dst, ident.unsqueeze(1).to_broadcast([P, t1 - t0, P]),
                                        w.to_broadcast([P, t1 - t0, P]), ALU.mult).then_inc(diag_lo, 1)
            pool.wait_ge(stat_ready, 1)
            for m in range(CONV_DVE):
                pool.wait_ge(conv_made, m + 1)
                if m == 0:
                    nc.gpsimd.tensor_copy(SSUM[:], CV[:, 0, :]).then_inc(ln_sum, 1)
                else:
                    pool.wait_ge(ln_sum, m)
                    nc.gpsimd.tensor_tensor(SSUM[:], SSUM[:], CV[:, m, :], ALU.add).then_inc(ln_sum, 1)

            def add_steps(name, norm=None):
                L = layers[name]

                def step(j):
                    split_lo(L, j)
                    if norm is not None:
                        add_square(norm, At(2 * j.c, None if j.i is None else j.i * 2))
                        add_square(norm, At(2 * j.c + 1, None if j.i is None else j.i * 2))
                steps(pool, L.n, step, first=1 if norm is not None else 0, last=2)

            def gate_steps(name):
                L = layers[name]
                steps(pool, L.n, lambda j: split_lo(L, j), last=2)

            add_steps("pw2", FFN0)
            gate_steps("gu0a")
            add_steps("dn0a")
            gate_steps("gu0b")
            add_steps("dn0b", MIX1)
            L = layers["qkv"]
            for j in range(L.n):
                split_lo(L, At(j))
                if j == 0:
                    nc.gpsimd.memset(B2[:], NEG).then_inc(b2_set, 1)
            add_steps("wo", FFN1)
            gate_steps("gu1a")
            add_steps("dn1a")
            gate_steps("gu1b")
            add_steps("dn1b", FINAL)

            L = layers["inp"]

            def rope(j):
                r = ROPE_UNITS.index(j)
                dst = {"iq": IQ, "rq": RQK, "rk": RQK, "aq": AQ}[INP_KINDS[j]]
                m0 = {1: 0, 2: 2, 3: 0, 4: 2, 5: 4, 6: 6, 11: 0, 12: 2}[j]
                if j == 1:
                    pool.wait_ge(cs_in, 16)
                for i in range(2):
                    pool.wait_ge(rt_made, 2 * j + 1 + i)
                    nc.gpsimd.tensor_tensor(dst[:, m0 + i, :], T4[2 * (j % 2) + i][:], CS[:, 0, :],
                                            ALU.mult).then_inc(rope_c, 1)
                for i in range(2):
                    pool.wait_ge(rope_s, 2 * r + 1 + i)
                    pool.wait_ge(rope_c, 2 * r + 1 + i)
                    nc.gpsimd.tensor_tensor(dst[:, m0 + i, :], dst[:, m0 + i, :], T4[2 * (j % 2) + i][:],
                                            ALU.add).then_inc(rope_made, 1)

            for j in range(L.n):
                split_lo(L, At(j))
                if j - 1 in ROPE_UNITS:
                    rope(j - 1)
            rope(L.n - 1)
            for t in range(4):
                pool.wait_ge(ro1, t + 1)
                nc.gpsimd.tensor_tensor(E2[:, 0, :], E2[:, 0, :], GS[:, t, :], ALU.mult).then_inc(ro2, 1)
                pool.wait_ge(m_hi_made, t + 1)
                nc.gpsimd.tensor_tensor(H_lo[:, t, :], E2[:, 0, :], H_hi[:, t, :].bitcast(F32),
                                        ALU.subtract).then_inc(m_lo_made, 1)
            for n, (t, b, half) in enumerate(DSA_JOBS):
                pool.wait_ge(a_rd, n + 1)
                e = E2[:, n % 2, 0:P * (b + 1)]
                nc.gpsimd.tensor_scalar(e, e, DEN[:, n % 2, 2:3], None, ALU.mult).then_inc(a_dg, 1)
            add_steps("wout", MIX_POST)
            for m in range(DT):
                pool.wait_ge(f_applied, m + 1)
                nc.gpsimd.tensor_tensor(X[:, m, :], X[:, m, :], T4[m % 2][:], ALU.add).then_inc(x_ready, 1)
                if m:
                    add_square(FFN_PRE, At(m - 1))
            add_square(FFN_PRE, At(DT - 1))
            nc.gpsimd.memset(GP[:, :, 0:2], 0.0).then_inc(pad3_set, 1)
            gate_steps("gu2a")
            add_steps("dn2a")
            gate_steps("gu2b")
            add_steps("dn2b", FFN_POST)

        @block.vector
        def _(dve):
            dve.wait_ge(vec_in, 16)
            def h_lo(n, gain, m):
                dve.wait_ge(h_hi_made, m.v(1, H_BASE[n] + 1))
                dst = H_lo[:, bass.ds(m.v(), 1), :].rearrange("p o n -> p (o n)")
                hi = H_hi[:, bass.ds(m.v(), 1), :].rearrange("p o n -> p (o n)").bitcast(F32)
                src = X[:, bass.ds(m.v(), 1), :].rearrange("p o n -> p (o n)")
                scale = vec(gain, m) if gain is not None else FG[:, bass.ds(m.v(), 1)]
                nc.vector.scalar_tensor_tensor(out=dst, in0=src, scalar=scale, in1=hi, op0=ALU.mult,
                                               op1=ALU.subtract).then_inc(h_lo_made, 1)

            def rms(n):
                dve.wait_ge(std_made, n + 1)
                nc.vector.reciprocal(R[:], STD[:]).then_inc(r_made, 1)
                dve.wait_ge(r_made, n + 1)

            for m in range(DT):
                h_lo(0, "norm_mix0", At(m))

            L = layers["pw1"]
            HALO = CONV_WIDTH - 1

            todo = [(m, t) for m in range(CONV_DVE) for t in range(CONV_WIDTH)]

            def conv(count, upto):
                while count and todo and todo[0][0] < upto:
                    m, t = todo.pop(0)
                    n = CONV_WIDTH * m + t
                    dst = (CV[:, m, :], CVacc[:])[t % 2]
                    w = vec("w_dw", t * DT + m)
                    src = U[:, m, t:t + SEQ]
                    if n >= 2 and t != 0:
                        dve.wait_ge(conv_step, n - 1)
                    if t == 0:
                        i = nc.vector.tensor_scalar(dst, src, w, vec("b_dw", m), ALU.mult, ALU.add)
                    elif t == 1:
                        i = nc.vector.tensor_scalar(dst, src, w, None, ALU.mult)
                    else:
                        i = nc.vector.scalar_tensor_tensor(out=dst, in0=src, scalar=w, in1=dst, op0=ALU.mult, op1=ALU.add)
                    i.then_inc(conv_step, 1)
                    count -= 1
                    if t == CONV_WIDTH - 1:
                        dve.wait_ge(conv_step, n + 1)
                        nc.vector.tensor_tensor(CV[:, m, :], CV[:, m, :], CVacc[:], ALU.add).then_inc(conv_made, 1)
                        dve.wait_ge(conv_made, m + 1)

            dve.wait_ge(tab_in, 32)
            dve.wait_ge(tab_pad, 1)
            nc.vector.tensor_copy(table_wide[:], table[:].unsqueeze(2).to_broadcast([BUCKETS + 1, 12, P])).then_inc(tab_wide, 1)

            dve.wait_ge(w_parts, 1)
            nc.vector.tensor_tensor(tap_lo[:], vecs[:, vec_at["w_dw"]:vec_at["w_dw"] + CONV_WIDTH * DT],
                                    tap_hi[:].bitcast(F32), ALU.subtract).then_inc(w_parts, 1)
            nc.vector.tensor_tensor(FG[:], vecs[:, vec_at["final"]:vec_at["final"] + DT],
                                    vecs[:, vec_at["mix_pre"]:vec_at["mix_pre"] + DT], ALU.mult).then_inc(fg_made, 1)
            dve.wait_ge(pads_set, 1)
            for j in range(L.n):
                u = At(L.base + j)
                if j == 0:
                    rms(0)
                dve.wait_ge(acc_ready, u.v(2, 2))
                b = u.parity
                if j:
                    dve.wait_ge(gate_act, j)
                nc.vector.tensor_tensor(T_g[:], PS[2 * b + 1][:], R[:], ALU.mult).then_inc(gate_in, 1)
                if j:
                    dve.wait_ge(glu_made, j)
                nc.vector.tensor_tensor(T_u[:], PS[2 * b][:], R[:], ALU.mult).then_inc(acc_free, 1)
                dve.wait_ge(gate_act, j + 1)
                dve.wait_ge(acc_free, j + 1)
                nc.vector.scalar_tensor_tensor(out=U[:, j, HALO:HALO + SEQ], in0=T_u[:], scalar=vec("b_pw1", j),
                                               in1=T_act[:], op0=ALU.add, op1=ALU.mult).then_inc(glu_made, 1)
                if j < L.n - 1:
                    conv(TAPS_PER_UNIT, j)
            dve.wait_ge(glu_made, L.n)
            conv(6, CONV_DVE)
            for p in range(DT - CONV_DVE):
                dve.wait_ge(u_hi, p + 1)
                n = SEQ + CONV_WIDTH - 1
                nc.vector.tensor_tensor(UP_lo[:, p, 0:n], U[:, CONV_DVE + p, 0:n], UP_hi[:, p, 0:n].bitcast(F32),
                                        ALU.subtract).then_inc(u_lo, 1)
            conv(len(todo), DT)
            dve.wait_ge(mu_made, 1)
            for m in range(DT):
                nc.vector.tensor_tensor(CV[:, m, :], CV[:, m, :], STD[:], ALU.subtract).then_inc(xc_made, 1)
            dve.wait_ge(ln_std, 1)
            nc.vector.reciprocal(T_g[:], STD[:]).then_inc(ln_r, 1)
            dve.wait_ge(ln_r, 1)
            for m in range(DT):
                nc.vector.tensor_tensor(CV[:, m, :], CV[:, m, :], T_g[:], ALU.mult).then_inc(ln_scaled, 1)
            dve.wait_ge(scr_out, 16)
            for m in range(DT):
                dve.wait_ge(ln_hi_made, m + 1)
                nc.vector.tensor_tensor(HID_lo[:, m, :], CV[:, m, :], HID_hi[:, m, :].bitcast(F32),
                                        ALU.subtract).then_inc(ln_lo_made, 1)

            def add_steps(name, x0, norm=None, gain=None, bias=None):
                L = layers[name]

                def step(j):
                    u = j.plus(L.base)
                    b = u.parity
                    for half in range(2):
                        m = At(2 * j.c + half, None if j.i is None else j.i * 2)
                        dve.wait_ge(acc_ready, u.v(2, half + 1))
                        x = X[:, bass.ds(m.v(), 1), :].rearrange("p o n -> p (o n)")
                        if bias is None:
                            i = nc.vector.tensor_tensor(x, x, PS[2 * b + half][:], ALU.add)
                        else:
                            i = nc.vector.scalar_tensor_tensor(out=x, in0=PS[2 * b + half][:], scalar=vec(bias, m),
                                                               in1=x, op0=ALU.add, op1=ALU.add)
                        i.then_inc(x_ready, 1) if x0 is not None else i.then_inc(x_half, 1)
                    if x0 is not None:
                        dve.wait_ge(x_ready, j.v(2, x0 + 2))
                    else:
                        dve.wait_ge(x_half, j.v(2, (0 if name == "dn0a" else 8) + 2))
                    nc.vector.sem_inc(acc_free, 1)
                    if norm is not None:
                        for half in range(2):
                            h_lo(norm, gain, At(2 * j.c + half, None if j.i is None else j.i * 2))
                steps(dve, L.n, step)

            def gate_steps(name, norm=None):
                L, q0 = layers[name], gu_base[name]

                def step(j):
                    u = j.plus(L.base)
                    b = u.parity
                    if j.i is None and j.c == 0 and norm is not None:
                        rms(norm)
                    dve.wait_ge(acc_ready, u.v(2, 1))
                    nc.vector.tensor_tensor(T_g[:], PS[2 * b][:], R[:], ALU.mult).then_inc(gate_in, 1)
                    dve.wait_ge(acc_ready, u.v(2, 2))
                    nc.vector.tensor_tensor(T_u[:], PS[2 * b + 1][:], R[:], ALU.mult).then_inc(acc_free, 1)
                    dve.wait_ge(acc_free, u.v(1, 1))
                    hidden(j, q0)
                steps(dve, L.n, step, first=1)

            def hidden(j, q0):
                dve.wait_ge(gate_act, j.v(1, 8 + q0 + 1))
                nc.vector.tensor_tensor(T_hid[:], T_u[:], T_act[:], ALU.mult).then_inc(hid_made, 1)
                dve.wait_ge(hid_hi_made, j.v(1, q0 + 1))
                k = bass.ds(j.v(), 1)
                hi = HID_hi[:, k, :].rearrange("p o n -> p (o n)").bitcast(F32)
                nc.vector.tensor_tensor(HID_lo[:, k, :].rearrange("p o n -> p (o n)"), T_hid[:], hi,
                                        ALU.subtract).then_inc(hid_lo_made, 1)
                dve.wait_ge(hid_lo_made, j.v(1, q0 + 1))

            add_steps("pw2", 0, FFN0, "norm_ffn0", bias="b_pw2")
            gate_steps("gu0a", norm=FFN0)
            add_steps("dn0a", None)
            gate_steps("gu0b")
            add_steps("dn0b", 8, MIX1, "norm_mix1")

            def take_pair(t):
                dve.wait_ge(pv_done, 1 + max(n for n, (h, _) in enumerate(JOBS) if h == 2 * t + 1))
                g = t // 2
                nc.vector.tensor_copy(unpermuted(OU[:, t, :], g), blocked(PS[4 + t % 2][:], g)).then_inc(ou_made, 1)

            L = layers["qkv"]
            rms(MIX1)
            for j in range(L.n):
                u = At(L.base + j)
                for half in range(2):
                    dve.wait_ge(acc_ready, u.v(2, 1 + half))
                    m = 2 * j + half
                    g = m % 6 // 2
                    nc.vector.tensor_tensor(permuted(VQK[:, m, :], g), by_step(PS[2 * u.parity + half][:], g),
                                            by_step(R[:], g), ALU.mult).then_inc(qkv_made, 1)
                dve.wait_ge(qkv_made, 2 * j + 2)
                nc.vector.sem_inc(acc_free, 1)
            dve.wait_ge(bias_in, 96)
            for n, (h, blks) in enumerate(JOBS):
                g, hh = h // GROUP_HEADS, h % GROUP_HEADS
                dve.wait_ge(s_made, n + 1)
                if n >= 2:
                    dve.wait_ge(e_made, n - 1)
                for blk, c, w, keys in blks:
                    bias = (B0[:, hh, 256 - w:256], B1[:, hh, :], B2[:, hh, :])[g]
                    last = nc.vector.scalar_tensor_tensor(out=L1[:, n % 2, c:c + w], in0=PS[n % 2][:, c:c + w],
                                                          scalar=HD ** -0.5, in1=bias, op0=ALU.mult, op1=ALU.add)
                last.then_inc(l_made, 1)
                dve.wait_ge(l_made, n + 1)
                for blk, c, w, keys in blks:
                    last = nc.vector.reduce_max(MD[:, 0, blk, h:h + 1], L1[:, n % 2, c:c + w], AX.X)
                last.then_inc(m_made, 1)
                dve.wait_ge(m_made, n + 1)
                b0, nb = blks[0][0], len(blks)
                nc.vector.tensor_scalar(NM[:, n % 2, 0:nb], MD[:, 0, b0:b0 + nb, h:h + 1].rearrange("p b o -> p (b o)"),
                                        -1.0, None, ALU.mult).then_inc(nm_made, 1)
                if h % 2 == 1 and blks[-1][0] == 3:
                    pass
                if n >= 1:
                    hp, bp = JOBS[n - 1]
                    if hp % 2 == 1 and bp[-1][0] == 3:
                        take_pair(hp // 2)
            take_pair(5)
            dve.wait_ge(row_made, 3)
            nc.vector.tensor_tensor(ROW_max[:], ROW_w[:, 0, :], ROW_w[:, 1, :], ALU.max).then_inc(rowmax, 1)
            dve.wait_ge(rowmax, 1)
            nc.vector.tensor_tensor(ROW_max[:], ROW_max[:], ROW_w[:, 2, :], ALU.max).then_inc(rowmax, 1)
            dve.wait_ge(rowmax, 2)
            for g in range(3):
                last = nc.vector.tensor_tensor(ROW_w[:, g, :], ROW_w[:, g, :], ROW_max[:], ALU.subtract)
            last.then_inc(rowd, 1)
            dve.wait_ge(roww, 1)
            dve.wait_ge(row_made, 6)
            nc.vector.tensor_tensor(ROW_den[:], ROW_den[:], ROW_w[:], ALU.mult).then_inc(rowwd, 1)
            dve.wait_ge(rowwd, 1)
            nc.vector.tensor_tensor(ROW_sum[:], ROW_den[:, 0, :], ROW_den[:, 1, :], ALU.add).then_inc(rows_, 1)
            dve.wait_ge(rows_, 1)
            nc.vector.tensor_tensor(ROW_sum[:], ROW_sum[:], ROW_den[:, 2, :], ALU.add).then_inc(rows_, 1)
            dve.wait_ge(rows_, 2)
            nc.vector.reciprocal(ROW_max[:], ROW_sum[:]).then_inc(rows_, 1)
            dve.wait_ge(rows_, 3)
            for g in range(3):
                last = nc.vector.tensor_tensor(ROW_w[:, g, :], ROW_w[:, g, :], ROW_max[:], ALU.mult)
            last.then_inc(rowf, 1)
            for t in range(6):
                dve.wait_ge(f_ps, t + 1)
                nc.vector.tensor_tensor(T4[t % 2][:], OU[:, t, :], PS[6 + t % 2][:], ALU.mult).then_inc(o_made, 1)
                dve.wait_ge(o_hi_made, t + 1)
                nc.vector.tensor_tensor(HID_lo[:, t, :], T4[t % 2][:], HID_hi[:, t, :].bitcast(F32),
                                        ALU.subtract).then_inc(o_lo_made, 1)
                dve.wait_ge(o_lo_made, t + 1)

            add_steps("wo", 16, FFN1, "norm_ffn1")
            gate_steps("gu1a", norm=FFN1)
            add_steps("dn1a", None)
            gate_steps("gu1b")
            dve.wait_ge(fg_made, 1)
            add_steps("dn1b", 24, FINAL)

            L = layers["inp"]

            def post(j):
                if INP_KINDS[j] == "kv":
                    dve.wait_ge(cs_in, 16)
                    for i, dst in enumerate((KK, II)):
                        dve.wait_ge(kv_ps, 2 * i + 1)
                        nc.vector.tensor_tensor(dst[:], AUX[2 * i][:], CS[:, 0, :], ALU.mult).then_inc(kv_c, 1)
                        dve.wait_ge(kv_ps, 2 * i + 2)
                        nc.vector.tensor_tensor(L2k[i], AUX[2 * i + 1][:], CS[:, 1, :], ALU.mult).then_inc(kv_s, 1)
                        dve.wait_ge(kv_s, i + 1)
                        dve.wait_ge(kv_c, i + 1)
                        nc.vector.tensor_tensor(dst[:], dst[:], L2k[i], ALU.add).then_inc(kv_made, 1)
                    dve.wait_ge(tr_ps, 1)
                    nc.vector.tensor_copy(AV[:], AUX[0][:].rearrange("p (b n) -> p b n", b=4)[:, :, HD:2 * HD]).then_inc(av_made, 1)
                    dve.wait_ge(tr_ps, 2)
                    nc.vector.tensor_scalar(IW[:], AUX[1][:].rearrange("p (b n) -> p b n", b=4)[:, :, HD:HD + 8],
                                            8.0 ** -0.5 * HD ** -0.5, None, ALU.mult).then_inc(av_made, 1)
                elif j in ROPE_UNITS:
                    r = ROPE_UNITS.index(j)
                    for i in range(2):
                        dve.wait_ge(sw_ps, 2 * r + 1 + i)
                        dve.wait_ge(rope_c, 2 * r + 1 + i)
                        nc.vector.tensor_tensor(T4[2 * (j % 2) + i][:], AUX[i][:], CS[:, 1, :], ALU.mult).then_inc(rope_s, 1)

            def index_sum(b):
                w = P * (b + 1)
                if b == 1:
                    dve.wait_ge(av_made, 2)
                for h in range(8):
                    n = 8 * (b - 1) + h
                    dve.wait_ge(idx_rel, n + 1)
                    dst = ISC[:, b - 1, 0:w]
                    if h == 0:
                        i = nc.vector.tensor_scalar(dst, SQ[:, n % 2, 0:w], IW[:, b, h:h + 1], None, ALU.mult)
                    else:
                        dve.wait_ge(isc_made, n)
                        i = nc.vector.scalar_tensor_tensor(out=dst, in0=SQ[:, n % 2, 0:w], scalar=IW[:, b, h:h + 1],
                                                           in1=dst, op0=ALU.mult, op1=ALU.add)
                    i.then_inc(isc_made, 1)
                dve.wait_ge(isc_made, 8 * b)
                dst = ISC[:, b - 1, b * P:(b + 1) * P]
                nc.vector.scalar_tensor_tensor(out=dst, in0=later, scalar=-3.0e38, in1=dst, op0=ALU.mult,
                                               op1=ALU.add).then_inc(isc_mask, 1)

            rounds = [(b, i) for b in (1, 2, 3) for i in range(TOPK // 8)]

            def choose(count):
                for _ in range(count):
                    b, i = rounds.pop(0)
                    n = (b - 1) * (TOPK // 8) + i
                    w = P * (b + 1)
                    src = ISC[:, b - 1, 0:w] if i == 0 else WK[:, 0:w]
                    if i == 0:
                        dve.wait_ge(isc_mask, b)
                        if b > 1:
                            dve.wait_ge(left_out, b - 1)
                    if n:
                        dve.wait_ge(top_rep, n)
                    nc.vector.max(TOP8[:], src).then_inc(top_max, 1)
                    dve.wait_ge(top_max, n + 1)
                    nc.vector.match_replace(WK[:, 0:w], TOP8[:], src, -3.4e38).then_inc(top_rep, 1)
                    if i == TOPK // 8 - 1:
                        dve.wait_ge(top_rep, n + 1)
                        nc.vector.tensor_tensor(ISC[:, b - 1, 0:w], ISC[:, b - 1, 0:w], WK[:, 0:w],
                                                ALU.is_equal).then_inc(left_out, 1)

            for j in range(L.n):
                u = At(L.base + j)
                if j == 0:
                    dve.wait_ge(std_made, FINAL + 1)
                    nc.vector.reciprocal(RF[:], STD[:]).then_inc(r_made, 1)
                    dve.wait_ge(r_made, FINAL + 1)
                    nc.vector.tensor_tensor(T_g[:], RF[:], RF[:], ALU.mult).then_inc(rf_sq, 1)
                    dve.wait_ge(rf_sq, 1)
                    dve.wait_ge(stat2_ready, 1)
                    nc.vector.tensor_tensor(T_u[:], T_g[:], AUX[1][:], ALU.mult).then_inc(rf_scaled, 1)
                    dve.wait_ge(std2_made, 1)
                    nc.vector.reciprocal(T_g[:], STD[:]).then_inc(r_pair, 1)
                    dve.wait_ge(r_pair, 1)
                    nc.vector.tensor_tensor(R[:], T_g[:], RF[:], ALU.mult).then_inc(r_pair, 1)
                    dve.wait_ge(r_pair, 2)
                if 4 <= j <= 6:
                    index_sum(j - 3)
                if j >= 2:
                    k = INP_KINDS[j - 2]
                    if k == "kv":
                        dve.wait_ge(tr_ps, 2)
                    elif j - 2 in ROPE_UNITS:
                        dve.wait_ge(rope_made, 2 * ROPE_UNITS.index(j - 2) + 2)
                    elif k == "rv":
                        dve.wait_ge(rv_ps, 2 * (j - 2 - 7) + 2)
                    else:
                        dve.wait_ge(rg_made, 2 * (j - 2 - 9) + 2)
                for half in range(2):
                    dve.wait_ge(acc_ready, u.v(2, 1 + half))
                    nc.vector.tensor_tensor(T4[2 * (j % 2) + half][:], PS[2 * u.parity + half][:], R[:],
                                            ALU.mult).then_inc(rt_made, 1)
                dve.wait_ge(rt_made, 2 * j + 2)
                nc.vector.sem_inc(acc_free, 1)
                if j:
                    post(j - 1)
                if j == 2:
                    for m in range(DT):
                        nc.vector.scalar_tensor_tensor(out=X[:, m, :], in0=X[:, m, :], scalar=vec("final", m), in1=RF[:],
                                                       op0=ALU.mult, op1=ALU.mult).then_inc(x_ready, 1)
                if j in TOPK_AFTER:
                    choose(TOPK_AFTER[j])
            post(L.n - 1)

            def ret_out(t, step):
                if step < 4:
                    dve.wait_ge(rstd, t + 1)
                    if t:
                        dve.wait_ge(ro1, t)
                    c = slice(step * P, (step + 1) * P)
                    nc.vector.reciprocal(L2[:, 1, c], STD[:, c]).then_inc(rrec, 1)
                elif step == 4:
                    dve.wait_ge(rrec, 4 * (t + 1))
                    if t:
                        dve.wait_ge(m_lo_made, t)
                    nc.vector.tensor_tensor(E2[:, 0, :], AUX[t % 2][:], L2[:, 1, :], ALU.mult).then_inc(ro1, 1)

            dve.wait_ge(rope_made, 16)
            for n, (h, mb) in enumerate(RET_JOBS):
                w = SEQ - P * mb
                dve.wait_ge(rs_ps, n + 1)
                if mb == 0:
                    dve.wait_ge(d_in, 16 * (h + 1) if h >= 1 else 32)
                if n >= 2:
                    dve.wait_ge(ro_ps, n - 1)
                nc.vector.tensor_tensor(T4[n % 2][:, 0:w], PS[n % 2][:, 0:w], SQ[:, h % 2, 0:w], ALU.mult).then_inc(rd_made, 1)
                if n > 8 and n % 8 < 5:
                    ret_out(n // 8 - 1, n % 8)
                if n == 8:
                    ret_out(0, 0)
            for step in range(5):
                ret_out(3, step)

            def dsa_logits(n):
                t, b, half = DSA_JOBS[n]
                w = P * (b + 1)
                dve.wait_ge(a_s, n + 1)
                if n >= 2:
                    dve.wait_ge(a_e, n - 1)
                out_mask = later if b == 0 else ISC[:, b - 1, 0:w]
                if n == 0:
                    dve.wait_ge(left_out, 3)
                    dve.wait_ge(m_lo_made, 4)
                nc.vector.scalar_tensor_tensor(out=L2[:, n % 2, 0:w], in0=out_mask, scalar=NEG, in1=PS[n % 2][:, 0:w],
                                               op0=ALU.mult, op1=ALU.add).then_inc(a_l, 1)
                dve.wait_ge(a_l, n + 1)
                nc.vector.reduce_max(NM2[:, n % 2:n % 2 + 1], L2[:, n % 2, 0:w], AX.X).then_inc(a_m, 1)
                dve.wait_ge(a_m, n + 1)
                nc.vector.tensor_scalar(DEN[:, n % 2, 0:1], NM2[:, n % 2:n % 2 + 1], -HD ** -0.5, None, ALU.mult).then_inc(a_nm, 1)

            def lo_of_pair(t):
                dve.wait_ge(m_hi_made, 4 + t + 1)
                nc.vector.tensor_tensor(H_lo[:, 4 + t, :], AUX[t % 2][:], H_hi[:, 4 + t, :].bitcast(F32),
                                        ALU.subtract).then_inc(m_lo_made, 1)

            dsa_logits(0)
            for n, (t, b, half) in enumerate(DSA_JOBS):
                if n + 1 < len(DSA_JOBS):
                    dsa_logits(n + 1)
                dve.wait_ge(a_e, n + 1)
                if n >= 2:
                    dve.wait_ge(a_dg, n - 1)
                nc.vector.reciprocal(DEN[:, n % 2, 2:3], DEN[:, n % 2, 1:2]).then_inc(a_rd, 1)
                if n % 8 == 3 and n > 8:
                    lo_of_pair(t - 1)
            lo_of_pair(3)

            def y_steps(name, y0, add):
                L = layers[name]

                def step(j):
                    u = j.plus(L.base)
                    for half in range(2):
                        dve.wait_ge(acc_ready, u.v(2, half + 1))
                        m = At(2 * j.c + half, None if j.i is None else j.i * 2)
                        y = Y[:, bass.ds(m.v(), 1), :].rearrange("p o n -> p (o n)")
                        ps = PS[2 * u.parity + half][:]
                        if add:
                            i = nc.vector.tensor_tensor(y, ps, y, ALU.add)
                        else:
                            i = nc.vector.tensor_copy(y, ps)
                        i.then_inc(x_half, 1) if y0 is None else i.then_inc(y_ready, 1)
                    if y0 is None:
                        dve.wait_ge(x_half, j.v(2, 16 + 2))
                    else:
                        dve.wait_ge(y_ready, j.v(2, y0 + 2))
                    nc.vector.sem_inc(acc_free, 1)
                steps(dve, L.n, step)

            def add_normed(n, gain, k, here):
                rms(n)
                for m in range(DT):
                    if m >= 2 or k:
                        dve.wait_ge(x_ready, 40 + 8 * k + m - 1 if m >= 2 else 48)
                    nc.vector.scalar_tensor_tensor(out=T4[m % 2][:], in0=Y[:, m, :], scalar=vec(gain, m), in1=R[:],
                                                   op0=ALU.mult, op1=ALU.mult).then_inc(f_applied, 1)
                    if here:
                        dve.wait_ge(f_applied, 8 * k + m + 1)
                        nc.vector.tensor_tensor(X[:, m, :], X[:, m, :], T4[m % 2][:], ALU.add).then_inc(x_ready, 1)
                    elif m:
                        h_lo(FFN_PRE, "ffn_pre", At(m - 1))

            y_steps("wout", 0, False)
            add_normed(MIX_POST, "mix_post", 0, False)
            h_lo(FFN_PRE, "ffn_pre", At(DT - 1))

            def conv_gate_steps(name, j0, norm=None):
                L, q0 = layers[name], gu_base[name]
                q = q0 - 44

                def step(j):
                    u = j.plus(L.base)
                    b = u.parity
                    if j.i is None and j.c == 0 and norm is not None:
                        rms(norm)
                        dve.wait_ge(pad3_set, 1)
                    for i in range(2):
                        dve.wait_ge(acc_ready, u.v(2, 1 + i))
                        nc.vector.tensor_tensor(GP[:, i, 2:SEQ + 2], PS[2 * b + i][:], R[:], ALU.mult).then_inc(g3_in, 1)
                    dve.wait_ge(g3_in, j.v(2, 2 * q + 2))
                    nc.vector.sem_inc(acc_free, 1)
                    for i, y in enumerate((T_g, T_u)):
                        dve.wait_ge(c3_y, j.v(2, 2 * q + 1 + i))
                        nc.vector.scalar_tensor_tensor(out=y[:], in0=GP[:, i, 1:SEQ + 1], scalar=vec("conv3_w", j.plus(44 + 22 * i + j0)),
                                                       in1=y[:], op0=ALU.mult, op1=ALU.add).then_inc(c3_y1, 1)
                    for i, y in enumerate((T_g, T_u)):
                        dve.wait_ge(c3_y1, j.v(2, 2 * q + 1 + i))
                        nc.vector.scalar_tensor_tensor(out=y[:], in0=GP[:, i, 0:SEQ], scalar=vec("conv3_w", j.plus(22 * i + j0)),
                                                       in1=y[:], op0=ALU.mult, op1=ALU.add).then_inc(gate_in if i == 0 else c3_y2, 1)
                    dve.wait_ge(c3_y2, j.v(1, q + 1))
                    hidden(j, q0)
                steps(dve, L.n, step, first=1)

            conv_gate_steps("gu2a", 0, norm=FFN_PRE)
            y_steps("dn2a", None, False)
            conv_gate_steps("gu2b", 11)
            y_steps("dn2b", 8, True)
            add_normed(FFN_POST, "ffn_post", 1, True)


def constants(np):
    f = np.float32
    cmat = np.zeros((P, 9, P), f)
    p = np.arange(P)
    cmat[p, 0, p] = 1
    cmat[:, 1] = 1
    cmat[(p // HD) * HD + (p + HD // 2) % HD, 2, p] = 1
    cmat[p % HD, 3, p] = 1
    cmat[(p + HD // 2) % HD, 4, p] = 1
    cmat[:, 5] = p[:, None] // HD == p[None, :] // HD
    for i in range(2):
        cmat[2 * i + p // HD, 6 + i, p] = 1
    cmat[:, 8] = p[None, :] > p[:, None]

    onehot = np.zeros((BUCKETS + 1, 3, DIAG), f)
    for g, (dilation, zero, far) in enumerate(((1, 2 * P - 1, P), (4, P - 1, P - 1), (16, 31, 31))):
        for x in range(DIAG):
            dist = zero - x
            if not 0 <= dist <= far:
                onehot[BUCKETS, g, x] = 1
                continue
            n = dist * dilation
            large = 16 + int(np.log(f(max(n, 1)) / f(16)) / f(np.log(2048 / 16)) * f(16)) if n >= 16 else 0
            onehot[n if n < 16 else min(large, BUCKETS - 1), g, x] = 1

    inv = f(10000.0) ** (-np.arange(0, HD, 2, dtype=f) / f(HD))
    ang = np.arange(SEQ, dtype=f)[:, None] * inv[None, :]
    cos, sin = np.cos(ang).T, np.sin(ang).T
    rotary = np.stack([np.concatenate([cos] * 4), np.concatenate([-sin, sin] * 2)], 1)

    diff = np.arange(SEQ)[None, :] - p[:, None]
    log_g = np.log(1.0 - 2.0 ** (-5.0 - np.arange(RET_HEADS)))
    decay = np.where(diff >= 0, np.exp(log_g[:, None, None] * np.maximum(diff, 0)), 0.0) * HD ** -0.5
    return {"cmat": cmat, "onehot": onehot, "rotary": rotary.astype(f), "decay": decay.astype(f)}


def kernel(**inputs):
    import numpy as np
    import concourse.bacc as bacc
    from concourse.bass_utils import run_bass_kernel_spmd as run

    g = {k: np.asarray(v) for k, v in inputs.items()}

    def rows(w, cols, kt):
        w = w[:, cols] if cols is not None else w
        k, n = w.shape
        return np.ascontiguousarray(w.reshape(k // P, P, n // COLS, COLS)[:].transpose(2, 1, 0, 3)
                                    .reshape(n // COLS, P, (k // P) * COLS))

    def paired(a, b):
        k, n = a.shape
        return np.stack([a.reshape(k, n // P, P), b.reshape(k, n // P, P)], 2).reshape(k, 2 * n)

    def tiles(v):
        v = v.reshape(-1, v.shape[-1] // P, P)
        return v.transpose(2, 0, 1).reshape(P, -1)

    arrays = {}
    pw1 = g["conv_w_pw1"][0]
    arrays["pw1"] = rows(paired(pw1[:, :D_MODEL], pw1[:, D_MODEL:]), None, 8)
    arrays["pw2"] = rows(g["conv_w_pw2"][0], None, 8)
    up2 = g["w_up_2"][0]
    gates = [g["ffn_w_gate"][0], g["ffn_w_gate"][1], up2[:, :FF_TILES * P]]
    ups = [g["ffn_w_up"][0], g["ffn_w_up"][1], up2[:, FF_TILES * P:]]
    downs = [g["ffn_w_down"][0], g["ffn_w_down"][1], g["w_down_2"][0]]
    qkv = g["attn_w_qkv"][0]
    arrays["qkv"] = rows(np.concatenate([qkv[:, 1536:], qkv[:, :1536]], 1), None, 8)
    arrays["wo"] = rows(g["attn_w_o"][0], None, 6)
    w_in = g["w_in_2"][0]
    arrays["inp"] = rows(np.concatenate([w_in[:, 2560:2688], w_in[:, 3200:3272], np.zeros((D_MODEL, 56), np.float32),
                                         w_in[:, 2688:3200], w_in[:, :2560]], 1), None, 8)
    arrays["wout"] = rows(g["w_out_2"][0], None, 8)
    arrays["rel_bias"] = g["rel_bias"]
    for l in range(3):
        gu = rows(paired(gates[l], ups[l]), None, 8)
        dn = downs[l]
        h = FF_HALF * P
        arrays[f"gu{l}a"], arrays[f"gu{l}b"] = gu[:FF_HALF], gu[FF_HALF:]
        arrays[f"dn{l}a"], arrays[f"dn{l}b"] = rows(dn[:h], None, 11), rows(dn[h:], None, 11)
    arrays["x"] = g["x"][0].T.reshape(DT, P, SEQ).transpose(1, 0, 2)
    parts = {"norm_mix0": g["norm_mix"][0], "norm_mix1": g["norm_mix"][1], "norm_ffn0": g["norm_ffn"][0],
             "norm_ffn1": g["norm_ffn"][1], "final": g["final_norm"], "b_pw1": g["conv_b_pw1"][0],
             "w_dw": g["conv_w_dw"][0], "b_dw": g["conv_b_dw"][0], "ln_g": g["conv_ln_g"][0],
             "ln_b": g["conv_ln_b"][0], "b_pw2": g["conv_b_pw2"][0],
             "mix_pre": g["mix_norm_pre_2"][0], "mix_post": g["mix_norm_post_2"][0],
             "ffn_pre": g["ffn_norm_pre_2"][0], "ffn_post": g["ffn_norm_post_2"][0],
             "conv3_w": g["conv_w_2"][0], "conv3_b": g["conv_b_2"][0]}
    arrays["vecs"] = np.concatenate([tiles(parts[n]) for n, _ in VECS], 1)
    arrays.update(constants(np))
    arrays = {k: np.ascontiguousarray(v) for k, v in arrays.items()}

    nc = bacc.Bacc("TRN2", target_bir_lowering=False, num_devices=1)
    aps = {k: nc.dram_tensor(f"in_{k}", v.shape, mybir.dt.from_np(v.dtype), kind="ExternalInput").ap()
           for k, v in arrays.items()}
    out = nc.dram_tensor("out", (P, DT, SEQ), F32, kind="ExternalOutput").ap()
    build(nc, aps, out)
    r = run(nc, [{f"in_{k}": v for k, v in arrays.items()}], core_ids=[0])
    y = r.results[0]["out"]
    return np.ascontiguousarray(np.asarray(y).transpose(1, 0, 2).reshape(D_MODEL, SEQ).T)[None]
```

```python
import concourse.bass as bass
from concourse import mybir
from concourse.alu_op_type import AluOpType as ALU
from contextlib import ExitStack

F32 = mybir.dt.float32
F32R = mybir.dt.float32r
ACT = mybir.ActivationFunctionType
AX = mybir.AxisListType

P = 128
SEQ = 512
D_MODEL = 1024
DT = D_MODEL // P
CONV_WIDTH = 31
FF_TILES = 22
FF_HALF = FF_TILES // 2
EPS = 1e-6
COLS = 256
UNIT_K = FF_HALF

LAYERS = [("pw1", 8, 8), ("pw2", 4, 8),
          ("gu0a", 11, 8), ("dn0a", 4, 11), ("gu0b", 11, 8), ("dn0b", 4, 11),
          ("qkv", 9, 8), ("wo", 4, 6),
          ("gu1a", 11, 8), ("dn1a", 4, 11), ("gu1b", 11, 8), ("dn1b", 4, 11),
          ("inp", 13, 8), ("wout", 4, 8),
          ("gu2a", 11, 8), ("dn2a", 4, 11), ("gu2b", 11, 8), ("dn2b", 4, 11)]

VECS = [("norm_mix0", 8), ("norm_mix1", 8), ("norm_ffn0", 8), ("norm_ffn1", 8), ("final", 8),
        ("b_pw1", 16), ("w_dw", CONV_WIDTH * 8), ("b_dw", 8), ("ln_g", 8), ("ln_b", 8), ("b_pw2", 8),
        ("mix_pre", 8), ("mix_post", 8), ("ffn_pre", 8), ("ffn_post", 8), ("conv3_w", 3 * 44), ("conv3_b", 44)]

MIX0, FFN0, MIX1, FFN1, FINAL, MIX_POST, FFN_PRE, FFN_POST = range(8)
X_BASE = {FFN0: 0, MIX1: 8, FFN1: 16, FINAL: 24, FFN_PRE: 40}
H_BASE = {MIX0: 0, FFN0: 8, MIX1: 16, FFN1: 24, FINAL: 32, FFN_PRE: 40}
Y_BASE = {MIX_POST: 0, FFN_POST: 8}

HD = 64
GROUP_HEADS = 4
BUCKETS = 32
NEG = -1e30
DIAG = 384
TOPK = 128
RET_HEADS = 8


CONV_DVE = 6
CONV_SPLIT = 16
TAP_CHUNK = 16
CONV_CHUNKS = [(CONV_DVE - 1, CONV_SPLIT, CONV_WIDTH)]
CONV_CHUNKS += [(m, c, min(CONV_WIDTH, c + TAP_CHUNK)) for m in range(CONV_DVE, DT) for c in range(0, CONV_WIDTH, TAP_CHUNK)]
TAPS_PER_UNIT = 15


def dilated_jobs():
    jobs = []
    for h in range(12):
        if h < GROUP_HEADS:
            jobs.append((h, [(0, 0, 128, [0]), (1, 128, 256, [0, 1])]))
            jobs.append((h, [(2, 0, 256, [1, 2]), (3, 256, 256, [2, 3])]))
        else:
            jobs.append((h, [(b, 128 * b, 128, [b]) for b in range(4)]))
    return jobs


GROUP_ENDS = [8, 12]
DSA_JOBS = [(t, half, b) for t in range(4) for half in range(2) for b in range(4)]
RET_JOBS = [(h, mb) for h in range(RET_HEADS) for mb in range(4)]
RET_IN_SLOT = [(0, 1), (2, None), (3, 4), (5, None), (6, 7), (None, None), (None, None), (None, None)]


def ret_jobs(slot):
    return [None if r is None else 8 * (slot // 8) + r for r in RET_IN_SLOT[slot % 8]]


INP_KINDS = ["kv", "iq", "iq", "aq", "aq", "rv", "rv", "rq", "rq", "rk", "rk", "rg", "rg"]
RV_UNIT, RG_UNIT = INP_KINDS.index("rv"), INP_KINDS.index("rg")
ROPE_UNITS = [j for j, k in enumerate(INP_KINDS) if k in ("iq", "rq", "rk", "aq")]
TOPK_AFTER = {4: 4, 5: 6, 6: 6, 7: 6, 8: 6, 9: 6, 10: 5, 11: 5, 12: 4}


class Layer:

    def __init__(self, name, n, kt, base):
        self.name, self.n, self.kt, self.base = name, n, kt, base


class At:

    def __init__(self, c, i=None):
        self.c, self.i = c, i

    def v(self, mult=1, add=0):
        if self.i is None:
            return mult * self.c + add
        return self.i * (2 * mult) + (mult * self.c + add)

    def plus(self, n):
        return At(self.c + n, self.i)

    def half(self, mult, add):
        if self.i is None:
            return mult * (self.c // 2) + add
        return self.i * mult + (mult * (self.c // 2) + add)

    @property
    def parity(self):
        return self.c % 2


def steps(eng, n, step, first=0, last=0):
    pairs = (n - first - last) // 2
    if pairs < 2:
        pairs = 0
    for j in range(first):
        step(At(j))
    if pairs:
        with eng.Fori(0, pairs) as i:
            step(At(first, i))
            step(At(first + 1, i))
    for j in range(first + 2 * pairs, n):
        step(At(j))


def build(nc, a, out):
    layers, base = {}, 0
    for name, n, kt in LAYERS:
        layers[name] = Layer(name, n, kt, base)
        base += n
    units = base
    order = [layers[x[0]] for x in LAYERS]
    kts = [l.kt for l in order for _ in range(l.n)]
    vec_at, n_vec = {}, 0
    for name, n in VECS:
        vec_at[name] = n_vec
        n_vec += n

    ctx = ExitStack()
    with ctx:
        top = [(nc.sbuf_base + 31) // 32 * 32]

        def sb(name, shape, dt=F32, at=None):
            size = 4
            for s in shape[1:]:
                size *= s
            size = (size + 31) // 32 * 32
            if at is None:
                at = top[0]
                top[0] += size
            return nc.alloc_sbuf_tensor_at(name, shape, dt, offset=at)

        X = sb("X", [P, DT, SEQ])
        H_hi = sb("H_hi", [P, DT, SEQ], F32R)
        H_lo = sb("H_lo", [P, DT, SEQ], F32R)
        W_raw = [sb(f"W_raw{b}", [P, UNIT_K * COLS]) for b in range(2)]
        W_hi = [sb(f"W_hi{b}", [P, UNIT_K * COLS], F32R) for b in range(2)]
        W_lo = [sb(f"W_lo{b}", [P, UNIT_K * COLS], F32R) for b in range(2)]
        cmat = sb("cmat", [P, 9, P])
        vecs = sb("vecs", [P, n_vec])
        epst = sb("epst", [P, 1])
        R = sb("R", [P, SEQ])
        STD = sb("STD", [P, SEQ])
        SSUM = sb("SSUM", [P, SEQ])
        SQ = sb("SQ", [P, 2, SEQ])
        T_g = sb("T_g", [P, SEQ])
        T_u = sb("T_u", [P, SEQ])
        T_act = sb("T_act", [P, SEQ])
        T_hid = sb("T_hid", [P, SEQ])
        FG = sb("FG", [P, DT])
        arena = top[0]
        HID_hi = sb("HID_hi", [P, FF_HALF, SEQ], F32R, at=arena)
        HID_lo = sb("HID_lo", [P, FF_HALF, SEQ], F32R, at=arena + FF_HALF * SEQ * 4)
        PADDED = SEQ + CONV_WIDTH - 1 + 2
        U = sb("U", [P, DT, PADDED], at=arena)
        CV = sb("CV", [P, DT, SEQ], at=arena + 2 * FF_HALF * SEQ * 4)
        VQK = sb("VQK", [P, 18, SEQ], at=arena)
        OU = sb("OU", [P, 6, SEQ], at=arena)
        ROW_w = sb("ROW_w", [GROUP_HEADS, 3, SEQ], at=arena + 12288)
        ROW_max = sb("ROW_max", [GROUP_HEADS, SEQ], at=arena + 18432)
        ROW_sum = sb("ROW_sum", [GROUP_HEADS, SEQ], at=arena + 20480)
        ROW_den = sb("ROW_den", [GROUP_HEADS, 3, SEQ], at=arena + 36864)
        B0 = sb("B0", [P, GROUP_HEADS, 256], at=arena + 36864)
        B1 = sb("B1", [P, GROUP_HEADS, P], at=arena + 40960)
        B2 = sb("B2", [P, GROUP_HEADS, P], at=arena + 43008)
        VT = sb("VT", [P, 6, 4, P], at=arena + 45056)
        L1 = sb("L1", [P, 2, SEQ], at=arena + 57344)
        E1 = sb("E1", [P, 2, SEQ], at=arena + 61440)
        PT1 = sb("PT1", [P, 2, SEQ], at=arena + 65536)
        MD = sb("MD", [P, 2, 4, 12], at=arena + 69632)
        NM = sb("NM", [P, 2, 4], at=arena + 70016)
        onehot = sb("onehot", [BUCKETS + 1, 3, DIAG], at=arena + 57344)
        table = sb("table", [BUCKETS + 1, 12], at=arena + 62080)
        table_wide = sb("table_wide", [BUCKETS + 1, 12, P], at=arena + 62208)
        fvec = sb("fvec", [P, 12, DIAG], at=arena + 26112)
        Y = sb("Y", [P, DT, SEQ], at=arena + 45056)
        GP = sb("GP", [P, 2, SEQ + 2], at=arena + 61440)
        AQ = sb("AQ", [P, 4, SEQ], at=arena)
        RQK = sb("RQK", [P, 8, SEQ], at=arena + 8192)
        RVT = sb("RVT", [P, 4, SEQ], at=arena + 24576)
        GS = sb("GS", [P, 4, SEQ], at=arena + 32768)
        IQ = sb("IQ", [P, 4, SEQ], at=arena + 40960)
        CS = sb("CS", [P, 2, SEQ], at=arena + 49152)
        KK = sb("KK", [P, SEQ], at=arena + 53248)
        II = sb("II", [P, SEQ], at=arena + 55296)
        ISC = sb("ISC", [P, 3, SEQ], at=arena + 57344)
        WK = sb("WK", [P, SEQ], at=arena + 63488)
        AV = sb("AV", [P, 4, P], at=arena + 67840)
        LEFT = sb("LEFT", [P, 3, SEQ], F32R, at=arena + 57344)
        LEFT0 = sb("LEFT0", [P, P], F32R, at=arena + 40960)
        neg_ident = sb("neg_ident", [P, P], F32R, at=arena + 41472)
        IW = sb("IW", [P, 4, 8], at=arena + 66560)
        TOP8 = sb("TOP8", [P, 8], at=arena + 66688)
        NEGMAX = sb("NEGMAX", [P, 2], at=arena + 66720)
        E2 = sb("E2", [P, 2, SEQ], at=arena + 45056)
        PT2 = sb("PT2", [P, 2, SEQ], at=arena + 49152)
        CVacc = T_hid
        UP_hi = sb("UP_hi", [P, DT - CONV_DVE, PADDED], F32R, at=arena + 17408)
        UP_lo = sb("UP_lo", [P, DT - CONV_DVE, PADDED], F32R, at=arena + 21760)
        UPS_hi = sb("UPS_hi", [P, 1, PADDED], F32R, at=arena + 62208)
        UPS_lo = sb("UPS_lo", [P, 1, PADDED], F32R, at=arena + 64384)
        UPS = [(UPS_hi, UPS_lo, 0)] + [(UP_hi, UP_lo, m) for m in range(DT - CONV_DVE)]
        tap_hi = sb("tap_hi", [P, CONV_WIDTH * DT], F32R, at=arena + 68352)
        tap_lo = sb("tap_lo", [P, CONV_WIDTH * DT], F32R, at=arena + 69344)
        RF = sb("RF", [P, SEQ], at=arena + 32768)
        SSUM2 = sb("SSUM2", [P, SEQ], at=arena + 61440)
        SQ2 = sb("SQ2", [P, 2, SEQ], at=arena + 63488)

        NM2 = sb("NM2", [P, 2], at=arena + 67776)
        L2k = [WK[:], ISC[:, 2, :]]
        T4 = [T_g, T_u, T_act, T_hid]
        bias_scratch = nc.dram_tensor("bias_scratch", (12, P, DIAG), F32, kind="Internal").ap()

        PS = [ctx.enter_context(nc.psum_tensor(f"PS{i}", [P, SEQ], F32)) for i in range(8)]
        AUX = PS[4:8]

        def vec(name, j, n=1):
            o = vec_at[name]
            if isinstance(j, At):
                return vecs[:, bass.ds(j.v(1, o), 1)]
            return vecs[:, o + j:o + j + 1]

        ident, ones, swap, dup, dupswap, headsum = (cmat[:, i, :] for i in range(6))
        sel = [cmat[0:GROUP_HEADS, 6 + i, :] for i in range(2)]
        later = cmat[:, 8, :]

        def tokens(ap, blk):
            return ap[:, blk * P:(blk + 1) * P]

        DILATION = (1, 4, 16)

        def permuted(ap, g):
            return ap.rearrange("p (r i) -> p i r", r=DILATION[g]) if g else ap

        def by_step(ap, g):
            return ap.rearrange("p (i r) -> p i r", r=DILATION[g]) if g else ap

        def unpermuted(ap, g):
            if g == 0:
                return ap
            if g == 1:
                return ap.rearrange("p (i b) -> p b i", b=4)
            return ap.rearrange("p (i r) -> p r i", r=16)

        def blocked(ap, g):
            if g == 0:
                return ap
            return ap.rearrange("p (b i) -> p b i", b=4 if g == 1 else 16)

        JOBS = dilated_jobs()

        def sem(name):
            return ctx.enter_context(nc.semaphore(name))

        x_in = [sem(f"x_in{i}") for i in range(4)]
        vec_in = sem("vec_in")
        const2_in = sem("const2_in")
        const_in = sem("const_in")
        eps_set = sem("eps_set")
        raw_in = [sem(f"raw_in{b}") for b in range(2)]
        w_hi = sem("w_hi")
        w_lo = sem("w_lo")
        acc_ready = sem("acc_ready")
        acc_free = sem("acc_free")
        x_ready = sem("x_ready")
        h_hi_made = sem("h_hi_made")
        h_lo_made = sem("h_lo_made")
        sq_made = sem("sq_made")
        ss_made = sem("ss_made")
        stat_ready = sem("stat_ready")
        std_made = sem("std_made")
        r_made = sem("r_made")
        gate_in = sem("gate_in")
        gate_act = sem("gate_act")
        hid_made = sem("hid_made")
        hid_hi_made = sem("hid_hi_made")
        hid_lo_made = sem("hid_lo_made")
        pads_set = sem("pads_set")
        glu_made = sem("glu_made")
        conv_step = sem("conv_step")
        conv_made = sem("conv_made")
        ln_sum = sem("ln_sum")
        ln_sum_ready = sem("ln_sum_ready")
        mu_made = sem("mu_made")
        xc_made = sem("xc_made")
        xc_sq = sem("xc_sq")
        ln_var_ready = sem("ln_var_ready")
        ln_std = sem("ln_std")
        ln_r = sem("ln_r")
        ln_scaled = sem("ln_scaled")
        ln_act = sem("ln_act")
        ln_hi_made = sem("ln_hi_made")
        ln_lo_made = sem("ln_lo_made")
        x_half = sem("x_half")
        out_done = sem("out_done")
        tab_wide = sem("tab_wide")
        pv_done = sem("pv_done")
        v_t = sem("v_t")
        v_tok = sem("v_tok")
        tab_in = sem("tab_in")
        tab_pad = sem("tab_pad")
        fvec_ps = sem("fvec_ps")
        fvec_made = sem("fvec_made")
        scr_out = sem("scr_out")
        b2_set = sem("b2_set")
        bias_in = sem("bias_in")
        qkv_made = sem("qkv_made")
        s_made = sem("s_made")
        l_made = sem("l_made")
        m_made = sem("m_made")
        nm_made = sem("nm_made")
        e_made = sem("e_made")
        pt_ps = sem("pt_ps")
        pt_made = sem("pt_made")
        ou_made = sem("ou_made")
        st_ps = sem("st_ps")
        row_made = sem("row_made")
        rowmax = sem("rowmax")
        rowd = sem("rowd")
        roww = sem("roww")
        rowwd = sem("rowwd")
        rows_ = sem("rows_")
        rowf = sem("rowf")
        f_ps = sem("f_ps")
        o_made = sem("o_made")
        o_hi_made = sem("o_hi_made")
        o_lo_made = sem("o_lo_made")
        y_ready = sem("y_ready")
        f_applied = sem("f_applied")
        cs_in = sem("cs_in")
        rt_made = sem("rt_made")
        sw_ps = sem("sw_ps")
        rope_c = sem("rope_c")
        rope_s = sem("rope_s")
        rope_made = sem("rope_made")
        kv_ps = sem("kv_ps")
        kv_c = sem("kv_c")
        kv_s = sem("kv_s")
        kv_made = sem("kv_made")
        tr_ps = sem("tr_ps")
        av_made = sem("av_made")
        rv_ps = sem("rv_ps")
        rv_tok = sem("rv_tok")
        rg_made = sem("rg_made")
        idx_ps = sem("idx_ps")
        idx_rel = sem("idx_rel")
        isc_made = sem("isc_made")
        isc_mask = sem("isc_mask")
        top_max = sem("top_max")
        top_rep = sem("top_rep")
        left_out = sem("left_out")
        d_in = [sem(f"d_in{b}") for b in range(2)]
        a_hi_made = sem("a_hi_made")
        a_lo_made = sem("a_lo_made")
        rs_ps = sem("rs_ps")
        rd_made = sem("rd_made")
        ro_ps = sem("ro_ps")
        r_sq = sem("r_sq")
        rsum_ps = sem("rsum_ps")
        rstd = sem("rstd")
        rrec = sem("rrec")
        ro1 = sem("ro1")
        ro2 = sem("ro2")
        m_hi_made = sem("m_hi_made")
        m_lo_made = sem("m_lo_made")
        a_s = sem("a_s")
        mask_made = sem("mask_made")
        av_ones = sem("av_ones")
        a_m = sem("a_m")
        a_nm = sem("a_nm")
        a_e = sem("a_e")
        a_rec = sem("a_rec")
        a_norm = sem("a_norm")
        a_pt_ps = sem("a_pt_ps")
        a_pt = sem("a_pt")
        a_o = sem("a_o")
        c3_y = sem("c3_y")
        c3_y1 = sem("c3_y1")
        c3_y2 = sem("c3_y2")
        pad3_set = sem("pad3_set")
        g3_in = sem("g3_in")
        w_parts = sem("w_parts")
        u_hi = sem("u_hi")
        u_lo = sem("u_lo")
        diag_hi = sem("diag_hi")
        diag_lo = sem("diag_lo")
        conv_pe = sem("conv_pe")
        conv_pe_taken = sem("conv_pe_taken")
        fg_made = sem("fg_made")
        rf_sq = sem("rf_sq")
        rf_scaled = sem("rf_scaled")
        r_pair = sem("r_pair")
        ssum2 = sem("ssum2")
        ssum2_sq = sem("ssum2_sq")
        stat2_ready = sem("stat2_ready")
        std2_made = sem("std2_made")

        block = ctx.enter_context(nc.Block())

        gu_base = {f"gu{l}{h}": 22 * l + 11 * k for l in range(3) for k, h in enumerate("ab")}

        @block.sync
        def _(sp):
            def load(L, src, j):
                u = j.plus(L.base)
                b = u.parity
                if u.i is not None or u.c >= 2:
                    sp.wait_ge(w_lo, u.v(1, -1))
                n = L.kt * COLS
                sp.dma_start(W_raw[b][:, 0:n], src[bass.ds(j.v(), 1)].rearrange("o p n -> p (o n)") if j.i is not None else src[j.c]).then_inc(raw_in[b], 16)

            sp.dma_start(vecs[:], a["vecs"]).then_inc(vec_in, 16)
            for i in range(4):
                sp.dma_start(X[:, 2 * i:2 * i + 2, :], a["x"][:, 2 * i:2 * i + 2, :]).then_inc(x_in[i], 16)
                if i < 2:
                    load(order[0], a["pw1"], At(i))

            for k, L in enumerate(order):
                if k == 0:
                    with sp.Fori(0, L.n // 2 - 1) as i:
                        load(L, a[L.name], At(2, i))
                        load(L, a[L.name], At(3, i))
                    continue
                steps(sp, L.n, lambda j: load(L, a[L.name], j))
            sp.wait_ge(x_ready, 56)
            sp.dma_start(out, X[:]).then_inc(out_done, 16)
            sp.wait_ge(out_done, 16)

        @block.tensor
        def _(pe):
            def after(made, base):
                return lambda k: (made, base + k + 1)

            def products(b, kt, half, x_hi, x_lo, ready=None, between=None):
                dst = PS[2 * b + half]
                for k in range(kt):
                    if ready is not None:
                        pe.wait_ge(*ready(k))
                    c = k * COLS + half * P
                    wh, wl = W_hi[b][:, c:c + P], W_lo[b][:, c:c + P]
                    nc.tensor.matmul(dst[:], wh, x_hi[:, k, :], start=(k == 0), stop=False)
                    nc.tensor.matmul(dst[:], wh, x_lo[:, k, :], start=False, stop=False)
                    last = nc.tensor.matmul(dst[:], wl, x_hi[:, k, :], start=False, stop=(k == kt - 1))
                    if between is not None and k % 2 and k < kt - 1:
                        between()
                last.then_inc(acc_ready, 1)
                if between is not None:
                    between()

            def unit(L, j, x_hi, x_lo, ready=None, between=None, beside_second=None):
                u = j.plus(L.base)
                pe.wait_ge(w_lo, u.v(1, 1))
                if u.i is not None or u.c >= 2:
                    pe.wait_ge(acc_free, u.v(1, -1))
                products(u.parity, L.kt, 0, x_hi, x_lo, ready, between)
                products(u.parity, L.kt, 1, x_hi, x_lo, None, between or beside_second)

            def rms_sum(n):
                if n:
                    pe.wait_ge(std_made, n)
                pe.wait_ge(ss_made, 7 * (n + 1))
                last = nc.tensor.matmul(AUX[0][:], ones, SSUM[:], start=True, stop=True)
                last.then_inc(stat_ready, 1)

            def linear(name, x_hi=H_hi, x_lo=H_lo, ready=None, norm=None, beside_last=None):
                L = layers[name]

                def step(j):
                    first = j.i is None and j.c == 0
                    last = j.i is None and j.c == L.n - 1
                    unit(L, j, x_hi, x_lo, ready if first else None, None, beside_last if last else None)
                    if first and norm is not None:
                        rms_sum(norm)
                steps(pe, L.n, step, first=1)

            pe.wait_ge(const_in, 16)
            heads_beside = [[], range(4), range(4, 8), range(8, 12)]

            def bias_products():
                for h in heads_beside.pop(0):
                    if h == 0:
                        pe.wait_ge(tab_wide, 1)
                        pe.wait_ge(const2_in, 16)
                    if h >= 2:
                        pe.wait_ge(fvec_made, h - 1)
                    nc.tensor.matmul(AUX[1 + h % 2][:, 0:DIAG], table_wide[:, h, :], onehot[:, h // GROUP_HEADS, :],
                                     start=True, stop=True).then_inc(fvec_ps, 1)

            linear("pw1", ready=after(h_lo_made, 0), norm=0, beside_last=bias_products)
            pe.wait_ge(fvec_made, 12)
            for n, (m, t0, t1) in enumerate(CONV_CHUNKS):
                p = m - CONV_DVE + 1
                xh, xl, row = UPS[p]
                pe.wait_ge(diag_lo, n + 1)
                pe.wait_ge(diag_hi, n + 1)
                pe.wait_ge(u_lo, p + 1)
                for t in range(t0, t1):
                    k = TAP_CHUNK * (n % 2) + t - t0
                    d_hi = H_hi[:, k // 4, P * (k % 4):P * (k % 4 + 1)]
                    d_lo = H_lo[:, k // 4, P * (k % 4):P * (k % 4 + 1)]
                    x_hi, x_lo = xh[:, row, t:t + SEQ], xl[:, row, t:t + SEQ]
                    first, end = t == (0 if p else CONV_SPLIT), t == CONV_WIDTH - 1
                    nc.tensor.matmul(AUX[p][:], d_hi, x_hi, start=first, stop=False)
                    nc.tensor.matmul(AUX[p][:], d_hi, x_lo, start=False, stop=False)
                    last = nc.tensor.matmul(AUX[p][:], d_lo, x_hi, start=False, stop=end)
                last.then_inc(conv_pe, 1)
            pe.wait_ge(ln_sum, CONV_DVE - 1)
            nc.tensor.matmul(AUX[3][:], ones, SSUM[:], start=True, stop=False)
            for m in range(CONV_DVE, DT):
                pe.wait_ge(conv_pe_taken, m - CONV_DVE + 1)
                nc.tensor.matmul(AUX[3][:], ones, CV[:, m, :], start=False, stop=False)
            pe.wait_ge(conv_made, CONV_DVE)
            last = nc.tensor.matmul(AUX[3][:], ones, CV[:, CONV_DVE - 1, :], start=False, stop=True)
            last.then_inc(ln_sum_ready, 1)
            for m in range(DT):
                pe.wait_ge(xc_sq, m + 1)
                nc.tensor.matmul(AUX[2][:], ones, SQ[:, m % 2, :], start=(m == 0), stop=(m == DT - 1)).then_inc(ln_var_ready, 1)
            linear("pw2", HID_hi, HID_lo, ready=after(ln_lo_made, 0))

            def feed_forward(l, norm):
                linear(f"gu{l}a", ready=after(h_lo_made, H_BASE[norm]), norm=norm)
                linear(f"dn{l}a", HID_hi, HID_lo, ready=after(hid_lo_made, gu_base[f"gu{l}a"]))
                linear(f"gu{l}b")
                linear(f"dn{l}b", HID_hi, HID_lo, ready=after(hid_lo_made, gu_base[f"gu{l}b"]))

            feed_forward(0, FFN0)

            linear("qkv", ready=after(h_lo_made, H_BASE[MIX1]), norm=MIX1)
            for t in range(6):
                pe.wait_ge(qkv_made, t + 1)
                if t == 0:
                    pe.wait_ge(std_made, MIX1 + 1)
                if t >= 4:
                    pe.wait_ge(v_tok, t - 3)
                for b in range(4):
                    last = nc.tensor.transpose(AUX[t % 4][:, b * P:(b + 1) * P], tokens(VQK[:, t, :], b), ident)
                last.then_inc(v_t, 1)

            def dilated_scores(n):
                h, blks = JOBS[n]
                g, t, lo = h // GROUP_HEADS, h // 2, HD * (h % 2)
                if n == 0:
                    pe.wait_ge(qkv_made, 18)
                if n >= 2:
                    pe.wait_ge(l_made, n - 1)
                for blk, c, w, keys in blks:
                    q = tokens(VQK[lo:lo + HD, 6 + t, :], blk)
                    k = VQK[lo:lo + HD, 12 + t, :]
                    k = k[:, P * keys[0]:P * (keys[-1] + 1)] if g == 0 else tokens(k, blk)
                    last = nc.tensor.matmul(PS[n % 2][:, c:c + w], q, k, start=True, stop=True)
                last.then_inc(s_made, 1)

            dilated_scores(0)
            dilated_scores(1)
            def chunks(n):
                return [(blk, c + P * i, key) for blk, c, w, keys in JOBS[n][1] for i, key in enumerate(keys)]

            def dilated_values(n):
                h, blks = JOBS[n]
                t, lo = h // 2, HD * (h % 2)
                pe.wait_ge(pt_made, n + 1)
                if n == 0:
                    pe.wait_ge(v_tok, 6)
                if h % 2 == 0 and blks[0][0] == 0 and t >= 2:
                    pe.wait_ge(ou_made, t - 1)
                ch = chunks(n)
                for i, (blk, c, key) in enumerate(ch):
                    first = i == 0 or ch[i - 1][0] != blk
                    end = i + 1 == len(ch) or ch[i + 1][0] != blk
                    last = nc.tensor.matmul(PS[4 + t % 2][lo:lo + HD, blk * P:(blk + 1) * P],
                                            VT[:, t, key, lo:lo + HD], PT1[:, n % 2, i * P:(i + 1) * P],
                                            start=first, stop=end)
                last.then_inc(pv_done, 1)

            def rows(g):
                for kind in range(2):
                    i = 2 * g + kind
                    if i >= 2:
                        pe.wait_ge(row_made, i - 1)
                    for b in range(4):
                        last = nc.tensor.matmul(PS[6 + i % 2][0:GROUP_HEADS, b * P:(b + 1) * P],
                                                MD[:, kind, b, 4 * g:4 * g + 4], ident, start=True, stop=True)
                    last.then_inc(st_ps, 1)

            for n in range(len(JOBS)):
                pe.wait_ge(e_made, n + 1)
                if n in GROUP_ENDS:
                    rows(GROUP_ENDS.index(n))
                if n >= 2:
                    pe.wait_ge(pt_made, n - 1)
                for i, (blk, c, key) in enumerate(chunks(n)):
                    last = nc.tensor.transpose(PS[2 + n % 2][:, i * P:(i + 1) * P], E1[:, n % 2, c:c + P], ident)
                last.then_inc(pt_ps, 1)
                if n:
                    dilated_values(n - 1)
                if n + 2 < len(JOBS):
                    dilated_scores(n + 2)
            rows(2)
            dilated_values(len(JOBS) - 1)
            for t in range(6):
                if t == 0:
                    pe.wait_ge(rowf, 1)
                    pe.wait_ge(row_made, 6)
                if t >= 2:
                    pe.wait_ge(o_made, t - 1)
                nc.tensor.matmul(PS[6 + t % 2][:], sel[t % 2], ROW_w[:, t // 2, :], start=True,
                                 stop=True).then_inc(f_ps, 1)
            linear("wo", HID_hi, HID_lo, ready=after(o_lo_made, 0))

            feed_forward(1, FFN1)
            L = layers["inp"]

            def post(j):
                kind = INP_KINDS[j]
                pe.wait_ge(rt_made, 2 * j + 2)
                if kind == "kv":
                    for i in range(4):
                        nc.tensor.matmul(AUX[i][:], (dup, dupswap)[i % 2], T4[i // 2][:], start=True,
                                         stop=True).then_inc(kv_ps, 1)
                    for i in range(2):
                        pe.wait_ge(kv_c, 2)
                        pe.wait_ge(kv_s, 2)
                        for b in range(4):
                            last = nc.tensor.transpose(AUX[i][:, b * P:(b + 1) * P], T4[i][:, b * P:(b + 1) * P], ident)
                        last.then_inc(tr_ps, 1)
                elif j in ROPE_UNITS:
                    r = ROPE_UNITS.index(j)
                    for i in range(2):
                        if j == ROPE_UNITS[0]:
                            pe.wait_ge(av_made, 2)
                        elif r:
                            pe.wait_ge(rope_s, 2 * r - 1 + i)
                        if j == RV_UNIT + 2:
                            pe.wait_ge(rv_tok, 4)
                        nc.tensor.matmul(AUX[i][:], swap, T4[2 * (j % 2) + i][:], start=True, stop=True).then_inc(sw_ps, 1)
                elif kind == "rv":
                    for i in range(2):
                        n = 2 * (j - RV_UNIT) + i
                        pe.wait_ge(rope_s, 8)
                        if n >= 2:
                            pe.wait_ge(rv_tok, n - 1)
                        for b in range(4):
                            last = nc.tensor.transpose(AUX[i][:, b * P:(b + 1) * P],
                                                       T4[2 * (j % 2) + i][:, b * P:(b + 1) * P], ident)
                        last.then_inc(rv_ps, 1)

            index_jobs = [(b, h) for b in (1, 2, 3) for h in range(8)]

            def index_scores():
                b, h = index_jobs.pop(0)
                n = 8 * (b - 1) + h
                if n == 0:
                    pe.wait_ge(rope_made, 4)
                    pe.wait_ge(kv_made, 2)
                if n >= 2:
                    pe.wait_ge(idx_rel, n - 1)
                lo, w = HD * (h % 2), P * (b + 1)
                nc.tensor.matmul(AUX[2 + n % 2][:, 0:w], IQ[lo:lo + HD, h // 2, b * P:(b + 1) * P],
                                 II[lo:lo + HD, 0:w], start=True, stop=True).then_inc(idx_ps, 1)

            for j in range(L.n):
                unit(L, At(j), H_hi, H_lo, after(h_lo_made, H_BASE[FINAL]) if j == 0 else None,
                     index_scores if 4 <= j <= 6 else None)
                if j == 0:
                    rms_sum(FINAL)
                    pe.wait_ge(ssum2, 7)
                    nc.tensor.matmul(AUX[1][:], ones, SSUM2[:], start=True, stop=True).then_inc(stat2_ready, 1)
                else:
                    post(j - 1)
            post(L.n - 1)

            dsa_bank, dsa_out = (PS[1], AUX[3]), (AUX[1], AUX[2])

            def ret_scores(n):
                h, mb = RET_JOBS[n]
                t, lo = h // 2, HD * (h % 2)
                if n:
                    pe.wait_ge(rd_made, n)
                if n % 8 == 0 and n:
                    pe.wait_ge(rstd, n // 8)
                nc.tensor.matmul(PS[0][:, 0:SEQ - P * mb], RQK[lo:lo + HD, 4 + t, P * mb:P * (mb + 1)],
                                 RQK[lo:lo + HD, t, P * mb:SEQ], start=True, stop=True).then_inc(rs_ps, 1)

            def ret_values(n):
                h, mb = RET_JOBS[n]
                lo = HD * (h % 2)
                pe.wait_ge(rd_made, n + 1)
                if n % 8 == 0 and n:
                    pe.wait_ge(ro1, n // 8)
                nc.tensor.matmul(AUX[0][lo:lo + HD, P * mb:SEQ], RVT[:, mb, HD * h:HD * (h + 1)],
                                 T4[n % 2][:, 0:SEQ - P * mb], start=(mb == 0), stop=(mb == 3)).then_inc(ro_ps, 1)
                if n % 8 < 7:
                    ret_scores(n + 1)

            def dsa_scores(n):
                t, half, b = DSA_JOBS[n]
                lo, w = HD * half, P * (b + 1)
                if n >= 2:
                    pe.wait_ge(a_e, n - 1)
                if n < 4 and b:
                    pe.wait_ge(left_out, b)
                nc.tensor.matmul(dsa_bank[n % 2][:, 0:w], AQ[lo:lo + HD, t, b * P:(b + 1) * P],
                                 KK[lo:lo + HD, 0:w], start=True, stop=False)
                nc.tensor.matmul(dsa_bank[n % 2][:, 0:w], neg_ident[:], LEFT[:, b - 1, 0:w] if b else LEFT0[:],
                                 start=False, stop=True).then_inc(a_s, 1)

            def dsa_values(n):
                t, half, b = DSA_JOBS[n]
                pe.wait_ge(a_pt, n + 1)
                if b == 0 and t:
                    pe.wait_ge(a_norm, 2 * t - 1 + half)
                for c in range(b + 1):
                    last = nc.tensor.matmul(dsa_out[half][:, b * P:(b + 1) * P], AV[:, c, :],
                                            PT2[:, n % 2, c * P:(c + 1) * P], start=(c == 0), stop=(c == b))
                last.then_inc(a_o, 1)

            pe.wait_ge(acc_free, L.base + L.n)
            pe.wait_ge(rope_made, 16)
            pe.wait_ge(rope_s, 16)
            pe.wait_ge(rv_tok, 4)
            pe.wait_ge(mask_made, 2)
            pe.wait_ge(av_ones, 1)
            dsa_scores(0)
            dsa_scores(1)
            ret_scores(0)
            for n, (t, half, b) in enumerate(DSA_JOBS):
                first, second = ret_jobs(n)
                if n + 2 < len(DSA_JOBS):
                    dsa_scores(n + 2)
                if first is not None:
                    ret_values(first)
                pe.wait_ge(a_e, n + 1)
                if n >= 2:
                    pe.wait_ge(a_pt, n - 1)
                for c in range(b + 1):
                    last = nc.tensor.transpose(PS[2 + n % 2][:, c * P:(c + 1) * P], E2[:, n % 2, c * P:(c + 1) * P], ident)
                last.then_inc(a_pt_ps, 1)
                if second is not None:
                    ret_values(second)
                if n:
                    dsa_values(n - 1)
                if n % 8 == 5:
                    pe.wait_ge(r_sq, t + 1)
                    nc.tensor.matmul(PS[0][:], headsum, T4[2][:], start=True, stop=True).then_inc(rsum_ps, 1)
                if n % 8 == 7 and t < 3:
                    ret_scores(n + 1)
            dsa_values(len(DSA_JOBS) - 1)
            linear("wout", ready=lambda k: (m_lo_made, k + 1) if k < 4 else (a_lo_made, k - 3))
            rms_sum(MIX_POST)
            feed_forward(2, FFN_PRE)
            rms_sum(FFN_POST)

        def split_hi(act, L, j):
            u = j.plus(L.base + 2)
            if u.i is None and u.c >= units:
                return
            kt = L.kt if u.i is not None else kts[u.c]
            hi_of(act, u, kt)

        def hi_of(act, u, kt):
            b = u.parity
            n = kt * COLS
            act.wait_ge(raw_in[b], u.half(16, 16))
            if u.i is not None or u.c >= 2:
                act.wait_ge(acc_ready, u.v(2, -2))
            nc.scalar.activation(W_hi[b][:, 0:n], W_raw[b][:, 0:n], ACT.Copy).then_inc(w_hi, 1)

        @block.scalar
        def _(act):
            act.dma_start(cmat[:, 0:2, :], a["cmat"][:, 0:2, :]).then_inc(const_in, 16)
            act.dma_start(onehot[:], a["onehot"]).then_inc(tab_in, 16)
            act.dma_start(table[0:BUCKETS, :], a["rel_bias"]).then_inc(tab_in, 16)
            act.wait_ge(vec_in, 16)
            act.wait_ge(eps_set, 1)

            def h_hi(n, gain, m):
                if n:
                    act.wait_ge(x_ready, m.v(1, X_BASE[n] + 1))
                dst = H_hi[:, bass.ds(m.v(), 1), :].rearrange("p o n -> p (o n)")
                src = X[:, bass.ds(m.v(), 1), :].rearrange("p o n -> p (o n)")
                scale = vec(gain, m) if gain is not None else FG[:, bass.ds(m.v(), 1)]
                nc.scalar.activation(dst, src, ACT.Copy, scale=scale).then_inc(h_hi_made, 1)

            def square(n, m, src=None):
                if src is None:
                    src = X[:, bass.ds(m.v(), 1), :].rearrange("p o n -> p (o n)")
                first = m.i is None and m.c == 0
                i = m.v(1, 7 * n - 2) if m.i is not None or m.c >= 2 else 7 * n
                if i if isinstance(i, int) else True:
                    act.wait_ge(ss_made, i)
                if first and n:
                    act.wait_ge(stat_ready, n)
                if first and n == FFN0:
                    act.wait_ge(ln_sum_ready, 1)
                dst = SSUM[:] if first else SQ[:, m.parity, :]
                nc.scalar.activation(dst, src, ACT.Square).then_inc(sq_made, 1)
                if n == FINAL:
                    dst = SSUM2[:] if first else SQ2[:, m.parity, :]
                    if m.i is not None or m.c >= 3:
                        act.wait_ge(ssum2, m.v(1, -2))
                    nc.scalar.activation(dst, src, ACT.Square, scale=vec("final", m)).then_inc(ssum2_sq, 1)

            def std(n):
                act.wait_ge(stat_ready, n + 1)
                nc.scalar.activation(STD[:], AUX[0][:], ACT.Sqrt, bias=epst[:], scale=1.0 / D_MODEL).then_inc(std_made, 1)

            for m in range(DT):
                if m % 2 == 0:
                    act.wait_ge(x_in[m // 2], 16)
                h_hi(MIX0, "norm_mix0", At(m))
                square(MIX0, At(m))
                if m == 1:
                    hi_of(act, At(0), kts[0])
                if m == 5:
                    hi_of(act, At(1), kts[1])
            act.dma_start(cmat[:, 2:9, :], a["cmat"][:, 2:9, :]).then_inc(const2_in, 16)
            nc.scalar.activation(tap_hi[:], vecs[:, vec_at["w_dw"]:vec_at["w_dw"] + CONV_WIDTH * DT], ACT.Copy).then_inc(w_parts, 1)

            L = layers["pw1"]
            act.wait_ge(eps_set, 1)

            def take_conv(m):
                act.wait_ge(conv_pe, 2 * (m - CONV_DVE + 1) + 1)
                nc.scalar.activation(CV[:, m, :], AUX[1 + m - CONV_DVE][:], ACT.Identity, bias=vec("b_dw", m)).then_inc(conv_pe_taken, 1)

            def conv_hi(p):
                dst, _, row = UPS[p]
                act.wait_ge(glu_made, CONV_DVE + p)
                n = SEQ + CONV_WIDTH - 1
                nc.scalar.activation(dst[:, row, 0:n], U[:, CONV_DVE - 1 + p, 0:n], ACT.Copy).then_inc(u_hi, 1)

            def diagonal_hi(n):
                m, t0, t1 = CONV_CHUNKS[n]
                act.wait_ge(w_parts, 2)
                act.wait_ge(acc_ready, 2 * (L.base + L.n))
                if n >= 2:
                    act.wait_ge(conv_pe, n - 1)
                for t in range(t0, t1):
                    k = TAP_CHUNK * (n % 2) + t - t0
                    w = tap_hi[:, t * DT + m:t * DT + m + 1].bitcast(F32)
                    last = nc.scalar.activation(H_hi[:, k // 4, P * (k % 4):P * (k % 4 + 1)], ident, ACT.Copy, scale=w)
                last.then_inc(diag_hi, 1)

            def glu_step(j):
                if j.i is None and j.c == L.n - 1:
                    act.wait_ge(const2_in, 16)
                    for h in range(12):
                        act.wait_ge(fvec_ps, h + 1)
                        nc.scalar.activation(fvec[:, h, :], AUX[1 + h % 2][:, 0:DIAG], ACT.Copy).then_inc(fvec_made, 1)
                    conv_hi(0)
                    conv_hi(1)
                    diagonal_hi(0)
                else:
                    split_hi(act, L, j)
                if j.i is None and j.c == 0:
                    std(0)
                act.wait_ge(gate_in, j.v(1, 1))
                nc.scalar.activation(T_act[:], T_g[:], ACT.Sigmoid, bias=vec("b_pw1", j.plus(DT))).then_inc(gate_act, 1)
            steps(act, L.n, glu_step, first=1, last=2)
            conv_hi(2)
            act.wait_ge(fvec_made, 12)
            act.dma_start(bias_scratch.rearrange("h p d -> p h d"), fvec[:]).then_inc(scr_out, 16)
            for n, (m, t0, t1) in enumerate(CONV_CHUNKS):
                if n:
                    diagonal_hi(n)
                if n == 0:
                    split_hi(act, L, At(L.n - 1))
                if t0 and m > CONV_DVE:
                    take_conv(m - 1)
            take_conv(DT - 1)
            act.wait_ge(ln_sum_ready, 1)
            nc.scalar.activation(STD[:], AUX[3][:], ACT.Copy, scale=1.0 / D_MODEL).then_inc(mu_made, 1)
            for m in range(DT):
                act.wait_ge(xc_made, m + 1)
                if m >= 2:
                    act.wait_ge(ln_var_ready, m - 1)
                nc.scalar.activation(SQ[:, m % 2, :], CV[:, m, :], ACT.Square).then_inc(xc_sq, 1)
            act.wait_ge(ln_var_ready, DT)
            nc.scalar.activation(STD[:], AUX[2][:], ACT.Sqrt, bias=epst[:], scale=1.0 / D_MODEL).then_inc(ln_std, 1)
            for m in range(DT):
                act.wait_ge(ln_scaled, m + 1)
                nc.scalar.activation(CV[:, m, :], CV[:, m, :], ACT.Silu, bias=vec("ln_b", m), scale=vec("ln_g", m)).then_inc(ln_act, 1)
                act.wait_ge(ln_act, m + 1)
                nc.scalar.activation(HID_hi[:, m, :], CV[:, m, :], ACT.Copy).then_inc(ln_hi_made, 1)

            def add_steps(name, norm=None, gain=None):
                L = layers[name]

                def step(j):
                    split_hi(act, L, j)
                    if norm is None:
                        return
                    for half in range(2):
                        m = At(2 * j.c + half, None if j.i is None else j.i * 2)
                        if norm in H_BASE or norm == FINAL:
                            h_hi(norm, gain, m)
                            square(norm, m)
                        else:
                            act.wait_ge(y_ready, m.v(1, Y_BASE[norm] + 1))
                            square(norm, m, Y[:, bass.ds(m.v(), 1), :].rearrange("p o n -> p (o n)"))
                steps(act, L.n, step, first=1 if norm is not None else 0, last=2)

            def gate_steps(name, norm=None):
                L, q0 = layers[name], gu_base[name]

                def step(j):
                    split_hi(act, L, j)
                    if j.i is None and j.c == 0 and norm is not None:
                        std(norm)
                    act.wait_ge(gate_in, j.v(1, 8 + q0 + 1))
                    nc.scalar.activation(T_act[:], T_g[:], ACT.Silu).then_inc(gate_act, 1)
                    hid_hi(j, q0)
                steps(act, L.n, step, first=1, last=2)

            def hid_hi(j, q0):
                act.wait_ge(hid_made, j.v(1, q0 + 1))
                dst = HID_hi[:, bass.ds(j.v(), 1), :].rearrange("p o n -> p (o n)")
                nc.scalar.activation(dst, T_hid[:], ACT.Copy).then_inc(hid_hi_made, 1)

            add_steps("pw2", FFN0, "norm_ffn0")
            gate_steps("gu0a", norm=FFN0)
            add_steps("dn0a")
            gate_steps("gu0b")
            add_steps("dn0b", MIX1, "norm_mix1")

            L = layers["qkv"]
            for j in range(L.n):
                split_hi(act, L, At(j))
                if j == 0:
                    std(MIX1)
                    act.wait_ge(scr_out, 16)
                    t = bias_scratch.tensor
                    def diagonals(h, rows, n):
                        return bass.AP(t, h * P * DIAG + rows - 1, [[DIAG - 1, rows], [P * DIAG, GROUP_HEADS], [1, n]])
                    act.dma_start(B0[:], diagonals(0, P, 2 * P)).then_inc(bias_in, 16)
                    act.dma_start(B1[:], diagonals(4, P, P)).then_inc(bias_in, 16)
                    act.wait_ge(b2_set, 1)
                    for r in range(4):
                        act.dma_start(B2[32 * r:32 * r + 32, :, 32 * r:32 * r + 32], diagonals(8, 32, 32)).then_inc(bias_in, 16)
            for t in range(6):
                act.wait_ge(v_t, t + 1)
                nc.scalar.activation(VT[:, t, :, :].rearrange("p b n -> p (b n)"), AUX[t % 4][:], ACT.Copy).then_inc(v_tok, 1)
            def dilated_exp(n):
                h, blks = JOBS[n]
                act.wait_ge(nm_made, n + 1)
                if n >= 2:
                    act.wait_ge(pt_ps, n - 1)
                for i, (blk, c, w, keys) in enumerate(blks):
                    last = nc.scalar.activation(E1[:, n % 2, c:c + w], L1[:, n % 2, c:c + w], ACT.Exp,
                                                bias=NM[:, n % 2, i:i + 1], accum_out=MD[:, 1, blk, h:h + 1])
                last.then_inc(e_made, 1)

            def take_rows(g):
                for kind, dst in enumerate((ROW_w, ROW_den)):
                    i = 2 * g + kind
                    act.wait_ge(st_ps, i + 1)
                    nc.scalar.activation(unpermuted(dst[:, g, :], g), blocked(PS[6 + i % 2][0:GROUP_HEADS, :], g),
                                         ACT.Copy).then_inc(row_made, 1)

            dilated_exp(0)
            for n, (h, blks) in enumerate(JOBS):
                if n + 1 < len(JOBS):
                    dilated_exp(n + 1)
                act.wait_ge(pt_ps, n + 1)
                if n >= 2:
                    act.wait_ge(pv_done, n - 1)
                w = P * sum(len(keys) for _, _, _, keys in blks)
                nc.scalar.activation(PT1[:, n % 2, 0:w], PS[2 + n % 2][:, 0:w], ACT.Copy).then_inc(pt_made, 1)
                if n in GROUP_ENDS:
                    take_rows(GROUP_ENDS.index(n))
            take_rows(2)
            act.wait_ge(rowd, 1)
            nc.scalar.activation(ROW_w[:], ROW_w[:], ACT.Exp).then_inc(roww, 1)
            for t in range(6):
                act.wait_ge(o_made, t + 1)
                nc.scalar.activation(HID_hi[:, t, :], T4[t % 2][:], ACT.Copy).then_inc(o_hi_made, 1)

            add_steps("wo", FFN1, "norm_ffn1")
            gate_steps("gu1a", norm=FFN1)
            add_steps("dn1a")
            gate_steps("gu1b")
            act.wait_ge(fg_made, 1)
            add_steps("dn1b", FINAL)

            L = layers["inp"]

            def index_relu(b):
                w = P * (b + 1)
                for h in range(8):
                    n = 8 * (b - 1) + h
                    act.wait_ge(idx_ps, n + 1)
                    if n >= 2:
                        act.wait_ge(isc_made, n - 1)
                    nc.scalar.activation(SQ[:, n % 2, 0:w], AUX[2 + n % 2][:, 0:w], ACT.Relu).then_inc(idx_rel, 1)

            def post(j):
                kind = INP_KINDS[j]
                if kind == "rv":
                    for i in range(2):
                        n = 2 * (j - RV_UNIT) + i
                        act.wait_ge(rv_ps, n + 1)
                        dst = RVT[:, :, n * P:(n + 1) * P]
                        nc.scalar.activation(dst, AUX[i][:].rearrange("p (b n) -> p b n", b=4), ACT.Copy).then_inc(rv_tok, 1)
                elif kind == "rg":
                    for i in range(2):
                        act.wait_ge(rt_made, 2 * j + 1 + i)
                        nc.scalar.activation(GS[:, 2 * (j - RG_UNIT) + i, :], T4[2 * (j % 2) + i][:], ACT.Silu).then_inc(rg_made, 1)

            for j in range(L.n):
                if 4 <= j <= 6:
                    index_relu(j - 3)
                split_hi(act, L, At(j))
                if j == 0:
                    std(FINAL)
                    act.wait_ge(rf_scaled, 1)
                    nc.scalar.activation(STD[:], T_u[:], ACT.Sqrt, bias=epst[:], scale=1.0 / D_MODEL).then_inc(std2_made, 1)
                    act.dma_start(CS[:], a["rotary"]).then_inc(cs_in, 16)
                else:
                    post(j - 1)
            post(L.n - 1)
            act.wait_ge(isc_made, 24)
            for h in range(2):
                act.dma_start(SQ[:, h, :], a["decay"][h]).then_inc(d_in[h], 16)

            dsa_bank = (PS[1], AUX[3])

            def dsa_exp(n):
                w = P * (DSA_JOBS[n][2] + 1)
                act.wait_ge(a_nm, n + 1)
                if n >= 2:
                    act.wait_ge(a_pt_ps, n - 1)
                nc.scalar.activation(E2[:, n % 2, 0:w], dsa_bank[n % 2][:, 0:w], ACT.Exp, scale=HD ** -0.5,
                                     bias=NEGMAX[:, n % 2:n % 2 + 1]).then_inc(a_e, 1)

            def dsa_hi(t):
                act.wait_ge(a_norm, 2 * t + 2)
                nc.scalar.activation(H_hi[:, 4 + t, :], SSUM[:], ACT.Copy).then_inc(a_hi_made, 1)

            def ret_hi(t):
                act.wait_ge(ro2, t + 1)
                nc.scalar.activation(H_hi[:, t, :], T4[3][:], ACT.Copy).then_inc(m_hi_made, 1)

            def next_decay(h):
                act.wait_ge(rd_made, 4 * (h - 1))
                act.dma_start(SQ[:, h % 2, :], a["decay"][h]).then_inc(d_in[h % 2], 16)

            dsa_exp(0)
            for n, (t, half, b) in enumerate(DSA_JOBS):
                w = P * (b + 1)
                if n % 8 == 6:
                    act.wait_ge(rsum_ps, t + 1)
                    nc.scalar.activation(STD[:], PS[0][:], ACT.Sqrt, bias=epst[:], scale=1.0 / HD).then_inc(rstd, 1)
                if n + 1 < len(DSA_JOBS):
                    dsa_exp(n + 1)
                act.wait_ge(a_pt_ps, n + 1)
                if n >= 2:
                    act.wait_ge(a_o, n - 1)
                nc.scalar.activation(PT2[:, n % 2, 0:w], PS[2 + n % 2][:, 0:w], ACT.Copy).then_inc(a_pt, 1)
                if n % 8 == 4:
                    act.wait_ge(ro_ps, 8 * t + 8)
                    nc.scalar.activation(T4[2][:], AUX[0][:], ACT.Square).then_inc(r_sq, 1)
                if t < 3 and n % 8 == 3:
                    next_decay(2 * t + 2)
                if t < 3 and n % 8 == 5:
                    next_decay(2 * t + 3)
                if n % 8 == 0 and t:
                    ret_hi(t - 1)
                if n % 8 == 5 and t:
                    dsa_hi(t - 1)
            ret_hi(3)
            dsa_hi(3)

            add_steps("wout", MIX_POST)
            std(MIX_POST)
            for m in range(DT):
                h_hi(FFN_PRE, "ffn_pre", At(m))
                square(FFN_PRE, At(m))

            def conv_gate_steps(name, j0, norm=None):
                L, q0 = layers[name], gu_base[name]

                def step(j):
                    split_hi(act, L, j)
                    if j.i is None and j.c == 0 and norm is not None:
                        std(norm)
                    q = q0 - 44
                    for i, y in enumerate((T_g, T_u)):
                        act.wait_ge(g3_in, j.v(2, 2 * q + 1 + i))
                        nc.scalar.activation(y[:], GP[:, i, 2:SEQ + 2], ACT.Identity, scale=vec("conv3_w", j.plus(88 + 22 * i + j0)),
                                             bias=vec("conv3_b", j.plus(22 * i + j0))).then_inc(c3_y, 1)
                    act.wait_ge(gate_in, j.v(1, 8 + q0 + 1))
                    nc.scalar.activation(T_act[:], T_g[:], ACT.Silu).then_inc(gate_act, 1)
                    hid_hi(j, q0)
                steps(act, L.n, step, first=1, last=2)

            conv_gate_steps("gu2a", 0, norm=FFN_PRE)
            add_steps("dn2a")
            conv_gate_steps("gu2b", 11)
            add_steps("dn2b", FFN_POST)
            std(FFN_POST)

        @block.gpsimd
        def _(pool):
            nc.gpsimd.memset(epst[:], EPS).then_inc(eps_set, 1)
            nc.gpsimd.memset(U[:, :, 0:CONV_WIDTH - 1], 0.0).then_inc(pads_set, 1)
            pool.wait_ge(pads_set, 1)
            nc.gpsimd.memset(table[BUCKETS:BUCKETS + 1, :], NEG).then_inc(tab_pad, 1)

            def lo_of(u, kt):
                b = u.parity
                n = kt * COLS
                pool.wait_ge(w_hi, u.v(1, 1))
                nc.gpsimd.tensor_tensor(W_lo[b][:, 0:n], W_raw[b][:, 0:n], W_hi[b][:, 0:n].bitcast(F32),
                                        ALU.subtract).then_inc(w_lo, 1)

            def split_lo(L, j):
                u = j.plus(L.base + 2)
                if u.i is None and u.c >= units:
                    return
                lo_of(u, L.kt if u.i is not None else kts[u.c])

            def add_square(n, m):
                if m.i is None and m.c == 0:
                    return
                pool.wait_ge(sq_made, m.v(1, 8 * n + 1))
                if m.i is not None or m.c >= 2:
                    pool.wait_ge(ss_made, m.v(1, 7 * n - 1))
                nc.gpsimd.tensor_tensor(SSUM[:], SSUM[:], SQ[:, m.parity, :], ALU.add).then_inc(ss_made, 1)
                if n == FINAL:
                    pool.wait_ge(ssum2_sq, m.v(1, 1))
                    if m.i is not None or m.c >= 2:
                        pool.wait_ge(ssum2, m.v(1, -1))
                    nc.gpsimd.tensor_tensor(SSUM2[:], SSUM2[:], SQ2[:, m.parity, :], ALU.add).then_inc(ssum2, 1)

            pool.wait_ge(tab_pad, 1)
            add_square(MIX0, At(1))
            lo_of(At(0), kts[0])
            for m in range(2, DT):
                add_square(MIX0, At(m))
            lo_of(At(1), kts[1])
            L = layers["pw1"]

            def diagonal_lo(n):
                m, t0, t1 = CONV_CHUNKS[n]
                pool.wait_ge(acc_ready, 2 * (L.base + L.n))
                pool.wait_ge(const2_in, 16)
                pool.wait_ge(w_parts, 2)
                if n >= 2:
                    pool.wait_ge(conv_pe, n - 1)
                k = TAP_CHUNK * (n % 2) // 4
                dst = H_lo[:, k:k + TAP_CHUNK // 4, :].rearrange("p a (b n) -> p (a b) n", n=P)[:, 0:t1 - t0]
                w = tap_lo[:].rearrange("p (t m) -> p t m", m=DT)[:, t0:t1, m:m + 1].bitcast(F32)
                nc.gpsimd.tensor_tensor(dst, ident.unsqueeze(1).to_broadcast([P, t1 - t0, P]),
                                        w.to_broadcast([P, t1 - t0, P]), ALU.mult).then_inc(diag_lo, 1)

            steps(pool, L.n - 1, lambda j: split_lo(L, j))
            diagonal_lo(0)
            split_lo(L, At(L.n - 1))
            for n in range(1, len(CONV_CHUNKS)):
                diagonal_lo(n)
            pool.wait_ge(stat_ready, 1)
            for m in range(CONV_DVE - 1):
                pool.wait_ge(conv_made, m + 1)
                if m == 0:
                    nc.gpsimd.tensor_copy(SSUM[:], CV[:, 0, :]).then_inc(ln_sum, 1)
                else:
                    pool.wait_ge(ln_sum, m)
                    nc.gpsimd.tensor_tensor(SSUM[:], SSUM[:], CV[:, m, :], ALU.add).then_inc(ln_sum, 1)

            def add_steps(name, norm=None):
                L = layers[name]

                def step(j):
                    split_lo(L, j)
                    if norm is not None:
                        add_square(norm, At(2 * j.c, None if j.i is None else j.i * 2))
                        add_square(norm, At(2 * j.c + 1, None if j.i is None else j.i * 2))
                steps(pool, L.n, step, first=1 if norm is not None else 0, last=2)

            def gate_steps(name):
                L = layers[name]
                steps(pool, L.n, lambda j: split_lo(L, j), last=2)

            add_steps("pw2", FFN0)
            gate_steps("gu0a")
            add_steps("dn0a")
            gate_steps("gu0b")
            add_steps("dn0b", MIX1)
            L = layers["qkv"]
            for j in range(L.n):
                split_lo(L, At(j))
                if j == 0:
                    nc.gpsimd.memset(B2[:], NEG).then_inc(b2_set, 1)
            add_steps("wo", FFN1)
            gate_steps("gu1a")
            add_steps("dn1a")
            gate_steps("gu1b")
            add_steps("dn1b", FINAL)

            L = layers["inp"]

            def rope(j):
                r = ROPE_UNITS.index(j)
                dst = {"iq": IQ, "rq": RQK, "rk": RQK, "aq": AQ}[INP_KINDS[j]]
                m0 = 4 * (INP_KINDS[j] == "rk") + 2 * (INP_KINDS[j - 1] == INP_KINDS[j])
                if j == 1:
                    pool.wait_ge(cs_in, 16)
                for i in range(2):
                    pool.wait_ge(rt_made, 2 * j + 1 + i)
                    nc.gpsimd.tensor_tensor(dst[:, m0 + i, :], T4[2 * (j % 2) + i][:], CS[:, 0, :],
                                            ALU.mult).then_inc(rope_c, 1)
                for i in range(2):
                    pool.wait_ge(rope_s, 2 * r + 1 + i)
                    pool.wait_ge(rope_c, 2 * r + 1 + i)
                    nc.gpsimd.tensor_tensor(dst[:, m0 + i, :], dst[:, m0 + i, :], T4[2 * (j % 2) + i][:],
                                            ALU.add).then_inc(rope_made, 1)

            for j in range(L.n):
                split_lo(L, At(j))
                if j - 1 in ROPE_UNITS:
                    rope(j - 1)
            def gated(t):
                pool.wait_ge(ro1, t + 1)
                pool.wait_ge(rg_made, 4)
                nc.gpsimd.tensor_tensor(T4[3][:], T4[3][:], GS[:, t, :], ALU.mult).then_inc(ro2, 1)

            def gated_lo(t):
                pool.wait_ge(m_hi_made, t + 1)
                nc.gpsimd.tensor_tensor(H_lo[:, t, :], T4[3][:], H_hi[:, t, :].bitcast(F32),
                                        ALU.subtract).then_inc(m_lo_made, 1)

            def dsa_lo(t):
                pool.wait_ge(a_hi_made, t + 1)
                nc.gpsimd.tensor_tensor(H_lo[:, 4 + t, :], SSUM[:], H_hi[:, 4 + t, :].bitcast(F32),
                                        ALU.subtract).then_inc(a_lo_made, 1)

            for t in range(4):
                if t:
                    gated_lo(t - 1)
                    dsa_lo(t - 1)
                gated(t)
            gated_lo(3)
            dsa_lo(3)
            add_steps("wout", MIX_POST)
            for m in range(DT):
                pool.wait_ge(f_applied, m + 1)
                nc.gpsimd.tensor_tensor(X[:, m, :], X[:, m, :], T4[m % 2][:], ALU.add).then_inc(x_ready, 1)
                if m:
                    add_square(FFN_PRE, At(m - 1))
            add_square(FFN_PRE, At(DT - 1))
            nc.gpsimd.memset(GP[:, :, 0:2], 0.0).then_inc(pad3_set, 1)
            gate_steps("gu2a")
            add_steps("dn2a")
            gate_steps("gu2b")
            add_steps("dn2b", FFN_POST)

        @block.vector
        def _(dve):
            dve.wait_ge(vec_in, 16)
            def h_lo(n, gain, m):
                dve.wait_ge(h_hi_made, m.v(1, H_BASE[n] + 1))
                dst = H_lo[:, bass.ds(m.v(), 1), :].rearrange("p o n -> p (o n)")
                hi = H_hi[:, bass.ds(m.v(), 1), :].rearrange("p o n -> p (o n)").bitcast(F32)
                src = X[:, bass.ds(m.v(), 1), :].rearrange("p o n -> p (o n)")
                scale = vec(gain, m) if gain is not None else FG[:, bass.ds(m.v(), 1)]
                nc.vector.scalar_tensor_tensor(out=dst, in0=src, scalar=scale, in1=hi, op0=ALU.mult,
                                               op1=ALU.subtract).then_inc(h_lo_made, 1)

            def rms(n):
                dve.wait_ge(std_made, n + 1)
                nc.vector.reciprocal(R[:], STD[:]).then_inc(r_made, 1)
                dve.wait_ge(r_made, n + 1)

            for m in range(DT):
                h_lo(0, "norm_mix0", At(m))

            L = layers["pw1"]
            HALO = CONV_WIDTH - 1

            todo = [(m, t) for m in range(CONV_DVE) for t in range(CONV_WIDTH if m < CONV_DVE - 1 else CONV_SPLIT)]

            def conv(count, upto):
                while count and todo and todo[0][0] < upto:
                    m, t = todo.pop(0)
                    n = CONV_WIDTH * m + t
                    dst = (CV[:, m, :], CVacc[:])[t % 2]
                    w = vec("w_dw", t * DT + m)
                    src = U[:, m, t:t + SEQ]
                    if n >= 2 and t != 0:
                        dve.wait_ge(conv_step, n - 1)
                    if t == 0:
                        i = nc.vector.tensor_scalar(dst, src, w, vec("b_dw", m), ALU.mult, ALU.add)
                    elif t == 1:
                        i = nc.vector.tensor_scalar(dst, src, w, None, ALU.mult)
                    else:
                        i = nc.vector.scalar_tensor_tensor(out=dst, in0=src, scalar=w, in1=dst, op0=ALU.mult, op1=ALU.add)
                    i.then_inc(conv_step, 1)
                    count -= 1
                    if not todo:
                        dve.wait_ge(conv_step, n + 1)
                        nc.vector.tensor_tensor(CV[:, m, :], CV[:, m, :], CVacc[:], ALU.add).then_inc(conv_step, 1)
                        dve.wait_ge(conv_step, n + 2)
                        dve.wait_ge(conv_pe, 1)
                        nc.vector.tensor_tensor(CV[:, m, :], CV[:, m, :], AUX[0][:], ALU.add).then_inc(conv_made, 1)
                        dve.wait_ge(conv_made, m + 1)
                    elif t == CONV_WIDTH - 1:
                        dve.wait_ge(conv_step, n + 1)
                        nc.vector.tensor_tensor(CV[:, m, :], CV[:, m, :], CVacc[:], ALU.add).then_inc(conv_made, 1)
                        dve.wait_ge(conv_made, m + 1)

            def conv_lo(p):
                hi, lo, row = UPS[p]
                dve.wait_ge(u_hi, p + 1)
                n = SEQ + CONV_WIDTH - 1
                nc.vector.tensor_tensor(lo[:, row, 0:n], U[:, CONV_DVE - 1 + p, 0:n], hi[:, row, 0:n].bitcast(F32),
                                        ALU.subtract).then_inc(u_lo, 1)

            dve.wait_ge(tab_in, 32)
            dve.wait_ge(tab_pad, 1)
            nc.vector.tensor_copy(table_wide[:], table[:].unsqueeze(2).to_broadcast([BUCKETS + 1, 12, P])).then_inc(tab_wide, 1)

            dve.wait_ge(w_parts, 1)
            nc.vector.tensor_tensor(tap_lo[:], vecs[:, vec_at["w_dw"]:vec_at["w_dw"] + CONV_WIDTH * DT],
                                    tap_hi[:].bitcast(F32), ALU.subtract).then_inc(w_parts, 1)
            nc.vector.tensor_tensor(FG[:], vecs[:, vec_at["final"]:vec_at["final"] + DT],
                                    vecs[:, vec_at["mix_pre"]:vec_at["mix_pre"] + DT], ALU.mult).then_inc(fg_made, 1)
            dve.wait_ge(pads_set, 1)
            for j in range(L.n):
                u = At(L.base + j)
                if j == 0:
                    rms(0)
                dve.wait_ge(acc_ready, u.v(2, 2))
                b = u.parity
                if j:
                    dve.wait_ge(gate_act, j)
                nc.vector.tensor_tensor(T_g[:], PS[2 * b + 1][:], R[:], ALU.mult).then_inc(gate_in, 1)
                if j:
                    dve.wait_ge(glu_made, j)
                nc.vector.tensor_tensor(T_u[:], PS[2 * b][:], R[:], ALU.mult).then_inc(acc_free, 1)
                dve.wait_ge(gate_act, j + 1)
                dve.wait_ge(acc_free, j + 1)
                nc.vector.scalar_tensor_tensor(out=U[:, j, HALO:HALO + SEQ], in0=T_u[:], scalar=vec("b_pw1", j),
                                               in1=T_act[:], op0=ALU.add, op1=ALU.mult).then_inc(glu_made, 1)
                if j < L.n - 1:
                    conv(TAPS_PER_UNIT, j)
                if j == L.n - 2:
                    conv(13, j)
                    conv_lo(0)
                    conv_lo(1)
                    conv(7, j)
            dve.wait_ge(glu_made, L.n)
            conv_lo(2)
            conv(len(todo), DT)
            dve.wait_ge(mu_made, 1)
            for m in range(DT):
                nc.vector.tensor_tensor(CV[:, m, :], CV[:, m, :], STD[:], ALU.subtract).then_inc(xc_made, 1)
            dve.wait_ge(ln_std, 1)
            nc.vector.reciprocal(T_g[:], STD[:]).then_inc(ln_r, 1)
            dve.wait_ge(ln_r, 1)
            for m in range(DT):
                nc.vector.tensor_tensor(CV[:, m, :], CV[:, m, :], T_g[:], ALU.mult).then_inc(ln_scaled, 1)
            dve.wait_ge(scr_out, 16)
            for m in range(DT):
                dve.wait_ge(ln_hi_made, m + 1)
                nc.vector.tensor_tensor(HID_lo[:, m, :], CV[:, m, :], HID_hi[:, m, :].bitcast(F32),
                                        ALU.subtract).then_inc(ln_lo_made, 1)

            def add_steps(name, x0, norm=None, gain=None, bias=None):
                L = layers[name]

                def step(j):
                    u = j.plus(L.base)
                    b = u.parity
                    for half in range(2):
                        m = At(2 * j.c + half, None if j.i is None else j.i * 2)
                        dve.wait_ge(acc_ready, u.v(2, half + 1))
                        x = X[:, bass.ds(m.v(), 1), :].rearrange("p o n -> p (o n)")
                        if bias is None:
                            i = nc.vector.tensor_tensor(x, x, PS[2 * b + half][:], ALU.add)
                        else:
                            i = nc.vector.scalar_tensor_tensor(out=x, in0=PS[2 * b + half][:], scalar=vec(bias, m),
                                                               in1=x, op0=ALU.add, op1=ALU.add)
                        i.then_inc(x_ready, 1) if x0 is not None else i.then_inc(x_half, 1)
                    if x0 is not None:
                        dve.wait_ge(x_ready, j.v(2, x0 + 2))
                    else:
                        dve.wait_ge(x_half, j.v(2, (0 if name == "dn0a" else 8) + 2))
                    nc.vector.sem_inc(acc_free, 1)
                    if norm is not None:
                        for half in range(2):
                            h_lo(norm, gain, At(2 * j.c + half, None if j.i is None else j.i * 2))
                steps(dve, L.n, step)

            def gate_steps(name, norm=None):
                L, q0 = layers[name], gu_base[name]

                def step(j):
                    u = j.plus(L.base)
                    b = u.parity
                    if j.i is None and j.c == 0 and norm is not None:
                        rms(norm)
                    dve.wait_ge(acc_ready, u.v(2, 1))
                    nc.vector.tensor_tensor(T_g[:], PS[2 * b][:], R[:], ALU.mult).then_inc(gate_in, 1)
                    dve.wait_ge(acc_ready, u.v(2, 2))
                    nc.vector.tensor_tensor(T_u[:], PS[2 * b + 1][:], R[:], ALU.mult).then_inc(acc_free, 1)
                    dve.wait_ge(acc_free, u.v(1, 1))
                    hidden(j, q0)
                steps(dve, L.n, step, first=1)

            def hidden(j, q0):
                dve.wait_ge(gate_act, j.v(1, 8 + q0 + 1))
                nc.vector.tensor_tensor(T_hid[:], T_u[:], T_act[:], ALU.mult).then_inc(hid_made, 1)
                dve.wait_ge(hid_hi_made, j.v(1, q0 + 1))
                k = bass.ds(j.v(), 1)
                hi = HID_hi[:, k, :].rearrange("p o n -> p (o n)").bitcast(F32)
                nc.vector.tensor_tensor(HID_lo[:, k, :].rearrange("p o n -> p (o n)"), T_hid[:], hi,
                                        ALU.subtract).then_inc(hid_lo_made, 1)
                dve.wait_ge(hid_lo_made, j.v(1, q0 + 1))

            add_steps("pw2", 0, FFN0, "norm_ffn0", bias="b_pw2")
            gate_steps("gu0a", norm=FFN0)
            add_steps("dn0a", None)
            gate_steps("gu0b")
            add_steps("dn0b", 8, MIX1, "norm_mix1")

            def take_pair(t):
                dve.wait_ge(pv_done, 1 + max(n for n, (h, _) in enumerate(JOBS) if h == 2 * t + 1))
                g = t // 2
                nc.vector.tensor_copy(unpermuted(OU[:, t, :], g), blocked(PS[4 + t % 2][:], g)).then_inc(ou_made, 1)

            L = layers["qkv"]
            rms(MIX1)
            for j in range(L.n):
                u = At(L.base + j)
                for half in range(2):
                    dve.wait_ge(acc_ready, u.v(2, 1 + half))
                    m = 2 * j + half
                    g = m % 6 // 2
                    nc.vector.tensor_tensor(permuted(VQK[:, m, :], g), by_step(PS[2 * u.parity + half][:], g),
                                            by_step(R[:], g), ALU.mult).then_inc(qkv_made, 1)
                dve.wait_ge(qkv_made, 2 * j + 2)
                nc.vector.sem_inc(acc_free, 1)
            dve.wait_ge(bias_in, 96)
            for n, (h, blks) in enumerate(JOBS):
                g, hh = h // GROUP_HEADS, h % GROUP_HEADS
                dve.wait_ge(s_made, n + 1)
                if n >= 2:
                    dve.wait_ge(e_made, n - 1)
                for blk, c, w, keys in blks if g == 0 else []:
                    bias = B0[:, hh, 256 - w:256]
                    last = nc.vector.scalar_tensor_tensor(out=L1[:, n % 2, c:c + w], in0=PS[n % 2][:, c:c + w],
                                                          scalar=HD ** -0.5, in1=bias, op0=ALU.mult, op1=ALU.add)
                by_block = L1[:, n % 2, :].rearrange("p (b n) -> p b n", b=4)
                if g:
                    bias = (B1, B2)[g - 1][:, hh:hh + 1, :].to_broadcast([P, 4, P])
                    last = nc.vector.scalar_tensor_tensor(out=by_block, in0=PS[n % 2][:].rearrange("p (b n) -> p b n", b=4),
                                                          scalar=HD ** -0.5, in1=bias, op0=ALU.mult, op1=ALU.add)
                last.then_inc(l_made, 1)
                dve.wait_ge(l_made, n + 1)
                if g:
                    last = nc.vector.reduce_max(MD[:, 0, :, h:h + 1].rearrange("p b o -> p (b o)"), by_block, AX.X)
                for blk, c, w, keys in blks if g == 0 else []:
                    last = nc.vector.reduce_max(MD[:, 0, blk, h:h + 1], L1[:, n % 2, c:c + w], AX.X)
                last.then_inc(m_made, 1)
                dve.wait_ge(m_made, n + 1)
                b0, nb = blks[0][0], len(blks)
                nc.vector.tensor_scalar(NM[:, n % 2, 0:nb], MD[:, 0, b0:b0 + nb, h:h + 1].rearrange("p b o -> p (b o)"),
                                        -1.0, None, ALU.mult).then_inc(nm_made, 1)
                if n >= 2:
                    hp, bp = JOBS[n - 2]
                    if hp % 2 == 1 and bp[-1][0] == 3:
                        take_pair(hp // 2)
                if n == len(JOBS) - 1:
                    dve.wait_ge(row_made, 4)
                    nc.vector.tensor_tensor(ROW_max[:], ROW_w[:, 0, :], ROW_w[:, 1, :], ALU.max).then_inc(rowmax, 1)
            take_pair(5)
            dve.wait_ge(row_made, 5)
            dve.wait_ge(rowmax, 1)
            nc.vector.tensor_tensor(ROW_max[:], ROW_max[:], ROW_w[:, 2, :], ALU.max).then_inc(rowmax, 1)
            dve.wait_ge(rowmax, 2)
            for g in range(3):
                last = nc.vector.tensor_tensor(ROW_w[:, g, :], ROW_w[:, g, :], ROW_max[:], ALU.subtract)
            last.then_inc(rowd, 1)
            dve.wait_ge(roww, 1)
            dve.wait_ge(row_made, 6)
            nc.vector.tensor_tensor(ROW_den[:], ROW_den[:], ROW_w[:], ALU.mult).then_inc(rowwd, 1)
            dve.wait_ge(rowwd, 1)
            nc.vector.tensor_tensor(ROW_sum[:], ROW_den[:, 0, :], ROW_den[:, 1, :], ALU.add).then_inc(rows_, 1)
            dve.wait_ge(rows_, 1)
            nc.vector.tensor_tensor(ROW_sum[:], ROW_sum[:], ROW_den[:, 2, :], ALU.add).then_inc(rows_, 1)
            dve.wait_ge(rows_, 2)
            nc.vector.reciprocal(ROW_max[:], ROW_sum[:]).then_inc(rows_, 1)
            dve.wait_ge(rows_, 3)
            for g in range(3):
                last = nc.vector.tensor_tensor(ROW_w[:, g, :], ROW_w[:, g, :], ROW_max[:], ALU.mult)
            last.then_inc(rowf, 1)
            def weighted(t):
                dve.wait_ge(f_ps, t + 1)
                nc.vector.tensor_tensor(T4[t % 2][:], OU[:, t, :], PS[6 + t % 2][:], ALU.mult).then_inc(o_made, 1)

            weighted(0)
            for t in range(6):
                if t < 5:
                    weighted(t + 1)
                dve.wait_ge(o_hi_made, t + 1)
                nc.vector.tensor_tensor(HID_lo[:, t, :], T4[t % 2][:], HID_hi[:, t, :].bitcast(F32),
                                        ALU.subtract).then_inc(o_lo_made, 1)
                dve.wait_ge(o_lo_made, t + 1)

            add_steps("wo", 16, FFN1, "norm_ffn1")
            gate_steps("gu1a", norm=FFN1)
            add_steps("dn1a", None)
            gate_steps("gu1b")
            dve.wait_ge(fg_made, 1)
            add_steps("dn1b", 24, FINAL)

            L = layers["inp"]

            def post(j):
                if INP_KINDS[j] == "kv":
                    dve.wait_ge(cs_in, 16)
                    for i, dst in enumerate((KK, II)):
                        dve.wait_ge(kv_ps, 2 * i + 1)
                        nc.vector.tensor_tensor(dst[:], AUX[2 * i][:], CS[:, 0, :], ALU.mult).then_inc(kv_c, 1)
                        dve.wait_ge(kv_ps, 2 * i + 2)
                        nc.vector.tensor_tensor(L2k[i], AUX[2 * i + 1][:], CS[:, 1, :], ALU.mult).then_inc(kv_s, 1)
                        dve.wait_ge(kv_s, i + 1)
                        dve.wait_ge(kv_c, i + 1)
                        nc.vector.tensor_tensor(dst[:], dst[:], L2k[i], ALU.add).then_inc(kv_made, 1)
                    dve.wait_ge(tr_ps, 1)
                    nc.vector.memset(AV[:, :, HD:P], 1.0).then_inc(av_ones, 1)
                    nc.vector.tensor_copy(AV[:, :, 0:HD], AUX[0][:].rearrange("p (b n) -> p b n", b=4)[:, :, HD:2 * HD]).then_inc(av_made, 1)
                    dve.wait_ge(tr_ps, 2)
                    nc.vector.tensor_scalar(IW[:], AUX[1][:].rearrange("p (b n) -> p b n", b=4)[:, :, HD:HD + 8],
                                            8.0 ** -0.5 * HD ** -0.5, None, ALU.mult).then_inc(av_made, 1)
                elif j in ROPE_UNITS:
                    r = ROPE_UNITS.index(j)
                    for i in range(2):
                        dve.wait_ge(sw_ps, 2 * r + 1 + i)
                        dve.wait_ge(rope_c, 2 * r + 1 + i)
                        nc.vector.tensor_tensor(T4[2 * (j % 2) + i][:], AUX[i][:], CS[:, 1, :], ALU.mult).then_inc(rope_s, 1)

            def index_sum(b):
                w = P * (b + 1)
                if b == 1:
                    dve.wait_ge(av_made, 2)
                for h in range(8):
                    n = 8 * (b - 1) + h
                    dve.wait_ge(idx_rel, n + 1)
                    dst = ISC[:, b - 1, 0:w]
                    if h == 0:
                        i = nc.vector.tensor_scalar(dst, SQ[:, n % 2, 0:w], IW[:, b, h:h + 1], None, ALU.mult)
                    else:
                        dve.wait_ge(isc_made, n)
                        i = nc.vector.scalar_tensor_tensor(out=dst, in0=SQ[:, n % 2, 0:w], scalar=IW[:, b, h:h + 1],
                                                           in1=dst, op0=ALU.mult, op1=ALU.add)
                    i.then_inc(isc_made, 1)
                dve.wait_ge(isc_made, 8 * b)
                dst = ISC[:, b - 1, b * P:(b + 1) * P]
                nc.vector.scalar_tensor_tensor(out=dst, in0=later, scalar=-3.0e38, in1=dst, op0=ALU.mult,
                                               op1=ALU.add).then_inc(isc_mask, 1)

            rounds = [(b, i) for b in (1, 2, 3) for i in range(TOPK // 8)]

            def choose(count):
                for _ in range(count):
                    b, i = rounds.pop(0)
                    n = (b - 1) * (TOPK // 8) + i
                    w = P * (b + 1)
                    src = ISC[:, b - 1, 0:w] if i == 0 else WK[:, 0:w]
                    if i == 0:
                        dve.wait_ge(isc_mask, b)
                        if b > 1:
                            dve.wait_ge(left_out, b - 1)
                    if n:
                        dve.wait_ge(top_rep, n)
                    nc.vector.max(TOP8[:], src).then_inc(top_max, 1)
                    dve.wait_ge(top_max, n + 1)
                    nc.vector.match_replace(WK[:, 0:w], TOP8[:], src, -3.4e38).then_inc(top_rep, 1)
                    if i == TOPK // 8 - 1:
                        dve.wait_ge(top_rep, n + 1)
                        nc.vector.tensor_tensor(LEFT[:, b - 1, 0:w], ISC[:, b - 1, 0:w], WK[:, 0:w],
                                                ALU.is_equal).then_inc(left_out, 1)

            for j in range(L.n):
                u = At(L.base + j)
                if j == 0:
                    dve.wait_ge(std_made, FINAL + 1)
                    nc.vector.reciprocal(RF[:], STD[:]).then_inc(r_made, 1)
                    dve.wait_ge(r_made, FINAL + 1)
                    nc.vector.tensor_tensor(T_g[:], RF[:], RF[:], ALU.mult).then_inc(rf_sq, 1)
                    dve.wait_ge(rf_sq, 1)
                    dve.wait_ge(stat2_ready, 1)
                    nc.vector.tensor_tensor(T_u[:], T_g[:], AUX[1][:], ALU.mult).then_inc(rf_scaled, 1)
                    dve.wait_ge(std2_made, 1)
                    nc.vector.reciprocal(T_g[:], STD[:]).then_inc(r_pair, 1)
                    dve.wait_ge(r_pair, 1)
                    nc.vector.tensor_tensor(R[:], T_g[:], RF[:], ALU.mult).then_inc(r_pair, 1)
                    dve.wait_ge(r_pair, 2)
                if 4 <= j <= 6:
                    index_sum(j - 3)
                if j >= 2:
                    k = INP_KINDS[j - 2]
                    if k == "kv":
                        dve.wait_ge(tr_ps, 2)
                    elif j - 2 in ROPE_UNITS:
                        dve.wait_ge(rope_made, 2 * ROPE_UNITS.index(j - 2) + 2)
                    elif k == "rv":
                        dve.wait_ge(rv_ps, 2 * (j - 2 - RV_UNIT) + 2)
                    else:
                        dve.wait_ge(rg_made, 2 * (j - 2 - RG_UNIT) + 2)
                for half in range(2):
                    dve.wait_ge(acc_ready, u.v(2, 1 + half))
                    nc.vector.tensor_tensor(T4[2 * (j % 2) + half][:], PS[2 * u.parity + half][:], R[:],
                                            ALU.mult).then_inc(rt_made, 1)
                dve.wait_ge(rt_made, 2 * j + 2)
                nc.vector.sem_inc(acc_free, 1)
                if j:
                    post(j - 1)
                if j == 2:
                    for m in range(DT):
                        nc.vector.scalar_tensor_tensor(out=X[:, m, :], in0=X[:, m, :], scalar=vec("final", m), in1=RF[:],
                                                       op0=ALU.mult, op1=ALU.mult).then_inc(x_ready, 1)
                if j == 7:
                    nc.vector.tensor_scalar(neg_ident[:], ident, NEG, None, ALU.mult).then_inc(mask_made, 1)
                    nc.vector.tensor_copy(LEFT0[:], later).then_inc(mask_made, 1)
                if j in TOPK_AFTER:
                    choose(TOPK_AFTER[j])
            post(L.n - 1)

            dsa_bank = (PS[1], AUX[3])

            def ret_decay(n):
                h, mb = RET_JOBS[n]
                w = SEQ - P * mb
                dve.wait_ge(rs_ps, n + 1)
                if mb == 0:
                    dve.wait_ge(d_in[h % 2], 16 * (h // 2 + 1))
                if n >= 2:
                    dve.wait_ge(ro_ps, n - 1)
                nc.vector.tensor_tensor(T4[n % 2][:, 0:w], PS[0][:, 0:w], SQ[:, h % 2, 0:w], ALU.mult).then_inc(rd_made, 1)

            def ret_reciprocal(t, part):
                dve.wait_ge(rstd, t + 1)
                c = slice(part * P, (part + 1) * P)
                nc.vector.reciprocal(T4[2][:, c], STD[:, c]).then_inc(rrec, 1)

            def ret_out(t):
                dve.wait_ge(rrec, 4 * (t + 1))
                if t:
                    dve.wait_ge(m_lo_made, t)
                nc.vector.tensor_tensor(T4[3][:], AUX[0][:], T4[2][:], ALU.mult).then_inc(ro1, 1)

            def dsa_max(n):
                w = P * (DSA_JOBS[n][2] + 1)
                dve.wait_ge(a_s, n + 1)
                nc.vector.reduce_max(NM2[:, n % 2:n % 2 + 1], dsa_bank[n % 2][:, 0:w], AX.X).then_inc(a_m, 1)
                dve.wait_ge(a_m, n + 1)
                if n >= 2:
                    dve.wait_ge(a_e, n - 1)
                nc.vector.tensor_scalar(NEGMAX[:, n % 2:n % 2 + 1], NM2[:, n % 2:n % 2 + 1], -HD ** -0.5, None,
                                        ALU.mult).then_inc(a_nm, 1)

            def dsa_reciprocal(k, part):
                dve.wait_ge(a_o, 4 * k + 4)
                if k and not part:
                    dve.wait_ge(a_norm, k)
                c = slice(part * P, (part + 1) * P)
                nc.vector.reciprocal(R[0:HD, c], AUX[1 + k % 2][HD:P, c]).then_inc(a_rec, 1)

            def dsa_norm(k):
                dve.wait_ge(a_rec, 4 * k + 4)
                if k >= 2:
                    dve.wait_ge(a_lo_made, k // 2)
                lo = HD * (k % 2)
                nc.vector.tensor_tensor(SSUM[lo:lo + HD, :], AUX[1 + k % 2][0:HD, :], R[0:HD, :], ALU.mult).then_inc(a_norm, 1)

            dve.wait_ge(left_out, 3)
            dve.wait_ge(rg_made, 4)
            dve.wait_ge(rope_made, 16)
            dsa_max(0)
            for n, (t, half, b) in enumerate(DSA_JOBS):
                slot = n % 8
                if n + 1 < len(DSA_JOBS):
                    dsa_max(n + 1)
                for job in ret_jobs(n):
                    if job is not None:
                        ret_decay(job)
                if t and 1 <= slot <= 4:
                    dsa_reciprocal(2 * t - 1, slot - 1)
                if t and slot == 4:
                    dsa_norm(2 * t - 1)
                if slot == 5:
                    dsa_reciprocal(2 * t, 0)
                    dsa_reciprocal(2 * t, 1)
                if slot == 6:
                    dsa_reciprocal(2 * t, 2)
                    dsa_reciprocal(2 * t, 3)
                    ret_reciprocal(t, 0)
                if slot == 7:
                    dsa_norm(2 * t)
                    for part in (1, 2, 3):
                        ret_reciprocal(t, part)
                    ret_out(t)
            for part in range(4):
                dsa_reciprocal(7, part)
            dsa_norm(7)

            def y_steps(name, y0, add):
                L = layers[name]

                def step(j):
                    u = j.plus(L.base)
                    for half in range(2):
                        dve.wait_ge(acc_ready, u.v(2, half + 1))
                        m = At(2 * j.c + half, None if j.i is None else j.i * 2)
                        y = Y[:, bass.ds(m.v(), 1), :].rearrange("p o n -> p (o n)")
                        ps = PS[2 * u.parity + half][:]
                        if add:
                            i = nc.vector.tensor_tensor(y, ps, y, ALU.add)
                        else:
                            i = nc.vector.tensor_copy(y, ps)
                        i.then_inc(x_half, 1) if y0 is None else i.then_inc(y_ready, 1)
                    if y0 is None:
                        dve.wait_ge(x_half, j.v(2, 16 + 2))
                    else:
                        dve.wait_ge(y_ready, j.v(2, y0 + 2))
                    nc.vector.sem_inc(acc_free, 1)
                steps(dve, L.n, step)

            def add_normed(n, gain, k, here):
                rms(n)
                for m in range(DT):
                    if m >= 2 or k:
                        dve.wait_ge(x_ready, 40 + 8 * k + m - 1 if m >= 2 else 48)
                    nc.vector.scalar_tensor_tensor(out=T4[m % 2][:], in0=Y[:, m, :], scalar=vec(gain, m), in1=R[:],
                                                   op0=ALU.mult, op1=ALU.mult).then_inc(f_applied, 1)
                    if here:
                        dve.wait_ge(f_applied, 8 * k + m + 1)
                        nc.vector.tensor_tensor(X[:, m, :], X[:, m, :], T4[m % 2][:], ALU.add).then_inc(x_ready, 1)
                    elif m:
                        h_lo(FFN_PRE, "ffn_pre", At(m - 1))

            y_steps("wout", 0, False)
            add_normed(MIX_POST, "mix_post", 0, False)
            h_lo(FFN_PRE, "ffn_pre", At(DT - 1))

            def conv_gate_steps(name, j0, norm=None):
                L, q0 = layers[name], gu_base[name]
                q = q0 - 44

                def step(j):
                    u = j.plus(L.base)
                    b = u.parity
                    if j.i is None and j.c == 0 and norm is not None:
                        rms(norm)
                        dve.wait_ge(pad3_set, 1)
                    for i in range(2):
                        dve.wait_ge(acc_ready, u.v(2, 1 + i))
                        nc.vector.tensor_tensor(GP[:, i, 2:SEQ + 2], PS[2 * b + i][:], R[:], ALU.mult).then_inc(g3_in, 1)
                    dve.wait_ge(g3_in, j.v(2, 2 * q + 2))
                    nc.vector.sem_inc(acc_free, 1)
                    for i, y in enumerate((T_g, T_u)):
                        dve.wait_ge(c3_y, j.v(2, 2 * q + 1 + i))
                        nc.vector.scalar_tensor_tensor(out=y[:], in0=GP[:, i, 1:SEQ + 1], scalar=vec("conv3_w", j.plus(44 + 22 * i + j0)),
                                                       in1=y[:], op0=ALU.mult, op1=ALU.add).then_inc(c3_y1, 1)
                    for i, y in enumerate((T_g, T_u)):
                        dve.wait_ge(c3_y1, j.v(2, 2 * q + 1 + i))
                        nc.vector.scalar_tensor_tensor(out=y[:], in0=GP[:, i, 0:SEQ], scalar=vec("conv3_w", j.plus(22 * i + j0)),
                                                       in1=y[:], op0=ALU.mult, op1=ALU.add).then_inc(gate_in if i == 0 else c3_y2, 1)
                    dve.wait_ge(c3_y2, j.v(1, q + 1))
                    hidden(j, q0)
                steps(dve, L.n, step, first=1)

            conv_gate_steps("gu2a", 0, norm=FFN_PRE)
            y_steps("dn2a", None, False)
            conv_gate_steps("gu2b", 11)
            y_steps("dn2b", 8, True)
            add_normed(FFN_POST, "ffn_post", 1, True)


def constants(np):
    f = np.float32
    cmat = np.zeros((P, 9, P), f)
    p = np.arange(P)
    cmat[p, 0, p] = 1
    cmat[:, 1] = 1
    cmat[(p // HD) * HD + (p + HD // 2) % HD, 2, p] = 1
    cmat[p % HD, 3, p] = 1
    cmat[(p + HD // 2) % HD, 4, p] = 1
    cmat[:, 5] = p[:, None] // HD == p[None, :] // HD
    for i in range(2):
        cmat[2 * i + p // HD, 6 + i, p] = 1
    cmat[:, 8] = p[None, :] > p[:, None]

    onehot = np.zeros((BUCKETS + 1, 3, DIAG), f)
    for g, (dilation, zero, far) in enumerate(((1, 2 * P - 1, P), (4, P - 1, P - 1), (16, 31, 31))):
        for x in range(DIAG):
            dist = zero - x
            if not 0 <= dist <= far:
                onehot[BUCKETS, g, x] = 1
                continue
            n = dist * dilation
            large = 16 + int(np.log(f(max(n, 1)) / f(16)) / f(np.log(2048 / 16)) * f(16)) if n >= 16 else 0
            onehot[n if n < 16 else min(large, BUCKETS - 1), g, x] = 1

    inv = f(10000.0) ** (-np.arange(0, HD, 2, dtype=f) / f(HD))
    ang = np.arange(SEQ, dtype=f)[:, None] * inv[None, :]
    cos, sin = np.cos(ang).T, np.sin(ang).T
    rotary = np.stack([np.concatenate([cos] * 4), np.concatenate([-sin, sin] * 2)], 1)

    diff = np.arange(SEQ)[None, :] - p[:, None]
    log_g = np.log(1.0 - 2.0 ** (-5.0 - np.arange(RET_HEADS)))
    decay = np.where(diff >= 0, np.exp(log_g[:, None, None] * np.maximum(diff, 0)), 0.0) * HD ** -0.5
    return {"cmat": cmat, "onehot": onehot, "rotary": rotary.astype(f), "decay": decay.astype(f)}


def kernel(**inputs):
    import numpy as np
    import concourse.bacc as bacc
    from concourse.bass_utils import run_bass_kernel_spmd as run

    g = {k: np.asarray(v) for k, v in inputs.items()}

    def rows(w):
        k, n = w.shape
        return np.ascontiguousarray(w.reshape(k // P, P, n // COLS, COLS)[:].transpose(2, 1, 0, 3)
                                    .reshape(n // COLS, P, (k // P) * COLS))

    def paired(a, b):
        k, n = a.shape
        return np.stack([a.reshape(k, n // P, P), b.reshape(k, n // P, P)], 2).reshape(k, 2 * n)

    def tiles(v):
        v = v.reshape(-1, v.shape[-1] // P, P)
        return v.transpose(2, 0, 1).reshape(P, -1)

    arrays = {}
    pw1 = g["conv_w_pw1"][0]
    arrays["pw1"] = rows(paired(pw1[:, :D_MODEL], pw1[:, D_MODEL:]))
    arrays["pw2"] = rows(g["conv_w_pw2"][0])
    up2 = g["w_up_2"][0]
    gates = [g["ffn_w_gate"][0], g["ffn_w_gate"][1], up2[:, :FF_TILES * P]]
    ups = [g["ffn_w_up"][0], g["ffn_w_up"][1], up2[:, FF_TILES * P:]]
    downs = [g["ffn_w_down"][0], g["ffn_w_down"][1], g["w_down_2"][0]]
    qkv = g["attn_w_qkv"][0]
    arrays["qkv"] = rows(np.concatenate([qkv[:, 1536:], qkv[:, :1536]], 1))
    arrays["wo"] = rows(g["attn_w_o"][0])
    w_in = g["w_in_2"][0]
    arrays["inp"] = rows(np.concatenate([w_in[:, 2560:2688], w_in[:, 3200:3272], np.zeros((D_MODEL, 56), np.float32),
                                         w_in[:, 2688:3200], w_in[:, 2048:2560], w_in[:, 1024:1536],
                                         w_in[:, :1024], w_in[:, 1536:2048]], 1))
    arrays["wout"] = rows(g["w_out_2"][0])
    arrays["rel_bias"] = g["rel_bias"]
    for l in range(3):
        gu = rows(paired(gates[l], ups[l]))
        dn = downs[l]
        h = FF_HALF * P
        arrays[f"gu{l}a"], arrays[f"gu{l}b"] = gu[:FF_HALF], gu[FF_HALF:]
        arrays[f"dn{l}a"], arrays[f"dn{l}b"] = rows(dn[:h]), rows(dn[h:])
    arrays["x"] = g["x"][0].T.reshape(DT, P, SEQ).transpose(1, 0, 2)
    parts = {"norm_mix0": g["norm_mix"][0], "norm_mix1": g["norm_mix"][1], "norm_ffn0": g["norm_ffn"][0],
             "norm_ffn1": g["norm_ffn"][1], "final": g["final_norm"], "b_pw1": g["conv_b_pw1"][0],
             "w_dw": g["conv_w_dw"][0], "b_dw": g["conv_b_dw"][0], "ln_g": g["conv_ln_g"][0],
             "ln_b": g["conv_ln_b"][0], "b_pw2": g["conv_b_pw2"][0],
             "mix_pre": g["mix_norm_pre_2"][0], "mix_post": g["mix_norm_post_2"][0],
             "ffn_pre": g["ffn_norm_pre_2"][0], "ffn_post": g["ffn_norm_post_2"][0],
             "conv3_w": g["conv_w_2"][0], "conv3_b": g["conv_b_2"][0]}
    arrays["vecs"] = np.concatenate([tiles(parts[n]) for n, _ in VECS], 1)
    arrays.update(constants(np))
    arrays = {k: np.ascontiguousarray(v) for k, v in arrays.items()}

    nc = bacc.Bacc("TRN2", target_bir_lowering=False, num_devices=1)
    aps = {k: nc.dram_tensor(f"in_{k}", v.shape, mybir.dt.from_np(v.dtype), kind="ExternalInput").ap()
           for k, v in arrays.items()}
    out = nc.dram_tensor("out", (P, DT, SEQ), F32, kind="ExternalOutput").ap()
    build(nc, aps, out)
    r = run(nc, [{f"in_{k}": v for k, v in arrays.items()}], core_ids=[0])
    y = r.results[0]["out"]
    return np.ascontiguousarray(np.asarray(y).transpose(1, 0, 2).reshape(D_MODEL, SEQ).T)[None]
```
